# Optimizing a Trainium2 kernel written in Bass

```python
import math
import jax, jax.numpy as jnp
from jax import lax
import numpy as np

D_MODEL = 1024
BATCH = 1
SEQ = 512
DEPTH = 2

GRID_W = 64
CTX_LEN = 256
N_EVEN = (DEPTH + 1) // 2
N_ODD = DEPTH // 2
NORM_EPS = 1e-6
N_MOD = 6

SSD_WIDTH = D_MODEL
SSD_HEAD_DIM = 64
SSD_HEADS = SSD_WIDTH // SSD_HEAD_DIM
SSD_STATE = 128
SSD_GROUPS = 2
SSD_CONV = 3
SSD_CHUNK = 128
SSD_XBC = SSD_WIDTH + 2 * SSD_GROUPS * SSD_STATE
DT_PROJ_SCALE = 0.1
HY_WIDTH = D_MODEL
HY_SHORT = 3
HY_BANDS = 16
HY_EMB = 1 + 2 * HY_BANDS
HY_FFN = 64
HY_FAST_DECAY = 0.3
HY_SLOW_DECAY = 1.5
HY_DECAY_TARGET = 1e-2
COL_XBC = SSD_WIDTH
COL_DT = COL_XBC + SSD_XBC
COL_HY = COL_DT + 2 * SSD_HEADS
IN_COLS = COL_HY + 3 * HY_WIDTH
MIX_WIDTH = SSD_WIDTH + HY_WIDTH
ATTN_HEAD_DIM = 64
ATTN_Q_HEADS = 16
ATTN_KV_HEADS = 4
ATTN_GROUP = ATTN_Q_HEADS // ATTN_KV_HEADS
ATTN_Q_WIDTH = ATTN_Q_HEADS * ATTN_HEAD_DIM
ATTN_KV_WIDTH = ATTN_KV_HEADS * ATTN_HEAD_DIM
QKV_COLS = ATTN_Q_WIDTH + 2 * ATTN_KV_WIDTH
ATTN_SCALE = ATTN_HEAD_DIM ** -0.5
WINDOW = 128
ATTN_BLOCK = 128
ROPE_BASE = 10000.0
FFN_HIDDEN = -(-8 * D_MODEL // (3 * 256)) * 256

kernel_name = 'hybrid_ssd_hyena_swa_flow_block'

def rmsnorm(t, g):
    t32 = t.astype(jnp.float32)
    y = t32 * lax.rsqrt(jnp.mean(t32 * t32, axis=-1, keepdims=True) + NORM_EPS)
    return (y * g.astype(jnp.float32)).astype(t.dtype)

def conv_centred(t, w, b):
    k_w = w.shape[0]
    pad = (k_w - 1) // 2
    L = t.shape[1]
    tp = jnp.pad(t, ((0, 0), (pad, k_w - 1 - pad), (0, 0)))
    out = tp[:, 0:L] * w[0]
    for k in range(1, k_w):
        out = out + tp[:, k:k + L] * w[k]
    return out + b

def axial_rope(t):
    L = t.shape[1]
    rows = L // GRID_W
    row = jnp.repeat(jnp.arange(rows), GRID_W).astype(jnp.float32)
    col = jnp.tile(jnp.arange(GRID_W), rows).astype(jnp.float32)
    half = t.shape[-1] // 2
    nf = half // 2
    inv = ROPE_BASE ** (-jnp.arange(nf, dtype=jnp.float32) / nf)

    def rot(u, pos):
        ang = (pos[:, None] * inv[None, :])[None, :, None, :]
        cos, sin = jnp.cos(ang), jnp.sin(ang)
        u1, u2 = u[..., :nf], u[..., nf:]
        return jnp.concatenate([u1 * cos - u2 * sin, u2 * cos + u1 * sin], axis=-1)

    t32 = t.astype(jnp.float32)
    return jnp.concatenate([rot(t32[..., :half], row), rot(t32[..., half:], col)], axis=-1).astype(t.dtype)

def ssd_chunked(x, dt, a_neg, bm, cm, h0):
    b, L, H, P = x.shape
    G, N = bm.shape[2], bm.shape[3]
    R = H // G
    Q = SSD_CHUNK
    nc = L // Q
    xc = (x.astype(jnp.float32) * dt[..., None]).reshape(b, nc, Q, G, R, P)
    acum = jnp.cumsum((dt * a_neg).reshape(b, nc, Q, G, R), axis=2)
    bc = bm.astype(jnp.float32).reshape(b, nc, Q, G, N)
    cc = cm.astype(jnp.float32).reshape(b, nc, Q, G, N)
    tri = jnp.tril(jnp.ones((Q, Q), dtype=bool))
    seg = acum[:, :, :, None] - acum[:, :, None, :]
    lmat = jnp.exp(jnp.where(tri[None, None, :, :, None, None], seg, -jnp.inf))
    cb = jnp.einsum('bcign,bcjgn->bcijg', cc, bc)
    y_diag = jnp.einsum('bcijg,bcijgr,bcjgrp->bcigrp', cb, lmat, xc)
    decay_to_end = jnp.exp(acum[:, :, -1:] - acum)
    states = jnp.einsum('bcjgn,bcjgr,bcjgrp->bcgrpn', bc, decay_to_end, xc)
    chunk_decay = jnp.exp(acum[:, :, -1])

    def step(h, inp):
        st, dec = inp
        return h * dec[..., None, None] + st, h

    h_last, h_in = lax.scan(step, h0.reshape(b, G, R, P, N).astype(jnp.float32),
                            (jnp.moveaxis(states, 1, 0), jnp.moveaxis(chunk_decay, 1, 0)))
    h_in = jnp.moveaxis(h_in, 0, 1)
    y_off = jnp.einsum('bcign,bcigr,bcgrpn->bcigrp', cc, jnp.exp(acum), h_in)
    return (y_diag + y_off).reshape(b, L, H, P), h_last.reshape(b, H, P, N)

def bidir_ssd(seq_c, seq_l, a_f, a_b, d_skip):
    xc, dfc, dbc, bmc, cmc = seq_c
    xl, dfl, dbl, bml, cml = seq_l
    b, _, H, P = xc.shape
    h0 = jnp.zeros((b, H, P, bmc.shape[-1]), jnp.float32)
    fl = lambda t: jnp.flip(t, axis=1)
    y_cf, s_cf = ssd_chunked(xc, dfc, a_f, bmc, cmc, h0)
    y_lf, _ = ssd_chunked(xl, dfl, a_f, bml, cml, s_cf)
    y_cb, s_cb = ssd_chunked(fl(xc), fl(dbc), a_b, fl(bmc), fl(cmc), h0)
    y_lb, _ = ssd_chunked(fl(xl), fl(dbl), a_b, fl(bml), fl(cml), s_cb)
    y_c = y_cf + fl(y_cb) + d_skip[:, None] * xc.astype(jnp.float32)
    y_l = y_lf + fl(y_lb) + d_skip[:, None] * xl.astype(jnp.float32)
    return y_c, y_l

def hyena_filter(L, w1, b1, w2, b2, w3, b3, w4, freq):
    t = jnp.arange(L, dtype=jnp.float32)
    t_unit = t / (L - 1)
    ang = 2.0 * math.pi * t / L
    f = jnp.linspace(1e-4, HY_BANDS - 1, HY_BANDS, dtype=jnp.float32)
    z = jnp.concatenate([t_unit[:, None], jnp.cos(ang[:, None] * f), -jnp.sin(ang[:, None] * f)], axis=-1)
    h = jnp.sin(freq[0] * (z @ w1 + b1))
    h = jnp.sin(freq[1] * (h @ w2 + b2))
    h = jnp.sin(freq[2] * (h @ w3 + b3))
    h = (h @ w4).astype(jnp.float32)
    max_decay = math.log(HY_DECAY_TARGET) / HY_FAST_DECAY
    min_decay = math.log(HY_DECAY_TARGET) / HY_SLOW_DECAY
    deltas = jnp.linspace(min_decay, max_decay, HY_WIDTH, dtype=jnp.float32)
    window = jnp.exp(-t_unit[:, None] * jnp.abs(deltas)[None, :])
    h_fwd = h[:, :HY_WIDTH] * window
    h_bwd = h[:, HY_WIDTH:] * window
    k = jnp.concatenate([h_fwd, jnp.zeros((1, HY_WIDTH), jnp.float32), h_bwd[1:][::-1]], axis=0)
    return k * lax.rsqrt(jnp.sum(k * k, axis=0, keepdims=True) + 1e-6)

def long_conv(u, k):
    L = u.shape[1]
    uf = jnp.fft.rfft(u.astype(jnp.float32), n=2 * L, axis=1)
    kf = jnp.fft.rfft(k, n=2 * L, axis=0)
    return jnp.fft.irfft(uf * kf[None], n=2 * L, axis=1)[:, :L]

def hyena_op(hp, conv_w, conv_b, filt, bias):
    hp = conv_centred(hp, conv_w, conv_b)
    x0, x1, v = jnp.split(hp, 3, axis=-1)
    u = (x1 * v).astype(jnp.float32)
    k = hyena_filter(hp.shape[1], *filt)
    y = long_conv(u, k) + bias.astype(jnp.float32) * u
    return (x0.astype(jnp.float32) * y).astype(hp.dtype)

def ssd_hyena_mixer(h_c, h_l, w_in, conv_w, conv_b, dt_bias, a_log, d_skip, norm_g,
                    hy_conv_w, hy_conv_b, hy_filt, hy_bias, w_out, need_ctx):
    G, N = SSD_GROUPS, SSD_STATE

    def prep(h):
        b, L = h.shape[:2]
        p = h @ w_in
        z = p[..., :COL_XBC]
        xbc = jax.nn.silu(conv_centred(p[..., COL_XBC:COL_DT], conv_w, conv_b))
        dt = p[..., COL_DT:COL_HY].astype(jnp.float32)
        hy = p[..., COL_HY:]
        xs = xbc[..., :SSD_WIDTH].reshape(b, L, SSD_HEADS, SSD_HEAD_DIM)
        bm = xbc[..., SSD_WIDTH:SSD_WIDTH + G * N].reshape(b, L, G, N)
        cm = xbc[..., SSD_WIDTH + G * N:].reshape(b, L, G, N)
        dt_f = jax.nn.softplus(dt[..., :SSD_HEADS] + dt_bias[0].astype(jnp.float32))
        dt_b = jax.nn.softplus(dt[..., SSD_HEADS:] + dt_bias[1].astype(jnp.float32))
        return z, (xs, dt_f, dt_b, bm, cm), hy

    z_c, seq_c, hy_c = prep(h_c)
    z_l, seq_l, hy_l = prep(h_l)
    a_f = -jnp.exp(a_log[0].astype(jnp.float32))
    a_b = -jnp.exp(a_log[1].astype(jnp.float32))
    y_c, y_l = bidir_ssd(seq_c, seq_l, a_f, a_b, d_skip.astype(jnp.float32))

    def finish(y, z, hy):
        b, L = z.shape[:2]
        y = rmsnorm(y.reshape(b, L, SSD_WIDTH) * jax.nn.silu(z.astype(jnp.float32)), norm_g).astype(z.dtype)
        g = hyena_op(hy, hy_conv_w, hy_conv_b, hy_filt, hy_bias)
        return jnp.concatenate([y, g], axis=-1) @ w_out

    out_l = finish(y_l, z_l, hy_l)
    if not need_ctx:
        return None, out_l
    return finish(y_c, z_c, hy_c), out_l

def sink_softmax(scores, sink):
    s_sink = jnp.broadcast_to(sink.astype(jnp.float32)[None, :, :, None, None], scores.shape[:-1] + (1,))
    p = jax.nn.softmax(jnp.concatenate([scores, s_sink], axis=-1), axis=-1)
    return p[..., :-1]

def windowed_attention(q, k, v, k_c, v_c, sink):
    b, L = q.shape[:2]
    nb = L // ATTN_BLOCK
    span = ATTN_BLOCK + 2 * WINDOW
    kp = jnp.pad(k, ((0, 0), (WINDOW, WINDOW), (0, 0), (0, 0)))
    vp = jnp.pad(v, ((0, 0), (WINDOW, WINDOW), (0, 0), (0, 0)))

    def block(i):
        start = i * ATTN_BLOCK
        qb = lax.dynamic_slice_in_dim(q, start, ATTN_BLOCK, axis=1)
        kb = lax.dynamic_slice_in_dim(kp, start, span, axis=1)
        vb = lax.dynamic_slice_in_dim(vp, start, span, axis=1)
        qpos = start + jnp.arange(ATTN_BLOCK)
        kpos = start - WINDOW + jnp.arange(span)
        ok = (jnp.abs(qpos[:, None] - kpos[None, :]) <= WINDOW) & (kpos[None, :] >= 0) & (kpos[None, :] < L)
        s_loc = jnp.einsum('bqgrd,bkgd->bgrqk', qb, kb).astype(jnp.float32) * ATTN_SCALE
        s_loc = jnp.where(ok[None, None, None], s_loc, -jnp.inf)
        s_ctx = jnp.einsum('bqgrd,bkgd->bgrqk', qb, k_c).astype(jnp.float32) * ATTN_SCALE
        p = sink_softmax(jnp.concatenate([s_loc, s_ctx], axis=-1), sink).astype(vb.dtype)
        return (jnp.einsum('bgrqk,bkgd->bqgrd', p[..., :span], vb)
                + jnp.einsum('bgrqk,bkgd->bqgrd', p[..., span:], v_c))

    o = lax.map(block, jnp.arange(nb))
    return jnp.moveaxis(o, 0, 1).reshape(b, L, ATTN_Q_WIDTH)

def attn_mixer(h_c, h_l, w_qkv, sinks, w_out, need_ctx):
    def proj(h):
        b, L = h.shape[:2]
        p = h @ w_qkv
        q = p[..., :ATTN_Q_WIDTH].reshape(b, L, ATTN_Q_HEADS, ATTN_HEAD_DIM)
        k = p[..., ATTN_Q_WIDTH:ATTN_Q_WIDTH + ATTN_KV_WIDTH].reshape(b, L, ATTN_KV_HEADS, ATTN_HEAD_DIM)
        v = p[..., ATTN_Q_WIDTH + ATTN_KV_WIDTH:].reshape(b, L, ATTN_KV_HEADS, ATTN_HEAD_DIM)
        return q, k, v

    q_c, k_c, v_c = proj(h_c)
    q_l, k_l, v_l = proj(h_l)
    q_l, k_l = axial_rope(q_l), axial_rope(k_l)
    sink = sinks.reshape(ATTN_KV_HEADS, ATTN_GROUP)
    b, L = h_l.shape[:2]
    o_l = windowed_attention(q_l.reshape(b, L, ATTN_KV_HEADS, ATTN_GROUP, ATTN_HEAD_DIM), k_l, v_l, k_c, v_c, sink)
    out_l = o_l @ w_out
    if not need_ctx:
        return None, out_l
    lc = h_c.shape[1]
    qg = q_c.reshape(b, lc, ATTN_KV_HEADS, ATTN_GROUP, ATTN_HEAD_DIM)
    s = jnp.einsum('bqgrd,bkgd->bgrqk', qg, k_c).astype(jnp.float32) * ATTN_SCALE
    p = sink_softmax(s, sink).astype(v_c.dtype)
    o_c = jnp.einsum('bgrqk,bkgd->bqgrd', p, v_c).reshape(b, lc, ATTN_Q_WIDTH)
    return o_c @ w_out, out_l

def swiglu(h, w_in, w_out):
    gu = h @ w_in
    return (jax.nn.silu(gu[..., :FFN_HIDDEN]) * gu[..., FFN_HIDDEN:]) @ w_out

def setup_inputs(seed: int = 0) -> dict:
    key = jax.random.key(seed)
    k = jax.random.split(key, 40)
    d = D_MODEL

    def nrm(kk, shape, scale):
        return scale * jax.random.normal(kk, shape, jnp.float32)

    hy_in_w = nrm(k[8], (N_EVEN, d, IN_COLS), d ** -0.5)
    hy_in_w = hy_in_w.at[:, :, COL_DT:COL_HY].multiply(DT_PROJ_SCALE)
    dt0 = jnp.exp(jax.random.uniform(k[11], (N_EVEN, 2, SSD_HEADS), jnp.float32, math.log(1e-3), math.log(1e-1)))
    ssd_dt_bias = dt0 + jnp.log(-jnp.expm1(-dt0))
    ssd_a_log = jnp.log(jax.random.uniform(k[12], (N_EVEN, 2, SSD_HEADS), jnp.float32, 1.0, 16.0))
    return {
        'x': nrm(k[0], (BATCH, SEQ, d), 1.0),
        'c': nrm(k[1], (BATCH, d), 1.0),
        'ctx': nrm(k[2], (BATCH, CTX_LEN, d), 1.0),
        'c_ctx': nrm(k[3], (d,), 1.0),
        'ada_w': nrm(k[4], (DEPTH, d, N_MOD * d), 0.5 * d ** -0.5),
        'ada_b': nrm(k[5], (DEPTH, N_MOD * d), 0.02),
        'norm1_g': 1.0 + nrm(k[6], (DEPTH, d), 0.05),
        'norm2_g': 1.0 + nrm(k[7], (DEPTH, d), 0.05),
        'hy_in_w': hy_in_w,
        'ssd_conv_w': nrm(k[9], (N_EVEN, SSD_CONV, SSD_XBC), SSD_CONV ** -0.5),
        'ssd_conv_b': nrm(k[10], (N_EVEN, SSD_XBC), 0.02),
        'ssd_dt_bias': ssd_dt_bias,
        'ssd_a_log': ssd_a_log,
        'ssd_d': 1.0 + nrm(k[13], (N_EVEN, SSD_HEADS), 0.1),
        'ssd_norm_g': 1.0 + nrm(k[14], (N_EVEN, SSD_WIDTH), 0.05),
        'hy_conv_w': nrm(k[15], (N_EVEN, HY_SHORT, 3 * HY_WIDTH), HY_SHORT ** -0.5),
        'hy_conv_b': nrm(k[16], (N_EVEN, 3 * HY_WIDTH), 0.02),
        'hy_w1': nrm(k[17], (N_EVEN, HY_EMB, HY_FFN), HY_EMB ** -0.5),
        'hy_b1': nrm(k[18], (N_EVEN, HY_FFN), 0.02),
        'hy_w2': nrm(k[19], (N_EVEN, HY_FFN, HY_FFN), HY_FFN ** -0.5),
        'hy_b2': nrm(k[20], (N_EVEN, HY_FFN), 0.02),
        'hy_w3': nrm(k[21], (N_EVEN, HY_FFN, HY_FFN), HY_FFN ** -0.5),
        'hy_b3': nrm(k[22], (N_EVEN, HY_FFN), 0.02),
        'hy_w4': nrm(k[23], (N_EVEN, HY_FFN, 2 * HY_WIDTH), HY_FFN ** -0.5),
        'hy_freq': 1.0 + nrm(k[24], (N_EVEN, 3, HY_FFN), 0.1),
        'hy_bias': nrm(k[25], (N_EVEN, HY_WIDTH), 0.1),
        'hy_out_w': nrm(k[26], (N_EVEN, MIX_WIDTH, d), MIX_WIDTH ** -0.5),
        'attn_qkv_w': nrm(k[27], (N_ODD, d, QKV_COLS), d ** -0.5),
        'attn_sinks': nrm(k[28], (N_ODD, ATTN_Q_HEADS), 0.5),
        'attn_out_w': nrm(k[29], (N_ODD, ATTN_Q_WIDTH, d), ATTN_Q_WIDTH ** -0.5),
        'ffn_w_in': nrm(k[30], (DEPTH, d, 2 * FFN_HIDDEN), d ** -0.5),
        'ffn_w_out': nrm(k[31], (DEPTH, FFN_HIDDEN, d), FFN_HIDDEN ** -0.5),
        'final_g': 1.0 + nrm(k[32], (d,), 0.05),
    }

def reference(x, c, ctx, c_ctx, ada_w, ada_b, norm1_g, norm2_g, hy_in_w, ssd_conv_w, ssd_conv_b,
              ssd_dt_bias, ssd_a_log, ssd_d, ssd_norm_g, hy_conv_w, hy_conv_b, hy_w1, hy_b1, hy_w2,
              hy_b2, hy_w3, hy_b3, hy_w4, hy_freq, hy_bias, hy_out_w, attn_qkv_w, attn_sinks,
              attn_out_w, ffn_w_in, ffn_w_out, final_g):
    sc = jax.nn.silu(c)
    scc = jax.nn.silu(c_ctx)
    for layer in range(DEPTH):
        need_ctx = layer < DEPTH - 1
        j = layer // 2
        mod_l = jnp.split((sc @ ada_w[layer] + ada_b[layer])[:, None, :], N_MOD, axis=-1)
        mod_c = jnp.split((scc @ ada_w[layer] + ada_b[layer])[None, None, :], N_MOD, axis=-1)
        h_l = rmsnorm(x, norm1_g[layer]) * (1.0 + mod_l[1]) + mod_l[0]
        h_c = rmsnorm(ctx, norm1_g[layer]) * (1.0 + mod_c[1]) + mod_c[0]
        if layer % 2 == 0:
            hy_filt = (hy_w1[j], hy_b1[j], hy_w2[j], hy_b2[j], hy_w3[j], hy_b3[j], hy_w4[j], hy_freq[j])
            o_c, o_l = ssd_hyena_mixer(h_c, h_l, hy_in_w[j], ssd_conv_w[j], ssd_conv_b[j], ssd_dt_bias[j],
                                       ssd_a_log[j], ssd_d[j], ssd_norm_g[j], hy_conv_w[j], hy_conv_b[j],
                                       hy_filt, hy_bias[j], hy_out_w[j], need_ctx)
        else:
            o_c, o_l = attn_mixer(h_c, h_l, attn_qkv_w[j], attn_sinks[j], attn_out_w[j], need_ctx)
        x = x + mod_l[2] * o_l
        h_l = rmsnorm(x, norm2_g[layer]) * (1.0 + mod_l[4]) + mod_l[3]
        x = x + mod_l[5] * swiglu(h_l, ffn_w_in[layer], ffn_w_out[layer])
        if need_ctx:
            ctx = ctx + mod_c[2] * o_c
            h_c = rmsnorm(ctx, norm2_g[layer]) * (1.0 + mod_c[4]) + mod_c[3]
            ctx = ctx + mod_c[5] * swiglu(h_c, ffn_w_in[layer], ffn_w_out[layer])
    return rmsnorm(x, final_g)


_drawn_inputs = setup_inputs


def setup_inputs(seed=0):
    import zlib

    import numpy as np

    out = dict(_drawn_inputs(seed))
    spreads = {}
    factors = {'ctx': 67.532,
     'norm2_g': 2.759,
     'ssd_conv_b': 8.0,
     'ssd_d': 5.682,
     'ssd_norm_g': 5.337,
     'hy_conv_b': 4.954,
     'hy_b1': 5.6,
     'hy_b2': 4.975,
     'hy_b3': 5.027,
     'attn_sinks': 200.0,
     'c_ctx': 2.738}
    for name, (base, spread) in spreads.items():
        noise = np.random.default_rng([zlib.crc32(name.encode()), seed]).standard_normal(out[name].shape)
        drawn = base * np.exp(spread * noise) if base else spread * noise
        out[name] = __import__('jax').numpy.asarray(drawn.astype(out[name].dtype))
    for name, factor in factors.items():
        out[name] = (out[name] * factor).astype(out[name].dtype)
    return out
```

```python
import concourse.bass as bass
import numpy as np
from concourse import mybir
from contextlib import ExitStack

D = 1024
LAT, CTX = 512, 256
TOK = LAT + CTX
P = 128
KT = D // P
HEADS, HD, GROUPS, STATE = 16, 64, 2, 128
XBC_BLKS = (D + 2 * GROUPS * STATE) // P
HY_FFN, HY_BANDS = 64, 16
HY_EMB = 1 + 2 * HY_BANDS
NEV = 6
FFN = 2816
FB = FFN // P
FH = FB // 2
KV, QH = 4, 16
EPS = 1e-6
GRID_W = 64
ROPE_BASE = 10000.0
ATTN_SCALE = 64 ** -0.5
NEG = -1.0e30
SLOTS = 3
JT = 16
SEGS = ((0, LAT), (LAT, TOK))

_cols = {}
_at = 0
for _n, _w in (("ada_b", 2 * 48), ("n1", 16), ("n2", 16), ("fin", 8), ("sng", 8), ("scw", 3 * 12), ("scb", 12),
               ("hcw", 3 * 24), ("hcb", 24), ("dskip", 8), ("cc", 16), ("sink", 16), ("dtb", 32), ("alog", 32),
               ("eps", 2)):
    _cols[_n] = _at
    _at += _w
VEC_W = _at
IDENT, ONES, KGTJ, KLTJ, LE, GE, ROT, MLEFT, MRIGHT = range(9)


def weight_jobs():
    jobs, at = [], {}

    def stage(name, items):
        at[name] = len(jobs)
        jobs.extend(items)

    ada0 = [("ada", 0, n) for n in range(24)]
    ada1 = [("ada", 1, n) for n in range(24)]
    stage("ada_a", ada0[:8] + ada1[:8])
    stage("uv", [j for n in range(8) for j in (("uv", 0, n), ada0[8 + 2 * n], ada0[9 + 2 * n])])
    stage("x0", [j for n in range(4) for j in (("x0", 0, n), ada1[8 + 2 * n], ada1[9 + 2 * n])])
    stage("z", [j for n in range(4) for j in (("z", 0, n), ada1[16 + 2 * n], ada1[17 + 2 * n])])
    stage("xbc", [("xbc", 0, n) for n in range(6)])
    stage("out0", [("out0", 0, n) for n in range(8)])
    for layer in range(2):
        if layer:
            stage("qkv", [("q", 0, n) for n in range(4)] + [("k", 0, 0), ("v", 0, 0)])
            stage("out1", [("out1", 0, n) for n in range(4)])
        for half in range(2):
            stage(f"up{layer}{half}", [("up", layer, half * FH + n) for n in range(FH)])
            stage(f"down{layer}{half}", [("down", layer, (half, n)) for n in range(8)])
    return jobs, at


JOBS, AT = weight_jobs()


def job_blocks(kind):
    return {"ada": 0, "out0": 1, "down": 1, "v": 0}.get(kind, 2)


def plan():
    used, turn, out, last = [0, 0, 1], 0, [], None
    for kind, layer, _ in JOBS:
        n = job_blocks(kind)
        if n == 1 and kind != last:
            turn = 0
        pairs = []
        for u in range(n):
            pair = u if n == 2 else turn
            pairs.append((pair, used[pair]))
            used[pair] += 1
        if n == 1:
            turn = (turn + 1) % 3
        last = kind
        out.append(pairs)
    return out


PLAN = plan()


def uses(u, g):
    return sum(p == u for blocks in PLAN[:g] for p, _ in blocks) + (u == 2)


def along(values, i):
    if isinstance(i, int):
        return values[i]
    step = values[1] - values[0]
    assert all(b - a == step for a, b in zip(values, values[1:])), values
    return i * step + values[0]


class Count:

    def __init__(self, eng, sem):
        self.eng, self.sem, self.n, self.i, self.per = eng, sem, 0, None, 0

    def now(self):
        return self.n if self.i is None else self.i * self.per + self.n

    def inc(self, ins):
        ins.then_inc(self.sem, 1)
        self.n += 1
        return self.now()

    def link(self, ins):
        self.eng.wait_ge(self.sem, self.inc(ins))

    def enter(self, i, per):
        self.i, self.per, self.base = i, per, self.n
        if not isinstance(i, int):
            self.first = True

    def leave(self, times):
        assert self.n - self.base == self.per, (self.n - self.base, self.per)
        self.n = self.base + self.per * times
        self.i = None


def build_kernel(nc, A, out):
    f32 = mybir.dt.float32
    ALU = mybir.AluOpType
    ACT = mybir.ActivationFunctionType
    AX = mybir.AxisListType
    ctx = ExitStack()
    with ctx:
        def sb(name, shape):
            return ctx.enter_context(nc.sbuf_tensor(name, shape, f32))

        def sem(name):
            return ctx.enter_context(nc.semaphore(name))

        X = sb("residual", [P, KT, TOK])
        HNt = sb("normed", [P, KT * TOK])
        W = sb("weights", [P, SLOTS, JT, P])
        C = sb("consts", [P, 9, P])
        V = sb("vectors", [P, VEC_W])
        MOD = sb("mods", [P, 2, 48, 2])
        GA = sb("gains", [P, 4, KT, 2])
        CS = sb("silu_c", [P, KT, 2])
        Tt = sb("temps", [P, 4 * TOK])
        R = sb("phase", [P, 29184])
        HN = HNt[:, :].rearrange("p (k t) -> p k t", k=KT)
        T = Tt[:, :].rearrange("p (k t) -> p k t", k=4)

        def region(at, *dims):
            n = 1
            for d in dims:
                n *= d
            names = "abcd"[:len(dims)]
            ap = R[:, at:at + n]
            if len(dims) == 1:
                return ap
            return ap.rearrange(f"p ({' '.join(names)}) -> p {' '.join(names)}",
                                **{names[i]: dims[i] for i in range(1, len(dims))})

        def inside(base, at, *dims):
            n = 1
            for d in dims:
                n *= d
            names = "abcd"[:len(dims)]
            ap = base[:, at:at + n]
            if len(dims) == 1:
                return ap
            return ap.rearrange(f"p ({' '.join(names)}) -> p {' '.join(names)}",
                                **{names[i]: dims[i] for i in range(1, len(dims))})

        KS = region(0, 2, 6, D)
        UT = region(12288, 6, KT, P)
        G = region(12288, KT, TOK)
        C4 = region(18432, 2, 2560)
        C3 = region(12288, 2, 2560)
        SD = region(17408, 2, 6, 512)
        W4 = region(23552, 2 * D)
        HF = region(25600, 3, TOK)
        WIN = inside(HNt, 0, 6, 512)
        INV = inside(HNt, 3072, 2, 512)
        BB = inside(HNt, 4096, 512)
        SQ2 = inside(HNt, 4608, 2, 512)
        W1S = region(27904, 64)
        WS = region(27968, 2, 64)
        FBV = region(28096, 9)
        ZT = region(28160, TOK)
        Z = region(0, KT, TOK)
        XBC = region(18432, XBC_BLKS, TOK)
        XT_ = region(6144, 6, KT, P)
        BT = region(27648, 6, 2, P)
        WDT = region(24576, KT, 32)
        HID = region(0, FH, TOK)
        QT = region(0, KT, LAT)
        KD = region(4096, KV, TOK)
        VT = region(7168, 6, 256)
        RC = region(8704, 2, LAT)
        OT = region(9728, KT, LAT)
        QG = region(13824, 2, LAT)
        PR = region(14848, 2, 640)
        PTS = region(16128, 2, 640)
        OTOK = region(17408, 4, 4, HD)
        AST = region(18432, 256)
        KG = region(18688, TOK)
        VG = region(19456, 6, HD)
        WD = sb("w_dt", [P, KT, 32])
        AT2 = inside(HNt, 0, 2, 512)
        LEB = inside(HNt, 1024, 2, 1024)
        XDT = inside(HNt, 3072, 1024)
        XDE = inside(HNt, 4096, 1024)
        BST = inside(HNt, 5120, 4, P)
        CBM = inside(HNt, 5632, 2, 2, P)
        HST = inside(Tt, 0, 2, 1024)
        DTS = inside(Tt, 2048, 1024)
        DTP = DTS[:, 0:192].rearrange("p (t h) -> p t h", t=6)
        DTA = DTS[:, 192:384].rearrange("p (t h) -> p t h", t=6)
        DEC = DTS[:, 384:768]
        SPT = DTS[:, 768:960]
        SPU = sb("softplus_tmp", [P, 2, 192])

        PS = ctx.enter_context(nc.psum_tensor("psum", [P, 8, 512], f32))
        PSF = PS[:, :, :].rearrange("p b c -> p (b c)")

        def pair(u):
            return PSF[:, 1024 * u:1024 * u + TOK]

        TP = PSF[:, 2048:2048 + TOK]
        MODP = PS[:, 7, 0:192].rearrange("p (l b c) -> p l b c", l=2, b=48)

        def vec(name, n, w=1):
            return V[:, _cols[name] + n:_cols[name] + n + w]

        def dvec(name, base, i, step=1):
            at = i * step + (_cols[name] + base)
            return V[:, bass.ds(at, 1)] if not isinstance(at, int) else V[:, at:at + 1]

        w_loaded = [sem(f"w_loaded{s}") for s in range(SLOTS)]
        blocks_done = sem("blocks_done")
        pair_free = [sem(f"pair_free{u}") for u in range(3)]
        a_ch, v_ch, g_ch = sem("act_order"), sem("dve_order"), sem("pool_order")
        x_in, c_in, v_in, small_in, t3_in, t4_in, win_in, rope_in = (
            sem(n) for n in ("x_in", "c_in", "v_in", "small_in", "t3_in", "t4_in", "win_in", "rope_in"))
        silu_c, mods_a, mods_b = sem("silu_c_ready"), sem("mods_a_ready"), sem("mods_b_ready")
        gains_ready = sem("gains_ready")
        names = """filter_bias filter_mm filter_arg filter_reduced filter_sin
            kg_mm kg_free kg_sd kg_sq kg_ssq kg_root kg_order kd_mm kd_ev bias_in
            sq_ready sq_mm norm_sqrt norm_mul hn_ready conv_first
            u_ready tp_mm tp_copied u_mm u_prod p_ready inv_mm g_ready
            x_stored xt_mm xt_copied dt_mm dt_abs dt_exp dt_ready dec_mm dec_ready dx_ready states_zero
            step_at step_seg step_exp step_mc step_y step_cb step_cbm step_xdt step_xde step_st step_added
            step_state step_b yz_ready yn_ready
            q_rot q_done k_done v_done
            at_q at_s at_neg at_sink at_exp at_pt at_ptc at_pv at_o at_ot at_otc
            fin_ready out_done eps_ready win2_in bias2_in at_group"""
        (fb_ready, mlp_mm, mlp_arg, mlp_red, mlp_sin,
         kg_mm, kg_free, kg_sd, kg_sq, kg_ssq, kg_root, kg_ord, kd_mm, kd_ev, bias_in,
         sq_ready, sq_mm, n_sqrt, n_mul, hn_ready, cv_act,
         u_ready, tp_mm, tp_copied, u_mm, u_prod, p_ready, inv_mm, g_ready,
         xs_ready, xt_mm, xt_copied, dt_mm, dta_raw, sp_exp, dt_a, dec_mm, dec_ready, dx_ready, st_zero,
         s_at, s_seg, s_exp, s_mc, s_y, s_cb, s_cbm, s_xdt, s_xde, s_st, s_yadd,
         s_stf, s_bst, yz_ready, yn_ready,
         q_rot, q_done, k_done, v_done,
         at_q, at_s, at_neg, at_sinkexp, at_exp, at_pt, at_ptc, at_pv, at_o, at_ot, at_otc,
         fin_ready, out_done, eps_ready, win2_in, bias2_in, at_group) = (sem(n) for n in names.split())

        def residual(k, name, eng):
            first = AT[name]
            if name == "out1":
                read([first + k // 2], 0, k % 2, eng)
            else:
                read([first + k], 0, 0, eng)

        def read(gs, i, b, eng):
            eng.wait_ge(pair_free[PLAN[gs[0]][b][0]], along([PLAN[g][b][1] + 1 for g in gs], i))

        def loops(eng, n, body, chain=None, per=0):
            if n == 0:
                return
            if n == 1:
                body(0)
                return
            if chain is None:
                with eng.Fori(0, n) as i:
                    body(i)
                return
            with eng.Fori(0, n) as i:
                chain.enter(i, per)
                body(i)
                chain.leave(n)

        def job_turns(eng, name, count, body, chain=None, per=0, unit=1):
            first = AT[name]
            full = count // SLOTS

            def turn(i):
                for r in range(SLOTS):
                    body([first + n * SLOTS + r for n in range(full)], i, r)
            loops(eng, full, turn, chain, per)
            for r in range(count - full * SLOTS):
                g = first + full * SLOTS + r
                body([g], 0, full * SLOTS + r)

        block = ctx.enter_context(nc.Block())

        @block.sync
        def _(sp):
            def load(gs, i, width=JT):
                s = gs[0] % SLOTS
                if gs[0] >= SLOTS:
                    sp.wait_ge(blocks_done, along([2 * (g - SLOTS + 1) for g in gs], i))
                sp.dma_start(W[:, s, 0:width, :], A["wall"][along(gs, i), :, 0:width * P].rearrange(
                    "p (t n) -> p t n", n=P)).then_inc(w_loaded[s], 16)

            def run(first, count, width=JT):
                start = first
                while start < SLOTS and count:
                    load([start], 0, width)
                    start, count = start + 1, count - 1
                full = count // SLOTS

                def turn(i):
                    for r in range(SLOTS):
                        load([start + n * SLOTS + r for n in range(full)], i, width)
                loops(sp, full, turn)
                for r in range(count - full * SLOTS):
                    load([start + full * SLOTS + r], 0, width)

            cuts, at = [], 0
            for name in sorted(AT, key=AT.get):
                if name.startswith("down"):
                    cuts.append((at, AT[name] - at, JT))
                    cuts.append((AT[name], 8, FH))
                    at = AT[name] + 8
            assert at == len(JOBS)
            for first, count, width in cuts:
                run(first, count, width)
            sp.wait_ge(fin_ready, KT)
            sp.dma_start(out, HN[:, :, 0:LAT]).then_inc(out_done, 16)
            sp.wait_ge(out_done, 16)

        @block.tensor
        def _(pe):
            mm = pe.matmul

            def slot_ready(gs, i):
                pe.wait_ge(w_loaded[gs[0] % SLOTS], along([16 * (g // SLOTS + 1) for g in gs], i))

            def pair_ready(gs, i, b):
                u = PLAN[gs[0]][b][0]
                if PLAN[gs[0]][b][1] or len(gs) > 1:
                    pe.wait_ge(pair_free[u], along([PLAN[g][b][1] for g in gs], i))
                return u

            def tiles(gs, acc, w0, n, rhs, segs=SEGS, first=True, last=True):
                s = gs[0] % SLOTS
                for k in range(n):
                    for a, b in segs:
                        ins = mm(acc[:, a:b], W[:, s, w0 + k, :], rhs(k)[:, a:b],
                                 start=first and k == 0, stop=last and k == n - 1)
                ins.then_inc(blocks_done, 1)

            def two_blocks(gs, i, rhs, segs=SEGS, between=None):
                slot_ready(gs, i)
                for b in range(2):
                    u = pair_ready(gs, i, b)
                    tiles(gs, pair(u), b * KT, KT, rhs, segs)
                    if b == 0 and between:
                        between()

            def one_block(gs, i, n, rhs, segs=SEGS):
                slot_ready(gs, i)
                u = pair_ready(gs, i, 0)
                half = n // 2
                tiles(gs, pair(u), 0, half, rhs, segs, True, False)
                tiles(gs, pair(u), half, n - half, lambda k: rhs(half + k), segs, False, True)

            def ada(gs, i):
                slot_ready(gs, i)
                s = gs[0] % SLOTS
                layer = JOBS[gs[0]][1]
                ns = [JOBS[g][2] for g in gs]
                for b in range(2):
                    at = along([2 * n + b for n in ns], i)
                    col = at * 2 + 96 * layer
                    dst = PS[:, 7, bass.ds(col, 2)] if not isinstance(col, int) else PS[:, 7, col:col + 2]
                    for k in range(KT):
                        ins = mm(dst, W[:, s, b * KT + k, :], CS[:, k, :], start=k == 0, stop=k == KT - 1)
                    ins.then_inc(blocks_done, 1)

            hn = lambda k: HN[:, k, :]

            def norm_sums(k0, segs=SEGS, after=None):
                if after:
                    pe.wait_ge(pair_free[2], uses(2, after))
                for k in range(KT):
                    pe.wait_ge(sq_ready, k0 + k + 1)
                    for a, b in segs:
                        ins = mm(TP[:, a:b], C[:, ONES, :], T[:, k % 2, a:b], start=k == 0, stop=k == KT - 1)
                    ins.then_inc(sq_mm, 1)

            pe.wait_ge(c_in, 16)
            pe.wait_ge(silu_c, 1)
            for n in range(16):
                ada([AT["ada_a"] + n], 0)

            pe.wait_ge(small_in, 16 * 6)
            for layer in range(3):
                if layer:
                    pe.wait_ge(mlp_sin, layer)
                for a, b in SEGS:
                    if layer == 0:
                        ins = mm(PSF[0:64, a:b], W1S[0:HY_EMB, :], ZT[0:HY_EMB, a:b], start=True, stop=True)
                    else:
                        ins = mm(PSF[0:64, a:b], WS[0:64, layer - 1, :], HF[0:64, layer - 1, a:b],
                                 start=True, stop=True)
                ins.then_inc(mlp_mm, 1)
            pe.wait_ge(mlp_sin, 3)
            pe.wait_ge(t3_in, 16)
            for c in range(2):
                def squares(t):
                    pe.wait_ge(kg_sq, 6 * c + t + 1)
                    if c and t in (0, 4):
                        pe.wait_ge(kg_root, 2 * c)
                    acc = PS[:, 4 + (t >= 4), :]
                    for j in range(2):
                        ins = mm(acc, C[:, ONES, :], SQ2[:, j, :], start=t in (0, 4) and j == 0,
                                 stop=t in (3, 5) and j == 1)
                    ins.then_inc(kg_ssq, 1)

                for t in range(6):
                    n = 6 * c + t
                    if n >= 2:
                        pe.wait_ge(kg_free, n - 1)
                    if c and t < 2:
                        pe.wait_ge(kd_ev, 12 * c)
                    for j in range(2):
                        ins = mm(PS[:, 2 * (n % 2) + j, :], HF[0:64, 2, t * P:t * P + P],
                                 W4[0:64, D * j + 512 * c:D * j + 512 * c + 512], start=True, stop=True)
                    ins.then_inc(kg_mm, 1)
                    if t:
                        squares(t - 1)
                squares(5)
                for f in range(6):
                    lat = f < 4
                    ts = range(4) if lat else range(4, 6)
                    L = LAT if lat else CTX
                    for j in range(2):
                        n = 12 * c + 2 * f + j
                        pe.wait_ge(kg_free, 6 * (c + 1))
                        if n >= 4:
                            pe.wait_ge(kd_ev, n - 3)
                        tab = C3[:, j, :]
                        for t in ts:
                            o = (t * 512 + f * P) if lat else (2048 + (t - 4) * 256 + (f - 4) * P)
                            ins = mm(PS[:, n % 4, :], tab[:, o:o + P], SD[:, j, t, :],
                                     start=t == ts[0], stop=t == ts[-1])
                        ins.then_inc(kd_mm, 1)

            norm_sums(0)
            pe.wait_ge(hn_ready, 16)
            pe.wait_ge(kd_ev, 24)

            def transposes_u(i, first=False):
                pe.wait_ge(u_ready, i + 1)
                if not first:
                    pe.wait_ge(tp_copied, i)
                for t in range(6):
                    ins = pe.transpose(TP[:, t * P:t * P + P], T[:, 2, t * P:t * P + P], C[:, IDENT, :])
                ins.then_inc(tp_mm, 1)

            def uv(i, gs, between=None):
                two_blocks(gs, i, hn, between=between)
                ada([g + 1 for g in gs], i)
                ada([g + 2 for g in gs], i)

            uv(0, [AT["uv"]])
            uv(0, [AT["uv"] + 3], lambda: transposes_u(0, True))
            with pe.Fori(0, 6) as i:
                uv(i, [AT["uv"] + 3 * (n + 2) for n in range(6)], lambda: transposes_u(i + 1))
            transposes_u(7)

            pe.wait_ge(tp_copied, 8)
            pe.wait_ge(t4_in, 16)
            for c in range(2):
                for f in range(6):
                    lat = f < 4
                    ts = range(4) if lat else range(4, 6)
                    n = 6 * c + f
                    if n < 2:
                        pe.wait_ge(pair_free[n % 2], uses(n % 2, AT["x0"]))
                    else:
                        pe.wait_ge(u_prod, n - 1)
                    for j in range(2):
                        tab = C4[:, j, :]
                        for t in ts:
                            o = (t * 512 + f * P) if lat else (2048 + (t - 4) * 256 + (f - 4) * P)
                            ins = mm(PS[:, 2 * (n % 2) + j, :], tab[:, o:o + P],
                                     UT[:, t, 4 * c:4 * c + 4, :].rearrange("p a b -> p (a b)"),
                                     start=t == ts[0], stop=t == ts[-1])
                    ins.then_inc(u_mm, 1)

            pe.wait_ge(u_prod, 12)
            for n in range(4):
                g = AT["x0"] + 3 * n
                two_blocks([g], 0, hn)
                ada([g + 1], 0)
                ada([g + 2], 0)
                pe.wait_ge(p_ready, 12)
                for b in range(2):
                    j = 2 * n + b
                    if j:
                        pe.wait_ge(g_ready, j)
                    for f in range(4):
                        for q in range(2):
                            mm(TP[:, 0:LAT], KS[:, q, f, j * P:j * P + P], C4[:, q, f * 512:f * 512 + 512],
                               start=f == 0 and q == 0, stop=f == 3 and q == 1)
                    for f in range(2):
                        for q in range(2):
                            o = 2048 + f * 256
                            ins = mm(TP[:, LAT:TOK], KS[:, q, 4 + f, j * P:j * P + P], C4[:, q, o:o + 256],
                                     start=f == 0 and q == 0, stop=f == 1 and q == 1)
                    ins.then_inc(inv_mm, 1)

            def z_turn(i):
                gs = [AT["z"] + 3 * n for n in range(4)]
                two_blocks(gs, i, hn)
                ada([g + 1 for g in gs], i)
                ada([g + 2 for g in gs], i)
            loops(pe, 4, z_turn)

            pe.wait_ge(g_ready, 8)

            def transposes_x(n):
                for b in range(2):
                    blk = 2 * n + b
                    pe.wait_ge(xs_ready, blk + 1)
                    if blk:
                        pe.wait_ge(xt_copied, blk)
                    for t in range(6):
                        ins = pe.transpose(TP[:, t * P:t * P + P], XBC[:, blk, t * P:t * P + P], C[:, IDENT, :])
                    ins.then_inc(xt_mm, 1)

            for n in range(6):
                two_blocks([AT["xbc"] + n], 0, hn)
                if n:
                    transposes_x(n - 1)
            for t in range(6):
                for k in range(KT):
                    ins = mm(PS[:, 6, 32 * t:32 * t + 32], HN[:, k, t * P:t * P + P], WD[:, k, :],
                             start=k == 0, stop=k == KT - 1)
            ins.then_inc(dt_mm, 1)
            pe.wait_ge(dt_a, 1)
            for d in range(2):
                mm(PS[:, 6, 192 * 0 + 96 * d:96 * d + 96].rearrange("p (t h) -> p t h", t=6),
                   C[:, KGTJ if d == 0 else KLTJ, :], DTA[:, :, 16 * d:16 * d + 16], start=True, stop=True)
            mm(PS[:, 6, 192:384], C[:, ONES, :], DTS[:, 192:384], start=True, stop=True).then_inc(dec_mm, 1)

            pe.wait_ge(xs_ready, 12)
            pe.wait_ge(dec_ready, 1)
            pe.wait_ge(mods_b, 1)
            pe.wait_ge(xt_copied, 10)
            for u in range(2):
                pe.wait_ge(pair_free[u], uses(u, AT["out0"]))

            def step(s, d, first):
                pe.wait_ge(s_bst, s + 1)
                if not (isinstance(s, int) and s == 0) and not first:
                    pe.wait_ge(s_cbm, s)
                for g in range(2):
                    ins = mm(PS[:, 5, g * P:g * P + P], BST[:, g, :], CT[g](s), start=True, stop=True)
                ins.then_inc(s_cb, 1)

                def segs(b):
                    pe.wait_ge(s_at, s * 4 + (b + 1))
                    if not (first and b < 2):
                        pe.wait_ge(s_exp, s * 4 + (b - 1))
                    r = b % 2
                    mm(PS[:, 2 * r, :], C[:, KGTJ if d == 0 else KLTJ, :], AT2[:, r, :], start=True, stop=True)
                    mm(PS[:, 2 * r + 1, :], C[:, ONES, :], AT2[:, r, :], start=True, stop=True).then_inc(s_seg, 1)

                def heads(b):
                    if b == 0:
                        pe.wait_ge(s_xdt, s + 1)
                        if not first:
                            pe.wait_ge(s_yadd, s)
                            if not (isinstance(s, int) and s == 1):
                                pe.wait_ge(s_stf, s * 2 - 2)
                    pe.wait_ge(s_mc, s * 4 + (b + 1))
                    r = b % 2
                    for h in range(4 * b, 4 * b + 4):
                        hh = h - 4 * b
                        acc = PSF[64 * (h % 2):64 * (h % 2) + 64, 3072 + P * (h // 2):3072 + P * (h // 2) + P]
                        mm(acc, XDT[:, 64 * h:64 * h + 64], LEB[:, r, hh * P:hh * P + P], start=True, stop=False)
                        ins = mm(acc, HST[:, d, 64 * h:64 * h + 64], LEB[:, r, 512 + hh * P:512 + hh * P + P],
                                 start=False, stop=True)
                    ins.then_inc(s_y, 1)

                segs(0)
                segs(1)
                heads(0)
                segs(2)
                heads(1)
                segs(3)
                heads(2)
                heads(3)
                pe.wait_ge(s_xde, s + 1)
                for g in range(2):
                    if not (first and g == 0):
                        pe.wait_ge(s_stf, s * 2 + g)
                    mm(PS[:, 4, :], BST[:, 2 + g, :], XDE[:, 512 * g:512 * g + 512], start=True, stop=True) \
                        .then_inc(s_st, 1)

            CT = [None, None]
            tile_of = {}

            def run_steps(n, tf, tb, s0):
                def turn(i):
                    for d in range(2):
                        s = i * 2 + (s0 + d)
                        t = tf(i) if d == 0 else tb(i)
                        for g in range(2):
                            CT[g] = (lambda g, t: lambda s: XBC[:, 10 + g, bass.ds(t * P, P)])(g, t)
                        step(s, d, s0 == 0 and d == 0 and peel[0])
                if s0 == 0:
                    peel[0] = True
                    turn(0)
                    peel[0] = False
                    turn(1)
                else:
                    loops(pe, n, turn)
            peel = [False]
            run_steps(2, lambda i: 4 + i, lambda i: 5 - i, 0)
            run_steps(4, lambda i: i * 1, lambda i: i * -1 + 3, 4)

            pe.wait_ge(yz_ready, 8)
            pe.wait_ge(s_exp, 48)
            norm_sums(8)
            pe.wait_ge(yn_ready, 8)
            YG = lambda k: XBC[:, k, :] if k < KT else G[:, k - KT, :]

            def res_block(name, n_tiles, rhs, segs=SEGS, count=8):
                def body(gs, i, r):
                    one_block(gs, i, n_tiles, rhs, segs)
                job_turns(pe, name, count, body)

            res_block("out0", 16, YG)

            def feed_forward(layer, k0, hn0, segs):
                norm_sums(k0, segs, AT[f"up{layer}0"])
                pe.wait_ge(hn_ready, hn0)
                for half in range(2):
                    name = f"{layer}{half}"

                    def up(gs, i, r):
                        two_blocks(gs, i, hn, segs)
                    job_turns(pe, "up" + name, FH, up)
                    pe.wait_ge(pair_free[1], uses(1, AT["up" + name] + FH))
                    res_block("down" + name, FH, lambda k: HID[:, k, :], segs)

            feed_forward(0, 16, 32, SEGS)

            norm_sums(24, after=AT["qkv"])
            pe.wait_ge(hn_ready, 48)
            LS = (SEGS[0],)

            def rotated(b, n):
                read([AT["qkv"] + n // 2], 0, b, pe)
                if n:
                    pe.wait_ge(q_done, n)
                mm(PS[:, 6, :], C[:, ROT, :], T[:, b, 0:LAT], start=True, stop=True).then_inc(q_rot, 1)

            for n in range(4):
                two_blocks([AT["qkv"] + n], 0, hn, LS)
                for b in range(2):
                    rotated(b, 2 * n + b)
            two_blocks([AT["qkv"] + 4], 0, hn)
            for b in range(2):
                rotated(b, 8 + b)
            g = AT["qkv"] + 5
            slot_ready([g], 0)
            for t in range(6):
                for k in range(KT):
                    ins = mm(PSF[:, 2048 + 256 * (t % 4):2048 + 256 * (t % 4) + 256] if t < 4 else
                             PS[:, 7, 256 * (t - 4):256 * (t - 4) + 256],
                             HN[:, k, t * P:t * P + P],
                             W[:, g % SLOTS, 2 * k:2 * k + 2, :].rearrange("p a b -> p (a b)"),
                             start=k == 0, stop=k == KT - 1)
                if t in (3, 5):
                    ins.then_inc(blocks_done, 1)

            pe.wait_ge(k_done, 2)
            pe.wait_ge(v_done, 2)
            for u in range(2):
                pe.wait_ge(pair_free[u], uses(u, AT["out1"]))

            def attend(i, first):
                pe.wait_ge(at_q, i + 1)

                def scores(n):
                    b, h = divmod(n, 4)
                    lo, hi = max(b - 1, 0) * P, min(b + 2, 4) * P
                    w = hi - lo
                    c0 = 512 - w
                    r = n % 2
                    if not (first and n < 2):
                        pe.wait_ge(at_exp, i * 16 + (n - 1))
                    S = PSF[:, 1024 * r:1024 * r + 768]
                    p0 = 64 * (h % 2)
                    q = QG[p0:p0 + 64, h // 2, b * P:b * P + P]
                    mm(S[:, c0:512], q, KG[p0:p0 + 64, lo:hi], start=True, stop=False)
                    if b > 0:
                        mm(S[:, c0:c0 + P], C[:, IDENT, :], C[:, MLEFT, :], start=False, stop=b == 3)
                    if b < 3:
                        mm(S[:, 384:512], C[:, IDENT, :], C[:, MRIGHT, :], start=False, stop=True)
                    mm(S[:, 512:768], q, KG[p0:p0 + 64, LAT:TOK], start=True, stop=True).then_inc(at_s, 1)

                def flip(n):
                    b = n // 4
                    w = (min(b + 2, 4) - max(b - 1, 0)) + 2
                    pe.wait_ge(at_exp, i * 16 + (n + 1))
                    if not (first and n == 0):
                        pe.wait_ge(at_ptc, i * 16 + n)
                    for t in range(w):
                        ins = pe.transpose(PSF[:, 2048 + t * P:2048 + t * P + P], PR[:, n % 2, t * P:t * P + P],
                                           C[:, IDENT, :])
                    ins.then_inc(at_pt, 1)

                def values(n):
                    b, h = divmod(n, 4)
                    lo, w = max(b - 1, 0), (min(b + 2, 4) - max(b - 1, 0)) + 2
                    pe.wait_ge(at_ptc, i * 16 + (n + 1))
                    if h == 0 and not (first and b == 0):
                        pe.wait_ge(at_o, i * 4 + b)
                    for t in range(w):
                        kt = lo + t if t < w - 2 else 4 + t - (w - 2)
                        ins = mm(PS[:, 6, 64 * h:64 * h + 64], PTS[:, n % 2, t * P:t * P + P],
                                 VG[:, kt, :],
                                 start=t == 0, stop=t == w - 1)
                    ins.then_inc(at_pv, 1)

                def out_t(b):
                    pe.wait_ge(at_o, i * 4 + (b + 1))
                    if not (first and b == 0):
                        pe.wait_ge(at_otc, i * 4 + b)
                    for j in range(2):
                        ins = pe.transpose(PS[:, 7, j * P:j * P + P],
                                           OTOK[:, b, 2 * j:2 * j + 2, :].rearrange("p a b -> p (a b)"),
                                           C[:, IDENT, :])
                    ins.then_inc(at_ot, 1)

                for n in range(16 + 3):
                    if n < 16:
                        scores(n)
                    if 1 <= n <= 16:
                        flip(n - 1)
                    if 2 <= n <= 17:
                        values(n - 2)
                    if n >= 6 and (n - 6) % 4 == 0:
                        out_t((n - 6) // 4)

            attend(0, True)
            with pe.Fori(1, KV) as i:
                attend(i, False)

            pe.wait_ge(at_otc, 16)

            def out1(gs, i, r):
                two_blocks(gs, i, lambda k: OT[:, k, :], LS)
            job_turns(pe, "out1", 4, out1)
            feed_forward(1, 32, 56, LS)
            norm_sums(40, LS, len(JOBS))

        @block.scalar
        def _(act):
            ch = Count(act, a_ch)
            run = act.activation
            Id = ACT.Identity

            def apart():
                act.wait_ge(v_in, 16)

            act.dma_start(V[:, 0:VEC_W - 2], A["vec"]).then_inc(v_in, 16)
            act.dma_start(C[:, :, :], A["const"].rearrange("p (a b) -> p a b", a=9)).then_inc(c_in, 16)
            act.dma_start(ZT[0:HY_EMB, :], A["zfeat"]).then_inc(small_in, 16)
            act.dma_start(W1S[0:HY_EMB, :], A["hy_w1"]).then_inc(small_in, 16)
            act.dma_start(WS[0:64, 0, :], A["hy_w2"]).then_inc(small_in, 16)
            act.dma_start(WS[0:64, 1, :], A["hy_w3"]).then_inc(small_in, 16)
            act.dma_start(FBV[0:64, 0:6], A["hy_fb"]).then_inc(small_in, 16)
            act.dma_start(W4[0:64, :], A["hy_w4"]).then_inc(small_in, 16)
            act.dma_start(C3[:, :, :], A["tab3"].rearrange("p (a b) -> p a b", a=2)).then_inc(t3_in, 16)
            act.dma_start(WIN[:, :, :], A["window"][:, 0, :, :]).then_inc(win_in, 16)
            act.dma_start(BB[:, :], A["hy_bias"][0:1, 0:512].broadcast_to([P, 512])).then_inc(bias_in, 16)
            act.dma_start(X[:, :, :], A["xT"]).then_inc(x_in, 16)
            act.dma_start(WD[:, :, :], A["w_dt"]).then_inc(x_in, 16)

            act.wait_ge(v_in, 16)
            act.wait_ge(eps_ready, 1)
            run(CS[:, :, :], V[:, _cols["cc"]:_cols["cc"] + 16].rearrange("p (k c) -> p k c", c=2),
                ACT.Silu).then_inc(silu_c, 1)

            for layer in range(3):
                act.wait_ge(mlp_mm, layer + 1)
                act.wait_ge(fb_ready, 1)
                run(HF[0:64, layer, :], PSF[0:64, 0:TOK], Id, scale=FBV[0:64, layer:layer + 1],
                    bias=FBV[0:64, 6 + layer:7 + layer]).then_inc(mlp_arg, 1)
                act.wait_ge(mlp_red, layer + 1)
                run(HF[0:64, layer, :], HF[0:64, layer, :], ACT.Sin).then_inc(mlp_sin, 1)
            for c in range(2):
                for t in range(6):
                    n = 6 * c + t
                    act.wait_ge(kg_sd, n + 1)
                    if n:
                        act.wait_ge(kg_ssq, n)
                    run(SQ2[:, :, :], SD[:, :, t, :], ACT.Square).then_inc(kg_sq, 1)
                    if t in (3, 5):
                        act.wait_ge(kg_ssq, n + 1)
                        j = t == 5
                        if c:
                            act.wait_ge(kd_ev, 12)
                        run(INV[:, j, :], PS[:, 4 + j, :], ACT.Sqrt, scale=0.5, bias=vec("eps", 0)) \
                            .then_inc(kg_root, 1)

            def norm(k0, root0, src, segs=SEGS, gain=None, dst=None, prep=None):
                lo, hi = segs[0][0], segs[-1][1]
                for k in range(KT):
                    if prep:
                        prep(k)
                    if k >= 2:
                        act.wait_ge(sq_mm, k0 + k - 1)
                    run(T[:, k % 2, lo:hi], src(k)[:, lo:hi], ACT.Square).then_inc(sq_ready, 1)
                act.wait_ge(sq_mm, k0 + KT)
                run(T[:, 2, lo:hi], TP[:, lo:hi], ACT.Sqrt, scale=1.0 / D, bias=vec("eps", 0)).then_inc(n_sqrt, 1)
                for k in range(KT):
                    act.wait_ge(n_mul, k0 + k + 1)
                    gain(k)

            def modulated(which, layer, shift, segs=SEGS):
                def gain(k):
                    for j, (a, b) in enumerate(segs):
                        run(HN[:, k, a:b], HN[:, k, a:b], Id, scale=GA[:, which, k, j:j + 1],
                            bias=MOD[:, layer, 8 * shift + k, j:j + 1]).then_inc(hn_ready, 1)
                    if len(segs) == 1:
                        pass
                return gain

            act.wait_ge(x_in, 32)
            act.wait_ge(gains_ready, 1)
            act.wait_ge(kd_ev, 24)
            norm(0, 0, lambda k: X[:, k, :], gain=modulated(0, 0, 0))

            def conv_first(gs, i, b, wname, bname, blk, tbuf, wait=None):
                act.wait_ge(blocks_done, along([2 * g + 1 + b for g in gs], i))
                if wait:
                    wait()
                u = PLAN[gs[0]][b][0]
                apart()
                run(T[:, tbuf, :], pair(u), Id, scale=blk(wname), bias=blk(bname)).then_inc(cv_act, 1)

            act.wait_ge(kd_mm, 24)
            act.dma_start(C4[:, :, :], A["tab4"].rearrange("p (a b) -> p a b", a=2)).then_inc(t4_in, 16)

            def uv(gs, i, first):
                for b in range(2):
                    def free():
                        if not first:
                            act.wait_ge(u_ready, i)
                    conv_first(gs, i, b, "hcw", "hcb", lambda nm: dvec(nm, (24 if nm == "hcw" else 0) + 8 + 8 * b, nm_i), b,
                               free)
                    if b == 0 and not first:
                        copy_u(i - 1)

            def copy_u(i):
                act.wait_ge(tp_mm, i + 1)
                apart()
                dst = UT[:, :, bass.ds(i, 1) if not isinstance(i, int) else slice(i, i + 1), :]
                run(dst, TP.rearrange("p (t a c) -> p t a c", t=6, a=1), ACT.Copy).then_inc(tp_copied, 1)

            firstj = AT["uv"]
            nm_i = 0
            uv([firstj], 0, True)
            with act.Fori(1, 8) as i:
                nm_i = i
                gs = [firstj + 3 * n for n in range(8)]
                uv(gs, i, False)
            copy_u(7)

            for n in range(4):
                g = AT["x0"] + 3 * n
                for b in range(2):
                    j = 2 * n + b

                    def free():
                        if j >= 2:
                            act.wait_ge(g_ready, j - 1)
                        else:
                            act.wait_ge(p_ready, 12)
                    conv_first([g], 0, b, "hcw", "hcb", lambda nm: dvec(nm, (24 if nm == "hcw" else 0), j), b, free)

            act.wait_ge(inv_mm, 8)

            def z_turn(i):
                gs = [AT["z"] + 3 * n for n in range(4)]
                for b in range(2):
                    act.wait_ge(blocks_done, along([2 * g + 1 + b for g in gs], i))
                    apart()
                    blk = i * 2 + b
                    dst = Z[:, blk, :] if isinstance(blk, int) else \
                        Z[:, bass.ds(blk, 1), :].rearrange("p a b -> p (a b)")
                    run(dst, pair(b), ACT.Silu).then_inc(pair_free[b], 1)
            loops(act, 4, z_turn)

            def copy_x(blk):
                act.wait_ge(xt_mm, blk + 1)
                if blk < 8:
                    dst = XT_[:, :, blk, :]
                else:
                    dst = BT[:, :, blk - 8, :]
                run(dst, TP.rearrange("p (t c) -> p t c", t=6), ACT.Copy).then_inc(xt_copied, 1)

            for n in range(6):
                g = AT["xbc"] + n
                for b in range(2):
                    blk = 2 * n + b

                    def free():
                        if blk < 2:
                            act.wait_ge(g_ready, 8)
                    if blk >= 2:
                        act.wait_ge(xs_ready, blk - 1)
                    conv_first([g], 0, b, "scw", "scb", lambda nm: dvec(nm, (12 if nm == "scw" else 0), blk), b, free)
                for b in range(2):
                    blk = 2 * n + b
                    read([g], 0, b, act)
                    run(XBC[:, blk, :], T[:, b, :], ACT.Silu).then_inc(xs_ready, 1)
                if n:
                    copy_x(2 * n - 2)
                    copy_x(2 * n - 1)
            act.wait_ge(dta_raw, 1)
            run(SPU[:, 1, :], SPU[:, 0, :], ACT.Exp, scale=-1.0).then_inc(sp_exp, 1)
            run(vec("alog", 0, 32), vec("alog", 0, 32), ACT.Exp).then_inc(sp_exp, 1)
            act.wait_ge(dec_mm, 1)
            run(DEC, PS[:, 6, 0:384], ACT.Exp).then_inc(dec_ready, 1)
            for k in range(KT):
                act.wait_ge(xt_mm, 10)
                run(XBC[:, k, :], XBC[:, k, :], ACT.Copy, scale=vec("dskip", k)).then_inc(dx_ready, 1)

            def step(s, t, first):
                if not first:
                    act.wait_ge(s_st, s * 2)
                src = XBC[:, 8:10, bass.ds(t * P, P)]
                apart()
                run(BST[:, 0:2, :], src, ACT.Copy)
                bt = BT[:, bass.ds(t, 1), :, :].rearrange("p a b c -> p (a b) c") if not isinstance(t, int) \
                    else BT[:, t, :, :]
                run(BST[:, 2:4, :], bt, ACT.Copy).then_inc(s_bst, 1)
                for b in range(4):
                    act.wait_ge(s_seg, s * 4 + (b + 1))
                    if not (first and b < 2):
                        act.wait_ge(s_y, s * 4 + (b - 1))
                    r = b % 2
                    run(LEB[:, r, :], PSF[:, 1024 * r:1024 * r + 1024], ACT.Exp).then_inc(s_exp, 1)

            def both(i, s0, tf, tb):
                step(i * 2 + s0, tf(i), s0 == 0 and isinstance(i, int) and i == 0)
                step(i * 2 + (s0 + 1), tb(i), False)
            for i in range(2):
                both(i, 0, lambda i: 4 + i, lambda i: 5 - i)
            loops(act, 4, lambda i: both(i, 4, lambda i: i * 1, lambda i: i * -1 + 3))

            def yz(k):
                act.wait_ge(yz_ready, k + 1)

            def gain_y(k):
                run(XBC[:, k, :], XBC[:, k, :], ACT.Copy, scale=vec("sng", k)).then_inc(yn_ready, 1)
            norm(8, 0, lambda k: XBC[:, k, :], gain=gain_y, prep=yz)

            def feed_forward(layer, k0, which, segs, resname):
                def wait_res(k):
                    residual(k, resname, act)
                norm(k0, 0, lambda k: X[:, k, :], segs, modulated(which, layer, 3, segs), prep=wait_res)
                lo, hi = segs[0][0], segs[-1][1]
                for half in range(2):
                    name = f"up{layer}{half}"

                    def up(gs, i, r):
                        act.wait_ge(blocks_done, along([2 * g + 1 for g in gs], i))
                        act.wait_ge(pair_free[1], along([PLAN[g][1][1] for g in gs], i))
                        run(T[:, 0, lo:hi], pair(0)[:, lo:hi], ACT.Silu).then_inc(pair_free[0], 1)
                    job_turns(act, name, FH, up)

            feed_forward(0, 16, 1, SEGS, "out0")

            norm(24, 0, lambda k: X[:, k, :], gain=modulated(2, 1, 0),
                 prep=lambda k: residual(k, "down01", act))
            for n in range(5):
                g = AT["qkv"] + n
                w = LAT if n < 4 else TOK
                for b in range(2):
                    m = 2 * n + b
                    act.wait_ge(blocks_done, 2 * g + 1 + b)
                    if m >= 2:
                        act.wait_ge(q_done, m - 1)
                    run(T[:, b, 0:w], pair(b)[:, 0:w], ACT.Copy).then_inc(pair_free[b], 1)
            g = AT["qkv"] + 5
            act.wait_ge(blocks_done, 2 * g + 1)
            run(VT[:, 0:4, :], PSF[:, 2048:3072].rearrange("p (t c) -> p t c", t=4), ACT.Copy).then_inc(v_done, 1)
            act.wait_ge(blocks_done, 2 * g + 2)
            run(VT[:, 4:6, :], PS[:, 7, :].rearrange("p (t c) -> p t c", t=2), ACT.Copy).then_inc(v_done, 1)

            def attend(i, first):
                act.wait_ge(q_done, 10)
                if not first:
                    act.wait_ge(at_pv, i * 16)
                act.wait_ge(k_done, 2)
                act.wait_ge(v_done, 2)
                apart()
                at = i * 4 + _cols["sink"]
                run(AST[:, 200:204], V[:, bass.ds(at, 4)], ACT.Copy).then_inc(at_group, 1)
                run(KG, KD[:, bass.ds(i, 1), :].rearrange("p a b -> p (a b)"), ACT.Copy)
                run(VG[:, :, :], VT[:, :, bass.ds(i * 64, 64)], ACT.Copy)
                src = QT[:, bass.ds(i * 2, 2), :] if not isinstance(i, int) else QT[:, 2 * i:2 * i + 2, :]
                run(QG[:, :, :], src, ACT.Copy).then_inc(at_q, 1)
                act.wait_ge(at_group, i + 1)

                def probs(n):
                    b, h = divmod(n, 4)
                    w = (min(b + 2, 4) - max(b - 1, 0) + 2) * P
                    c0 = 768 - w
                    act.wait_ge(at_neg, i * 16 + (n + 1))
                    if not (first and n < 2):
                        act.wait_ge(at_pt, i * 16 + (n - 1))
                    r = n % 2
                    run(AST[:, 64 + n:65 + n], AST[:, 200 + h:201 + h], ACT.Exp, bias=AST[:, 32 + n:33 + n]) \
                        .then_inc(at_sinkexp, 1)
                    run(PR[:, r, 0:w], PSF[:, 1024 * r + c0:1024 * r + 768], ACT.Exp, scale=ATTN_SCALE,
                        bias=AST[:, 32 + n:33 + n], accum_out=AST[:, 96 + n:97 + n]).then_inc(at_exp, 1)

                def out_copy(b):
                    act.wait_ge(at_ot, i * 4 + (b + 1))
                    apart()
                    dst = OT[:, bass.ds(i * 2, 2), b * P:b * P + P] if not isinstance(i, int) else \
                        OT[:, 2 * i:2 * i + 2, b * P:b * P + P]
                    run(dst, PS[:, 7, 0:256].rearrange("p (a c) -> p a c", a=2), ACT.Copy).then_inc(at_otc, 1)

                for n in range(16 + 3):
                    if n < 16:
                        probs(n)
                    if n >= 7 and (n - 7) % 4 == 0:
                        out_copy((n - 7) // 4)
                out_copy(3)

            attend(0, True)
            with act.Fori(1, KV) as i:
                attend(i, False)

            feed_forward(1, 32, 3, (SEGS[0],), "out1")

            def gain_f(k):
                ins = run(HN[:, k, 0:LAT], HN[:, k, 0:LAT], ACT.Copy, scale=vec("fin", k))
                ins.then_inc(fin_ready, 1)
            norm(40, 0, lambda k: X[:, k, :], (SEGS[0],), gain_f,
                 prep=lambda k: residual(k, "down11", act))

        @block.vector
        def _(dve):
            ch = Count(dve, v_ch)
            TS, TT, STT = dve.tensor_scalar, dve.tensor_tensor, dve.scalar_tensor_tensor

            def halves(ap, n):
                return ap.rearrange("p (a c) -> p a c", a=n)

            dve.wait_ge(small_in, 16 * 6)
            TT(FBV[0:64, 6:9], FBV[0:64, 0:3], FBV[0:64, 3:6], ALU.mult).then_inc(fb_ready, 1)

            MAGIC = 1.5 * 2.0 ** 23
            TWO_PI_HI, TWO_PI_LO = 6.28125, 2 * float(np.pi) - 6.28125
            PI_IN = 3.1415925
            for layer in range(3):
                dve.wait_ge(mlp_arg, layer + 1)
                h, q = HF[0:64, layer, :], T[0:64, 0, :]
                ch.link(TS(q, h, 1.0 / (2 * float(np.pi)), MAGIC, ALU.mult, ALU.add))
                ch.link(TS(q, q, MAGIC, None, ALU.subtract))
                ch.link(STT(h, q, -TWO_PI_HI, h, ALU.mult, ALU.add))
                ch.link(STT(h, q, -TWO_PI_LO, h, ALU.mult, ALU.add))
                TS(h, h, PI_IN, -PI_IN, ALU.min, ALU.max).then_inc(mlp_red, 1)

            def mods(layer, lo, hi):
                ab = V[:, _cols["ada_b"] + 48 * layer + lo:_cols["ada_b"] + 48 * layer + hi]
                return TT(MOD[:, layer, lo:hi, :], MODP[:, layer, lo:hi, :],
                          ab.unsqueeze(2).broadcast_to([P, hi - lo, 2]), ALU.add)

            def gains(which, layer, m, name):
                g = vec(name, 8 * layer, 8).unsqueeze(2).broadcast_to([P, KT, 2])
                return STT(GA[:, which, :, :], MOD[:, layer, 8 * m:8 * m + 8, :], 1.0, g, ALU.add, ALU.mult)

            dve.wait_ge(v_in, 16)
            dve.wait_ge(blocks_done, 2 * AT["uv"])
            mods(0, 0, 16)
            ch.link(mods(1, 0, 16))
            gains(0, 0, 1, "n1").then_inc(gains_ready, 1)

            hf, hb = Tt[:, 0:512], Tt[:, 512:1024]
            for c in range(2):
                for t in range(6):
                    n = 6 * c + t
                    if t == 0:
                        dve.wait_ge(win2_in if c else win_in, 16)
                        if c:
                            dve.wait_ge(kd_mm, 12)
                    dve.wait_ge(kg_mm, n + 1)
                    TT(hf, PS[:, 2 * (n % 2), :], WIN[:, t, :], ALU.mult)
                    ins = TT(hb, PS[:, 2 * (n % 2) + 1, :], WIN[:, t, :], ALU.mult)
                    ins.then_inc(kg_free, 1)
                    dve.wait_ge(kg_free, n + 1)
                    if t in (0, 4):
                        ch.link(dve.memset(hb[0:1, :], 0.0))
                    TT(SD[:, 0, t, :], hf, hb, ALU.add)
                    TT(SD[:, 1, t, :], hf, hb, ALU.subtract).then_inc(kg_sd, 1)
                    dve.wait_ge(kg_sd, n + 1)
                dve.wait_ge(kg_root, 2 * c + 2)
                dve.wait_ge(bias2_in if c else bias_in, 16)
                ch.link(dve.reciprocal(INV[:, :, :], INV[:, :, :]))
                for f in range(6):
                    inv = INV[:, f >= 4, :]
                    for j in range(2):
                        n = 12 * c + 2 * f + j
                        dst = KS[:, j, f, 512 * c:512 * c + 512]
                        dve.wait_ge(kd_mm, n + 1)
                        ins = TT(dst, PS[:, n % 4, :], inv, ALU.mult)
                        if j == 0:
                            ch.link(ins)
                            ins = TT(dst, dst, BB[:, :], ALU.add)
                        ins.then_inc(kd_ev, 1)

            def norm(k0, src, dst, segs=SEGS):
                lo, hi = segs[0][0], segs[-1][1]
                dve.wait_ge(n_sqrt, k0 // KT + 1)
                ch.link(dve.reciprocal(T[:, 3, lo:hi], T[:, 2, lo:hi]))
                for k in range(KT):
                    TT(dst(k)[:, lo:hi], src(k)[:, lo:hi], T[:, 3, lo:hi], ALU.mult).then_inc(n_mul, 1)

            hn = lambda k: HN[:, k, :]
            xk = lambda k: X[:, k, :]
            norm(0, xk, hn)

            conv_at = [0]

            def conv(gs, i, b, wname, n, blk, count):
                dve.wait_ge(cv_act, count)
                p, t = pair(PLAN[gs[0]][b][0]), T[:, b, :]
                w0, w2 = blk(wname, 0), blk(wname, 2 * n)
                for w, shift in ((w0, -1), (w2, 1)):
                    for j, (lo, hi) in enumerate(SEGS):
                        a, e = (lo + 1, hi) if shift < 0 else (lo, hi - 1)
                        ins = STT(t[:, a:e], p[:, a + shift:e + shift], w, t[:, a:e], ALU.mult, ALU.add)
                    if shift < 0:
                        ch.link(ins)
                ins.then_inc(pair_free[PLAN[gs[0]][b][0]], 1)

            def uv(i):
                gs = [AT["uv"] + 3 * n for n in range(8)]
                for b in range(2):
                    conv(gs, i, b, "hcw", 24, lambda nm, o: dvec(nm, o + 8 + 8 * b, i), i * 2 + (b + 1))
            with dve.Fori(0, 8) as i:
                ch.enter(i, 2)
                uv(i)
                ch.leave(8)

            for c in range(2):
                for f in range(6):
                    n = 6 * c + f
                    kc, ks = (KS[:, j, f, 512 * c:512 * c + 512] for j in range(2))
                    dve.wait_ge(u_mm, n + 1)
                    if n:
                        dve.wait_ge(p_ready, n)
                    uc, us = PS[:, 2 * (n % 2), :], PS[:, 2 * (n % 2) + 1, :]
                    for m, (x, y) in enumerate(((uc, kc), (us, ks), (uc, ks), (us, kc))):
                        ins = TT(Tt[:, 512 * m:512 * m + 512], x, y, ALU.mult)
                    ins.then_inc(u_prod, 1)

            for n in range(4):
                g = AT["x0"] + 3 * n
                for b in range(2):
                    conv([g], 0, b, "hcw", 24, lambda nm, o: dvec(nm, o, 2 * n + b), 16 + 2 * n + b + 1)
                read([g], 0, 1, dve)
                for b in range(2):
                    j = 2 * n + b
                    dve.wait_ge(inv_mm, j + 1)
                    STT(G[:, j, 0:LAT], TP[:, 0:LAT], 1.0 / LAT, T[:, b, 0:LAT], ALU.mult, ALU.mult)
                    STT(G[:, j, LAT:TOK], TP[:, LAT:TOK], 1.0 / CTX, T[:, b, LAT:TOK], ALU.mult, ALU.mult) \
                        .then_inc(g_ready, 1)

            dve.wait_ge(blocks_done, 2 * AT["xbc"])
            mods(0, 16, 48)
            mods(1, 16, 48).then_inc(mods_b, 1)
            dve.wait_ge(mods_b, 1)
            gains(1, 0, 4, "n2").then_inc(pair_free[2], 1)
            gains(2, 1, 1, "n1")
            gains(3, 1, 4, "n2").then_inc(gains_ready, 1)

            for n in range(6):
                for b in range(2):
                    conv([AT["xbc"] + n], 0, b, "scw", 12, lambda nm, o: dvec(nm, o, 2 * n + b), 24 + 2 * n + b + 1)

            dve.wait_ge(dt_mm, 1)
            raw, e, q = SPT, SPU[:, 1, :], SPU[:, 0, :]
            ch.link(TT(raw.rearrange("p (t h) -> p t h", t=6), PS[:, 6, 0:192].rearrange("p (t h) -> p t h", t=6),
                       vec("dtb", 0, 32).unsqueeze(1).broadcast_to([P, 6, 32]), ALU.add))
            STT(q, raw, -1.0, raw, ALU.mult, ALU.max).then_inc(dta_raw, 1)
            dve.wait_ge(sp_exp, 2)
            s2, r = DTS[:, 0:192], DTS[:, 192:384]
            ch.link(TS(r, e, 2.0, None, ALU.add))
            ch.link(dve.reciprocal(r, r))
            ch.link(TT(e, e, r, ALU.mult))
            ch.link(TT(s2, e, e, ALU.mult))
            ch.link(TS(q, s2, 1.0 / 17, None, ALU.mult))
            for m in range(7, 0, -1):
                ch.link(STT(q, q, 1.0 / (2 * m + 1), s2, ALU.add, ALU.mult))
            ch.link(STT(q, q, 1.0, e, ALU.add, ALU.mult))
            ch.link(TS(raw, raw, 0.0, None, ALU.max))
            ch.link(STT(DTS[:, 0:192], q, 2.0, raw, ALU.mult, ALU.add))
            STT(DTA[:, :, :], DTP[:, :, :], -1.0, vec("alog", 0, 32).unsqueeze(1).broadcast_to([P, 6, 32]),
                ALU.mult, ALU.mult).then_inc(dt_a, 1)

            dve.wait_ge(st_zero, 1)
            dve.wait_ge(dec_ready, 1)
            dve.wait_ge(xt_copied, 10)
            dve.wait_ge(dx_ready, KT)

            def at(ap3, t):
                return ap3[:, bass.ds(t, 1), :].rearrange("p a b -> p (a b)")

            DECF = DEC[:, 0:96].rearrange("p (t h) -> p t h", t=6)
            DECB = DEC[:, 96:192].rearrange("p (t h) -> p t h", t=6)
            TOT = DEC[:, 192:384].rearrange("p (t h) -> p t h", t=6)
            XTF = region(6144, 6, D)

            def step(s, d, t, first):
                if not first:
                    dve.wait_ge(s_y, s * 4)
                    dve.wait_ge(s_xde, s)
                TT(XDT.rearrange("p (h c) -> p h c", h=HEADS), at(XTF, t).rearrange("p (h c) -> p h c", h=HEADS),
                   at(DTP, t)[:, 16 * d:16 * d + 16].unsqueeze(2).broadcast_to([P, HEADS, HD]), ALU.mult) \
                    .then_inc(s_xdt, 1)
                dve.wait_ge(s_cb, s + 1)
                mask = C[:, LE if d == 0 else GE, :].unsqueeze(1)
                TT(CBM[:, 0, :, :], PS[:, 5, 0:256].rearrange("p (g c) -> p g c", g=2),
                   mask.broadcast_to([P, 2, P]), ALU.mult).then_inc(s_cbm, 1)
                dve.wait_ge(s_cbm, s + 1)
                for b in range(4):
                    g, r = b // 2, b % 2
                    dve.wait_ge(s_exp, s * 4 + (b + 1))
                    l3 = LEB[:, r, 0:512].rearrange("p (h c) -> p h c", h=4)
                    e3 = LEB[:, r, 512:1024].rearrange("p (h c) -> p h c", h=4)
                    TT(l3, l3, CBM[:, 0, g, :].unsqueeze(1).broadcast_to([P, 4, P]), ALU.mult)
                    ct = XBC[:, 10 + g, bass.ds(t * P, P)].unsqueeze(1)
                    TT(e3, e3, ct.broadcast_to([P, 4, P]), ALU.mult).then_inc(s_mc, 1)
                dve.wait_ge(s_y, s * 4 + 4)
                xs = XBC[:, 0:KT, bass.ds(t * P, P)]
                TT(xs, xs, PSF[:, 3072:4096].rearrange("p (k c) -> p k c", k=KT), ALU.add).then_inc(s_yadd, 1)
                h3 = HST[:, d, :].rearrange("p (h c) -> p h c", h=HEADS)
                ch.link(TT(h3, h3, at(TOT, t)[:, 16 * d:16 * d + 16].unsqueeze(2).broadcast_to([P, HEADS, HD]),
                           ALU.mult))
                for g in range(2):
                    dve.wait_ge(s_st, s * 2 + (g + 1))
                    hg = HST[:, d, 512 * g:512 * g + 512]
                    TT(hg, hg, PS[:, 4, :], ALU.add).then_inc(s_stf, 1)

            def both(i, s0, tf, tb):
                first = s0 == 0 and isinstance(i, int) and i == 0
                step(i * 2 + s0, 0, tf(i), first)
                step(i * 2 + (s0 + 1), 1, tb(i), False)
            for i in range(2):
                both(i, 0, lambda i: 4 + i, lambda i: 5 - i)
            with dve.Fori(0, 4) as i:
                ch.enter(i, 2)
                both(i, 4, lambda i: i * 1, lambda i: i * -1 + 3)
                ch.leave(4)
            dve.wait_ge(s_yadd, 12)

            for k in range(KT):
                TT(XBC[:, k, :], XBC[:, k, :], Z[:, k, :], ALU.mult).then_inc(yz_ready, 1)
            yk = lambda k: XBC[:, k, :]
            norm(8, yk, yk)

            def column(layer, m, k, j):
                c = k * 1 + 8 * m if not isinstance(k, int) else k + 8 * m
                return MOD[:, layer, bass.ds(c, 1), j:j + 1].rearrange("p a b -> p (a b)")

            def res(name, layer, m, segs, two=False):
                def body(gs, i, r):
                    for b in range(2 if two else 1):
                        k = i * SLOTS + r if not two else 2 * r + b
                        dve.wait_ge(blocks_done, along([2 * g + (1 + b if two else 2) for g in gs], i))
                        u = PLAN[gs[0]][b][0]
                        x = X[:, bass.ds(k, 1), :].rearrange("p a b -> p (a b)")
                        for j, (lo, hi) in enumerate(segs):
                            ins = STT(x[:, lo:hi], pair(u)[:, lo:hi], column(layer, m, k, j), x[:, lo:hi],
                                      ALU.mult, ALU.add)
                        ins.then_inc(pair_free[u], 1)
                if two:
                    for r in range(4):
                        body([AT[name] + r], 0, r)
                else:
                    job_turns(dve, name, 8, body)

            def feed_forward(layer, k0, segs):
                norm(k0, xk, hn, segs)
                lo, hi = segs[0][0], segs[-1][1]
                for half in range(2):
                    name = f"{layer}{half}"

                    def up(gs, i, r):
                        dve.wait_ge(blocks_done, along([2 * g + 2 for g in gs], i))
                        read(gs, i, 0, dve)
                        if gs[0] == AT["up" + name] and half == 0:
                            pass
                        n = i * SLOTS + r
                        hid = HID[:, bass.ds(n, 1), :].rearrange("p a b -> p (a b)")
                        TT(hid[:, lo:hi], T[:, 0, lo:hi], pair(1)[:, lo:hi], ALU.mult).then_inc(pair_free[1], 1)
                    job_turns(dve, "up" + name, FH, up)
                    res("down" + name, layer, 5, segs)

            res("out0", 0, 2, SEGS)
            feed_forward(0, 16, SEGS)
            norm(24, xk, hn)

            dve.wait_ge(rope_in, 16)
            for m in range(10):
                b = m % 2
                dve.wait_ge(q_rot, m + 1)
                TT(T[:, 2, 0:LAT], PS[:, 6, :], RC[:, 1, :], ALU.mult)
                ch.link(TT(T[:, 3, 0:LAT], T[:, b, 0:LAT], RC[:, 0, :], ALU.mult))
                dst = QT[:, m, :] if m < 8 else T[:, b, 0:LAT]
                TT(dst, T[:, 3, 0:LAT], T[:, 2, 0:LAT], ALU.add).then_inc(q_done, 1)
                dve.wait_ge(q_done, m + 1)
                if m >= 8:
                    for g in range(2):
                        for half in range(2):
                            ins = dve.tensor_copy(KD[64 * half:64 * half + 64, 2 * b + g, :],
                                                  T[64 * g:64 * g + 64, b, :])
                    ins.then_inc(k_done, 1)

            def attend(i, first):
                def row_max(n):
                    b, h = divmod(n, 4)
                    w = (min(b + 2, 4) - max(b - 1, 0) + 2) * P
                    r = n % 2
                    dve.wait_ge(at_s, i * 16 + (n + 1))
                    ch.link(dve.tensor_reduce(AST[:, n:n + 1], PSF[:, 1024 * r + 768 - w:1024 * r + 768], AX.X, ALU.max))
                    at = i * 4 + (_cols["sink"] + h)
                    sink = V[:, bass.ds(at, 1)]
                    ch.link(TS(AST[:, 16 + n:17 + n], AST[:, n:n + 1], ATTN_SCALE, sink, ALU.mult, ALU.max))
                    TS(AST[:, 32 + n:33 + n], AST[:, 16 + n:17 + n], -1.0, None, ALU.mult).then_inc(at_neg, 1)

                def keys(n):
                    b = n // 4
                    w = (min(b + 2, 4) - max(b - 1, 0) + 2) * P
                    dve.wait_ge(at_pt, i * 16 + (n + 1))
                    if not (first and n < 2):
                        dve.wait_ge(at_pv, i * 16 + (n - 1))
                    dve.tensor_copy(PTS[:, n % 2, 0:w], PSF[:, 2048:2048 + w]).then_inc(at_ptc, 1)

                def outputs(b):
                    dve.wait_ge(at_pv, i * 16 + (4 * b + 4))
                    c = 4 * b
                    ch.link(TT(AST[:, 112 + c:116 + c], AST[:, 64 + c:68 + c], AST[:, 96 + c:100 + c], ALU.add))
                    ch.link(dve.reciprocal(AST[:, 128 + c:132 + c], AST[:, 112 + c:116 + c]))
                    if not first:
                        dve.wait_ge(at_ot, i * 4 + (b - 3))
                    TT(OTOK[:, b, :, :], PS[:, 6, 0:256].rearrange("p (h c) -> p h c", h=4),
                       AST[:, 128 + c:132 + c].unsqueeze(2).broadcast_to([P, 4, HD]), ALU.mult).then_inc(at_o, 1)

                for n in range(16 + 3):
                    if n < 16:
                        row_max(n)
                    if 1 <= n <= 16:
                        keys(n - 1)
                    if n >= 5 and (n - 5) % 4 == 0:
                        outputs((n - 5) // 4)

            attend(0, True)
            with dve.Fori(1, KV) as i:
                ch.enter(i, 2 * 16 + 2 * 4)
                ch.n -= ch.per
                ch.base = ch.n
                attend(i, False)
                ch.leave(KV)

            res("out1", 1, 2, (SEGS[0],), two=True)
            feed_forward(1, 32, (SEGS[0],))
            norm(40, xk, hn, (SEGS[0],))

        @block.gpsimd
        def _(pool):
            TT = pool.tensor_tensor
            pool.memset(vec("eps", 0), EPS).then_inc(eps_ready, 1)
            pool.wait_ge(kg_free, 6)
            pool.dma_start(WIN[:, :, :], A["window"][:, 1, :, :]).then_inc(win2_in, 16)
            pool.wait_ge(kd_ev, 12)
            pool.dma_start(BB[:, :], A["hy_bias"][0:1, 512:1024].broadcast_to([P, 512])).then_inc(bias2_in, 16)

            def product(i, first):
                read([AT["uv"] + 3 * n for n in range(8)], i, 0, pool)
                read([AT["uv"] + 3 * n for n in range(8)], i, 1, pool)
                if not first:
                    pool.wait_ge(tp_mm, i)
                TT(T[:, 2, :], T[:, 0, :], T[:, 1, :], ALU.mult).then_inc(u_ready, 1)
            product(0, True)
            with pool.Fori(1, 8) as i:
                product(i, False)

            for c in range(2):
                for f in range(6):
                    n = 6 * c + f
                    kc, ks = (KS[:, j, f, 512 * c:512 * c + 512] for j in range(2))
                    pool.wait_ge(u_prod, n + 1)
                    TT(kc, Tt[:, 0:512], Tt[:, 512:1024], ALU.subtract)
                    TT(ks, Tt[:, 1024:1536], Tt[:, 1536:2048], ALU.add).then_inc(p_ready, 1)

            pool.wait_ge(xs_ready, XBC_BLKS)
            pool.memset(HST[:, :, :], 0.0).then_inc(st_zero, 1)
            pool.wait_ge(dec_ready, 1)

            def step(s, d, t, first):
                tri = C[:, LE if d == 0 else GE, :].unsqueeze(1).broadcast_to([P, 4, P])

                def ramp(b):
                    if not (first and b < 2):
                        pool.wait_ge(s_seg, s * 4 + (b - 1))
                    a = DTA[:, bass.ds(t, 1), 16 * d + 4 * b:16 * d + 4 * b + 4].rearrange("p a b -> p (a b)")
                    TT(AT2[:, b % 2, :].rearrange("p (h c) -> p h c", h=4), tri,
                       a.unsqueeze(2).broadcast_to([P, 4, P]), ALU.mult).then_inc(s_at, 1)
                ramp(0)
                ramp(1)
                pool.wait_ge(s_xdt, s + 1)
                if not first:
                    pool.wait_ge(s_st, s * 2)
                dec = DEC[:, 96 * d:96 * d + 96].rearrange("p (t h) -> p t h", t=6)
                TT(XDE.rearrange("p (h c) -> p h c", h=HEADS), XDT.rearrange("p (h c) -> p h c", h=HEADS),
                   dec[:, bass.ds(t, 1), :].rearrange("p a b -> p (a b)").unsqueeze(2)
                   .broadcast_to([P, HEADS, HD]), ALU.mult).then_inc(s_xde, 1)
                ramp(2)
                ramp(3)

            def both(i, s0, tf, tb):
                step(i * 2 + s0, 0, tf(i), s0 == 0 and isinstance(i, int) and i == 0)
                step(i * 2 + (s0 + 1), 1, tb(i), False)
            for i in range(2):
                both(i, 0, lambda i: 4 + i, lambda i: 5 - i)
            loops(pool, 4, lambda i: both(i, 4, lambda i: i * 1, lambda i: i * -1 + 3))
            pool.wait_ge(blocks_done, 2 * AT["qkv"])
            pool.dma_start(RC[:, :, :], A["rope"].rearrange("p (a b) -> p a b", a=2)).then_inc(rope_in, 16)


def _constants():
    k = np.arange(P)
    K, J = k[:, None], k[None, :]
    c = np.zeros((P, 9, P), np.float32)
    c[:, IDENT] = K == J
    c[:, ONES] = 1
    c[:, KGTJ] = K > J
    c[:, KLTJ] = K < J
    c[:, LE] = K <= J
    c[:, GE] = K >= J
    for m in range(P):
        c[m + 16 if m % 32 < 16 else m - 16, ROT, m] = -1 if m % 32 < 16 else 1
    c[:, MLEFT] = np.where(J >= K, 0, NEG)
    c[:, MRIGHT] = np.where(J <= K, 0, NEG)

    def table(shift):
        parts = []
        for fn in (np.cos, np.sin):
            cols = []
            for L in (LAT, CTX):
                t, f = np.arange(L)[:, None] + shift, np.arange(L)[None, :] + 0.5
                m = fn(np.pi * t * f / L)
                cols.append(m.reshape(L // P, P, L).transpose(1, 0, 2).reshape(P, -1))
            parts.append(np.concatenate(cols, 1))
        return np.concatenate(parts, 1).astype(np.float32)

    f4 = np.float32
    feats, wins = [], []
    for L in (LAT, CTX):
        t = np.arange(L, dtype=f4)
        unit = t / f4(L - 1)
        ang = f4(2.0 * np.pi) * t / f4(L)
        f = np.linspace(1e-4, HY_BANDS - 1, HY_BANDS, dtype=f4)
        feats.append(np.concatenate([unit[:, None], np.cos(ang[:, None] * f), -np.sin(ang[:, None] * f)], 1).T)
        deltas = np.linspace(np.log(1e-2) / 1.5, np.log(1e-2) / 0.3, D, dtype=f4)
        w = np.exp(-unit[:, None] * np.abs(deltas)[None, :])
        wins.append(w.reshape(L // P, P, 2, 512).transpose(1, 2, 0, 3))
    rows = LAT // GRID_W
    row = np.repeat(np.arange(rows), GRID_W).astype(f4)
    col = np.tile(np.arange(GRID_W), rows).astype(f4)
    inv = f4(ROPE_BASE) ** (-np.arange(16, dtype=f4) / f4(16))
    ang = np.zeros((P, LAT), f4)
    for m in range(P):
        ang[m] = (row if m % 64 < 32 else col) * inv[m % 16]
    rope = np.concatenate([np.cos(ang), np.sin(ang)], 1)
    return {"const": c.reshape(P, 9 * P), "tab3": table(0.0), "tab4": table(0.5),
            "zfeat": np.concatenate(feats, 1).astype(f4), "window": np.concatenate(wins, 2).astype(f4),
            "rope": rope.astype(f4)}


def _layout(a):
    def tiles(w, cols):
        return w[:, cols:cols + P].reshape(-1, P, P).transpose(1, 0, 2)

    hy, z0, x0 = a["hy_in_w"][0], 0, D
    h0 = D + XBC_BLKS * P + 2 * HEADS
    wall = np.zeros((len(JOBS), P, JT, P), np.float32)
    for g, (kind, layer, n) in enumerate(JOBS):
        if kind == "ada":
            two = [(a["ada_w"][layer], (2 * n + b) * P) for b in range(2)]
        elif kind == "uv":
            two = [(hy, h0 + (8 + 8 * b + n) * P) for b in range(2)]
        elif kind == "x0":
            two = [(hy, h0 + (2 * n + b) * P) for b in range(2)]
        elif kind == "z":
            two = [(hy, (2 * n + b) * P) for b in range(2)]
        elif kind == "xbc":
            two = [(hy, D + (2 * n + b) * P) for b in range(2)]
        elif kind == "out0":
            wall[g] = tiles(a["hy_out_w"][0], n * P)
            continue
        elif kind == "up":
            two = [(a["ffn_w_in"][layer], b * FFN + n * P) for b in range(2)]
        elif kind == "down":
            half, blk = n
            wall[g, :, 0:FH] = tiles(a["ffn_w_out"][layer][half * FH * P:(half + 1) * FH * P], blk * P)
            continue
        elif kind in ("q", "k"):
            two = [(a["attn_qkv_w"][0], (8 if kind == "k" else 0) * P + (2 * n + b) * P) for b in range(2)]
        elif kind == "v":
            w = a["attn_qkv_w"][0][:, D + 256:D + 512].reshape(KT, P, 2, P)
            wall[g] = w.transpose(1, 0, 2, 3).reshape(P, JT, P)
            continue
        elif kind == "out1":
            two = [(a["attn_out_w"][0], (2 * n + b) * P) for b in range(2)]
        for b, (w, c) in enumerate(two):
            wall[g, :, KT * b:KT * b + KT] = tiles(w, c)

    def feat(v):
        return v.reshape(-1, P).T

    vec = np.zeros((P, VEC_W - 2), np.float32)

    def put(name, v):
        vec[:, _cols[name]:_cols[name] + v.shape[1]] = v

    put("ada_b", feat(a["ada_b"].reshape(-1)))
    put("n1", feat(a["norm1_g"].reshape(-1)))
    put("n2", feat(a["norm2_g"].reshape(-1)))
    put("fin", feat(a["final_g"]))
    put("sng", feat(a["ssd_norm_g"][0]))
    put("scw", feat(a["ssd_conv_w"][0].reshape(-1)))
    put("scb", feat(a["ssd_conv_b"][0]))
    put("hcw", feat(a["hy_conv_w"][0].reshape(-1)))
    put("hcb", feat(a["hy_conv_b"][0]))
    put("dskip", feat(np.repeat(a["ssd_d"][0], HD)))
    put("cc", np.stack([feat(a["c"][0]), feat(a["c_ctx"])], 2).reshape(P, 16))
    put("sink", np.repeat(a["attn_sinks"][0:1], P, 0))
    put("dtb", np.repeat(a["ssd_dt_bias"].reshape(1, 32), P, 0))
    put("alog", np.repeat(a["ssd_a_log"].reshape(1, 32), P, 0))
    xt = np.concatenate([a["x"][0].T, a["ctx"][0].T], 1)
    wdt = hy[:, D + XBC_BLKS * P:h0]
    return {
        "wall": wall.reshape(len(JOBS), P, JT * P), "vec": vec,
        "xT": xt.reshape(KT, P, TOK).transpose(1, 0, 2), "w_dt": wdt.reshape(KT, P, 32).transpose(1, 0, 2),
        "hy_w1": a["hy_w1"][0], "hy_w2": a["hy_w2"][0], "hy_w3": a["hy_w3"][0], "hy_w4": a["hy_w4"][0],
        "hy_fb": np.concatenate([a["hy_freq"][0].T, np.stack([a["hy_b1"][0], a["hy_b2"][0], a["hy_b3"][0]], 1)], 1),
        "hy_bias": a["hy_bias"],
    }


def kernel(**inputs):
    import concourse.bacc as bacc
    from concourse.bass_utils import run_bass_kernel_spmd as run

    arrays = {k: np.ascontiguousarray(v) for k, v in
              {**_layout({k: np.asarray(v) for k, v in inputs.items()}), **_constants()}.items()}
    nc = bacc.Bacc("TRN2", target_bir_lowering=False, num_devices=1)
    args = {k: nc.dram_tensor(f"in_{k}", v.shape, mybir.dt.from_np(v.dtype), kind="ExternalInput").ap()
            for k, v in arrays.items()}
    out = nc.dram_tensor("out_T", (P, KT, LAT), mybir.dt.float32, kind="ExternalOutput").ap()
    build_kernel(nc, args, out)
    r = run(nc, [{f"in_{k}": v for k, v in arrays.items()}], core_ids=[0])
    y = r.results[0]["out_T"]
    return np.ascontiguousarray(y.transpose(1, 0, 2).reshape(D, LAT).T).reshape(1, LAT, D)
```

```python
import concourse.bass as bass
import numpy as np
from concourse import mybir
from contextlib import ExitStack

D = 1024
LAT, CTX = 512, 256
TOK = LAT + CTX
P = 128
KT = D // P
HEADS, HD, GROUPS, STATE = 16, 64, 2, 128
XBC_BLKS = (D + 2 * GROUPS * STATE) // P
HY_FFN, HY_BANDS = 64, 16
HY_EMB = 1 + 2 * HY_BANDS
NEV = 6
FFN = 2816
FB = FFN // P
FH = FB // 2
KV, QH = 4, 16
EPS = 1e-6
GRID_W = 64
ROPE_BASE = 10000.0
ATTN_SCALE = 64 ** -0.5
NEG = -1.0e30
SLOTS = 3
JT = 16
HALF = JT // 2
DOWN = (6, 5)
SEGS = ((0, LAT), (LAT, TOK))

_cols = {}
_at = 0
for _n, _w in (("ada_b", 2 * 48), ("n1", 16), ("n2", 16), ("fin", 8), ("sng", 8), ("scw", 3 * 12), ("scb", 12),
               ("hcw", 3 * 24), ("hcb", 24), ("dskip", 8), ("cc", 16), ("sink", 16), ("dtb", 32), ("alog", 32),
               ("eps", 2)):
    _cols[_n] = _at
    _at += _w
VEC_W = _at
IDENT, ONES, KGTJ, KLTJ, LE, GE, ROT, MLEFT, MRIGHT = range(9)


def weight_jobs():
    jobs, at = [], {}

    def stage(name, items):
        at[name] = len(jobs)
        jobs.extend(items)

    ada0 = [("ada", 0, n) for n in range(24)]
    ada1 = [("ada", 1, n) for n in range(24)]
    stage("ada_a", ada0[:8] + ada1[:8])
    stage("uv", [j for n in range(8) for j in (("uv", 0, n), ada0[8 + 2 * n], ada0[9 + 2 * n])])
    stage("x0", [j for n in range(4) for j in (("x0", 0, n), ada1[8 + 2 * n], ada1[9 + 2 * n])])
    stage("z", [j for n in range(4) for j in (("z", 0, n), ada1[16 + 2 * n], ada1[17 + 2 * n])])
    stage("xbc", [("xbc", 0, n) for n in range(6)])
    stage("out0", [("out0", 0, n) for n in range(8)])
    for layer in range(2):
        if layer:
            stage("qkv", [("q", 0, n) for n in range(4)] + [("k", 0, 0), ("v", 0, 0)])
            stage("out1", [("out1", 0, n) for n in range(4)])
        for half in range(2):
            stage(f"up{layer}{half}", [("up", layer, half * FH + n) for n in range(FH)])
            stage(f"down{layer}{half}", [("down", layer, (half, n)) for n in range(8)])
    return jobs, at


JOBS, AT = weight_jobs()


def job_blocks(kind):
    return {"ada": 0, "out0": 1, "down": 1, "v": 0}.get(kind, 2)


def plan():
    used, turn, out, last = [0, 0, 1], 0, [], None
    for kind, layer, _ in JOBS:
        n = job_blocks(kind)
        if n == 1 and kind != last:
            turn = 0
        pairs = []
        for u in range(n):
            pair = u if n == 2 else turn
            pairs.append((pair, used[pair]))
            used[pair] += 1
        if n == 1:
            turn = (turn + 1) % 3
        last = kind
        out.append(pairs)
    return out


PLAN = plan()
G0 = AT["out0"]


def width(g, b):
    return DOWN[b] if JOBS[g][0] == "down" else HALF


def uses(u, g):
    return sum(p == u for blocks in PLAN[:g] for p, _ in blocks) + (u == 2)


def along(values, i):
    if isinstance(i, int):
        return values[i]
    step = values[1] - values[0]
    assert all(b - a == step for a, b in zip(values, values[1:])), values
    return i * step + values[0]


class Count:

    def __init__(self, eng, sem):
        self.eng, self.sem, self.n, self.i, self.per = eng, sem, 0, None, 0

    def now(self):
        return self.n if self.i is None else self.i * self.per + self.n

    def inc(self, ins):
        ins.then_inc(self.sem, 1)
        self.n += 1
        return self.now()

    def link(self, ins):
        self.eng.wait_ge(self.sem, self.inc(ins))

    def enter(self, i, per):
        self.i, self.per, self.base = i, per, self.n
        if not isinstance(i, int):
            self.first = True

    def leave(self, times):
        assert self.n - self.base == self.per, (self.n - self.base, self.per)
        self.n = self.base + self.per * times
        self.i = None


def build_kernel(nc, A, out):
    f32 = mybir.dt.float32
    f32r = mybir.dt.float32r
    ALU = mybir.AluOpType
    ACT = mybir.ActivationFunctionType
    AX = mybir.AxisListType
    ctx = ExitStack()
    with ctx:
        def sb(name, shape):
            return ctx.enter_context(nc.sbuf_tensor(name, shape, f32))

        def sem(name):
            return ctx.enter_context(nc.semaphore(name))

        X = sb("residual", [P, KT, TOK])
        hn_at = nc.sbuf_base
        HNt = sb("normed", [P, KT * TOK])
        W = sb("weights", [P, SLOTS, JT, P])
        C = sb("consts", [P, 9, P])
        V = sb("vectors", [P, VEC_W])
        MOD = sb("mods", [P, 2, 48, 2])
        GA = sb("gains", [P, 4, KT, 2])
        CS = sb("silu_c", [P, KT, 2])
        Tt = sb("temps", [P, 4 * TOK])
        r_at = nc.sbuf_base
        R = sb("phase", [P, 29184])

        def part(name, base, at, *dims):
            return nc.alloc_sbuf_tensor_at(name, [P, *dims], f32r, offset=base + 4 * at)

        WH = part("weights_hi", r_at, 24576, 2, HALF, P)
        WL = part("weights_lo", r_at, 24576 + JT * P, 2, HALF, P)
        YGH = part("mixed_hi", r_at, 0, 2, KT, TOK)
        YGL = [part("ssd_lo", r_at, 18432, KT, TOK), part("hyena_lo", r_at, 12288, KT, TOK)]
        HNH = part("normed_hi", r_at, 16896, KT, TOK)
        HNL = part("normed_lo", hn_at, 0, KT, TOK)
        HIDH = part("hidden_hi", r_at, 0, FH, TOK)
        HIDL = part("hidden_lo", r_at, FH * TOK, FH, TOK)
        OTH = part("attended_hi", hn_at, 0, KT, LAT)
        OTL = part("attended_lo", r_at, 16896, KT, LAT)
        HN = HNt[:, :].rearrange("p (k t) -> p k t", k=KT)
        T = Tt[:, :].rearrange("p (k t) -> p k t", k=4)

        def region(at, *dims):
            n = 1
            for d in dims:
                n *= d
            names = "abcd"[:len(dims)]
            ap = R[:, at:at + n]
            if len(dims) == 1:
                return ap
            return ap.rearrange(f"p ({' '.join(names)}) -> p {' '.join(names)}",
                                **{names[i]: dims[i] for i in range(1, len(dims))})

        def inside(base, at, *dims):
            n = 1
            for d in dims:
                n *= d
            names = "abcd"[:len(dims)]
            ap = base[:, at:at + n]
            if len(dims) == 1:
                return ap
            return ap.rearrange(f"p ({' '.join(names)}) -> p {' '.join(names)}",
                                **{names[i]: dims[i] for i in range(1, len(dims))})

        KS = region(0, 2, 6, D)
        UT = region(12288, 6, KT, P)
        G = region(12288, KT, TOK)
        C4 = region(18432, 2, 2560)
        C3 = region(12288, 2, 2560)
        SD = region(17408, 2, 6, 512)
        W4 = region(23552, 2 * D)
        HF = region(25600, 3, TOK)
        WIN = inside(HNt, 0, 6, 512)
        INV = inside(HNt, 3072, 2, 512)
        BB = inside(HNt, 4096, 512)
        SQ2 = inside(HNt, 4608, 2, 512)
        SSA = Tt[:, 1024:2048].rearrange("p (a c) -> p a c", a=2)
        W1S = region(27904, 64)
        WS = region(27968, 2, 64)
        FBV = region(28096, 9)
        ZT = region(28160, TOK)
        Z = region(0, KT, TOK)
        XBC = region(18432, XBC_BLKS, TOK)
        XT_ = region(6144, 6, KT, P)
        BT = region(27648, 6, 2, P)
        QT = region(0, KT, LAT)
        KD = region(4096, KV, TOK)
        VT = region(7168, 6, 256)
        RC = region(8704, 2, LAT)
        QG = region(9728, 2, LAT)
        PR = region(10752, 2, 640)
        PTS = region(12032, 2, 640)
        OTOK = region(13312, 4, 4, HD)
        AST = region(14336, 256)
        KG = region(14592, TOK)
        VG = region(15360, 6, HD)
        WD = sb("w_dt", [P, KT, 32])
        AT2 = inside(HNt, 0, 2, 512)
        LEB = inside(HNt, 1024, 2, 1024)
        XDT = inside(HNt, 3072, 1024)
        XDE = inside(HNt, 4096, 1024)
        BST = inside(HNt, 5120, 4, P)
        CBM = inside(HNt, 5632, 2, 2, P)
        HST = inside(Tt, 0, 2, 1024)
        DTS = inside(Tt, 2048, 1024)
        DTP = DTS[:, 0:192].rearrange("p (t h) -> p t h", t=6)
        DTA = DTS[:, 192:384].rearrange("p (t h) -> p t h", t=6)
        DEC = DTS[:, 384:768]
        SPT = DTS[:, 768:960]
        SPU = sb("softplus_tmp", [P, 2, 192])

        PS = ctx.enter_context(nc.psum_tensor("psum", [P, 8, 512], f32))
        PSF = PS[:, :, :].rearrange("p b c -> p (b c)")

        def pair(u):
            return PSF[:, 1024 * u:1024 * u + TOK]

        TP = PSF[:, 2048:2048 + TOK]
        NP = PSF[:, 3072:3072 + TOK]
        MODP = PS[:, 7, 0:192].rearrange("p (l b c) -> p l b c", l=2, b=48)

        def vec(name, n, w=1):
            return V[:, _cols[name] + n:_cols[name] + n + w]

        def dvec(name, base, i, step=1):
            at = i * step + (_cols[name] + base)
            return V[:, bass.ds(at, 1)] if not isinstance(at, int) else V[:, at:at + 1]

        w_loaded = [[sem(f"w_loaded{s}{b}") for b in range(2)] for s in range(SLOTS)]
        w_hi, w_lo = sem("weights_hi_ready"), sem("weights_lo_ready")
        blocks_done = sem("blocks_done")
        pair_free = [sem(f"pair_free{u}") for u in range(3)]
        a_ch, v_ch, g_ch = sem("act_order"), sem("dve_order"), sem("pool_order")
        x_in, c_in, v_in, small_in, t3_in, t4_in, win_in, rope_in = (
            sem(n) for n in ("x_in", "c_in", "v_in", "small_in", "t3_in", "t4_in", "win_in", "rope_in"))
        silu_c, mods_a, mods_b = sem("silu_c_ready"), sem("mods_a_ready"), sem("mods_b_ready")
        gains_ready = sem("gains_ready")
        names = """filter_bias filter_mm filter_arg filter_reduced filter_sin
            kg_mm kg_free kg_sd kg_sq kg_ssq kg_root kg_order kd_mm kd_ev bias_in
            sq_ready sq_mm norm_sqrt norm_mul hn_ready conv_first
            u_ready tp_mm tp_copied u_mm u_prod p_ready inv_mm g_ready
            x_stored xt_mm xt_copied dt_mm dt_abs dt_exp dt_ready dec_mm dec_ready dx_ready states_zero
            step_at step_seg step_exp step_mc step_y step_cb step_cbm step_xdt step_xde step_st step_added
            step_state step_b yz_ready yn_ready
            q_rot q_done k_done v_done
            at_q at_s at_neg at_sink at_exp at_pt at_ptc at_pv at_o at_ot at_otc
            fin_ready out_done eps_ready win2_in bias2_in at_group
            wdt_in sums_ready norm_summed hn_hi hid_hi hid_ready ssq_added mixed_hi mixed_lo at_othi at_otlo"""
        (fb_ready, mlp_mm, mlp_arg, mlp_red, mlp_sin,
         kg_mm, kg_free, kg_sd, kg_sq, kg_ssq, kg_root, kg_ord, kd_mm, kd_ev, bias_in,
         sq_ready, sq_mm, n_sqrt, n_mul, hn_ready, cv_act,
         u_ready, tp_mm, tp_copied, u_mm, u_prod, p_ready, inv_mm, g_ready,
         xs_ready, xt_mm, xt_copied, dt_mm, dta_raw, sp_exp, dt_a, dec_mm, dec_ready, dx_ready, st_zero,
         s_at, s_seg, s_exp, s_mc, s_y, s_cb, s_cbm, s_xdt, s_xde, s_st, s_yadd,
         s_stf, s_bst, yz_ready, yn_ready,
         q_rot, q_done, k_done, v_done,
         at_q, at_s, at_neg, at_sinkexp, at_exp, at_pt, at_ptc, at_pv, at_o, at_ot, at_otc,
         fin_ready, out_done, eps_ready, win2_in, bias2_in, at_group,
         wdt_in, sums_ready, n_summed, hn_hi, hid_hi, hid_ready, ssq_added, mix_hi, mix_lo, at_othi, at_otlo) = (sem(n) for n in names.split())

        def at_row(ap, k):
            return ap[:, bass.ds(k, 1), :].rearrange("p a b -> p (a b)")

        def read(gs, i, b, eng):
            eng.wait_ge(pair_free[PLAN[gs[0]][b][0]], along([PLAN[g][b][1] + 1 for g in gs], i))

        def loops(eng, n, body, chain=None, per=0):
            if n == 0:
                return
            if n == 1:
                body(0)
                return
            if chain is None:
                with eng.Fori(0, n) as i:
                    body(i)
                return
            with eng.Fori(0, n) as i:
                chain.enter(i, per)
                body(i)
                chain.leave(n)

        def job_turns(eng, name, count, body, chain=None, per=0, peel=0):
            first = AT[name]
            for r in range(peel):
                body([first + r], 0, r)
            full = (count - peel) // SLOTS

            def turn(i):
                for r in range(SLOTS):
                    body([first + peel + n * SLOTS + r for n in range(full)], i, i * SLOTS + (peel + r))
            loops(eng, full, turn, chain, per)
            for r in range(peel + full * SLOTS, count):
                body([first + r], 0, r)

        block = ctx.enter_context(nc.Block())

        @block.sync
        def _(sp):
            def load(gs, i, old):
                s = gs[0] % SLOTS
                for b in range(2):
                    if old == "product":
                        sp.wait_ge(blocks_done, along([2 * (g - SLOTS) + 1 + b for g in gs], i))
                    if old == "split":
                        sp.wait_ge(w_lo, along([2 * (g - SLOTS - G0) + 1 + b for g in gs], i))
                    n = width(gs[0], b)
                    sp.dma_start(W[:, s, HALF * b:HALF * b + n, :],
                                 A["wall"][along(gs, i), :, HALF * b * P:(HALF * b + n) * P].rearrange(
                                     "p (t n) -> p t n", n=P)).then_inc(w_loaded[s][b], 16)

            def run(first, end, old):
                full = (end - first) // SLOTS

                def turn(i):
                    for r in range(SLOTS):
                        load([first + n * SLOTS + r for n in range(full)], i, old)
                loops(sp, full, turn)
                for g in range(first + full * SLOTS, end):
                    load([g], 0, old)

            cuts = {0, SLOTS, G0 + SLOTS, len(JOBS)}
            for g in range(1, len(JOBS)):
                if (JOBS[g][0] == "down") != (JOBS[g - 1][0] == "down"):
                    cuts.add(g)
            cuts = sorted(cuts)
            for lo, hi in zip(cuts, cuts[1:]):
                run(lo, hi, "" if lo < SLOTS else "product" if lo < G0 + SLOTS else "split")
            sp.wait_ge(fin_ready, KT)
            sp.dma_start(out, HN[:, :, 0:LAT]).then_inc(out_done, 16)
            sp.wait_ge(out_done, 16)

        @block.tensor
        def _(pe):
            mm = pe.matmul

            def half_ready(gs, i, b):
                if gs[0] < G0:
                    pe.wait_ge(w_loaded[gs[0] % SLOTS][b], along([16 * (g // SLOTS + 1) for g in gs], i))
                else:
                    pe.wait_ge(w_lo, along([2 * (g - G0) + b + 1 for g in gs], i))

            def pair_ready(gs, i, b):
                u = PLAN[gs[0]][b][0]
                if PLAN[gs[0]][b][1] or len(gs) > 1:
                    pe.wait_ge(pair_free[u], along([PLAN[g][b][1] for g in gs], i))
                return u

            def tiles(gs, acc, b, n, rhs, segs, first, last, by_tile=None):
                s = gs[0] % SLOTS
                for k in range(n):
                    if by_tile:
                        by_tile(k)
                    st, en = first and k == 0, last and k == n - 1
                    if gs[0] < G0:
                        for lo, hi in segs:
                            ins = mm(acc[:, lo:hi], W[:, s, HALF * b + k, :], rhs(k)[:, lo:hi], start=st, stop=en)
                        continue
                    high, low = rhs(k)
                    for lo, hi in segs:
                        mm(acc[:, lo:hi], WH[:, b, k, :], high[:, lo:hi], start=st, stop=False)
                        mm(acc[:, lo:hi], WH[:, b, k, :], low[:, lo:hi], start=False, stop=False)
                    for lo, hi in segs:
                        ins = mm(acc[:, lo:hi], WL[:, b, k, :], high[:, lo:hi], start=False, stop=en)
                ins.then_inc(blocks_done, 1)

            def two_blocks(gs, i, rhs, segs=SEGS, between=None, by_tile=None):
                for b in range(2):
                    half_ready(gs, i, b)
                    u = pair_ready(gs, i, b)
                    tiles(gs, pair(u), b, KT, rhs, segs, True, True, by_tile if b == 0 else None)
                    if b == 0 and between:
                        between()

            def one_block(gs, i, rhs, segs=SEGS, by_tile=None):
                u = pair_ready(gs, i, 0)
                n0 = width(gs[0], 0)
                for b in range(2):
                    half_ready(gs, i, b)
                    tiles(gs, pair(u), b, width(gs[0], b), lambda k: rhs(n0 * b + k), segs, b == 0, b == 1,
                          by_tile and (lambda k: by_tile(n0 * b + k)))

            def ada(gs, i):
                s = gs[0] % SLOTS
                layer = JOBS[gs[0]][1]
                ns = [JOBS[g][2] for g in gs]
                for b in range(2):
                    half_ready(gs, i, b)
                    at = along([2 * n + b for n in ns], i)
                    col = at * 2 + 96 * layer
                    dst = PS[:, 7, bass.ds(col, 2)] if not isinstance(col, int) else PS[:, 7, col:col + 2]
                    for k in range(KT):
                        ins = mm(dst, W[:, s, b * KT + k, :], CS[:, k, :], start=k == 0, stop=k == KT - 1)
                    ins.then_inc(blocks_done, 1)

            hn = lambda k: HN[:, k, :]

            def norm_sums(segs=SEGS):
                for k in range(KT):
                    pe.wait_ge(sq_ready, k + 1)
                    for a, b in segs:
                        ins = mm(NP[:, a:b], C[:, ONES, :], T[:, k % 2, a:b], start=k == 0, stop=k == KT - 1)
                    ins.then_inc(sq_mm, 1)

            def norm_sum(n, segs=SEGS):
                pe.wait_ge(sums_ready, n + 1)
                for a, b in segs:
                    ins = mm(NP[:, a:b], C[:, ONES, :], T[:, 3, a:b], start=True, stop=True)
                ins.then_inc(n_summed, 1)

            pe.wait_ge(c_in, 16)
            pe.wait_ge(silu_c, 1)
            early = list(range(AT["ada_a"], AT["uv"]))

            def fill(n=1):
                for _ in range(min(n, len(early))):
                    ada([early.pop(0)], 0)

            pe.wait_ge(small_in, 16 * 6)
            for layer in range(3):
                if layer:
                    pe.wait_ge(mlp_sin, layer)
                for a, b in SEGS:
                    if layer == 0:
                        ins = mm(PSF[0:64, a:b], W1S[0:HY_EMB, :], ZT[0:HY_EMB, a:b], start=True, stop=True)
                    else:
                        ins = mm(PSF[0:64, a:b], WS[0:64, layer - 1, :], HF[0:64, layer - 1, a:b],
                                 start=True, stop=True)
                ins.then_inc(mlp_mm, 1)
            pe.wait_ge(mlp_sin, 3)
            pe.wait_ge(t3_in, 16)
            for c in range(2):
                for t in range(6):
                    n = 6 * c + t
                    if n >= 2:
                        pe.wait_ge(kg_free, n - 1)
                    if c and t < 2:
                        pe.wait_ge(kd_ev, 12 * c)
                    for j in range(2):
                        ins = mm(PS[:, 2 * (n % 2) + j, :], HF[0:64, 2, t * P:t * P + P],
                                 W4[0:64, D * j + 512 * c:D * j + 512 * c + 512], start=True, stop=True)
                    ins.then_inc(kg_mm, 1)
                    fill()
                pe.wait_ge(ssq_added, 6 * (c + 1))
                if c:
                    pe.wait_ge(kg_root, 1)
                for j in range(2):
                    ins = mm(PS[:, 4 + j, :], C[:, ONES, :], SSA[:, j, :], start=True, stop=True)
                ins.then_inc(kg_ssq, 1)
                for f in range(6):
                    lat = f < 4
                    ts = range(4) if lat else range(4, 6)
                    L = LAT if lat else CTX
                    for j in range(2):
                        n = 12 * c + 2 * f + j
                        pe.wait_ge(kg_free, 6 * (c + 1))
                        if n >= 4:
                            pe.wait_ge(kd_ev, n - 3)
                        tab = C3[:, j, :]
                        for t in ts:
                            o = (t * 512 + f * P) if lat else (2048 + (t - 4) * 256 + (f - 4) * P)
                            ins = mm(PS[:, n % 4, :], tab[:, o:o + P], SD[:, j, t, :],
                                     start=t == ts[0], stop=t == ts[-1])
                        ins.then_inc(kd_mm, 1)
                        fill(j)

            fill(len(early))
            pe.wait_ge(mods_a, 1)
            norm_sum(0)
            pe.wait_ge(kd_ev, 24)
            pe.wait_ge(hn_ready, KT)

            def transposes_u(i, first=False):
                pe.wait_ge(u_ready, i + 1)
                if not first:
                    pe.wait_ge(tp_copied, i)
                for t in range(6):
                    ins = pe.transpose(TP[:, t * P:t * P + P], T[:, 2, t * P:t * P + P], C[:, IDENT, :])
                ins.then_inc(tp_mm, 1)

            def uv(i, gs, between=None):
                two_blocks(gs, i, hn, between=between)
                ada([g + 1 for g in gs], i)
                ada([g + 2 for g in gs], i)

            uv(0, [AT["uv"]])
            uv(0, [AT["uv"] + 3], lambda: transposes_u(0, True))
            with pe.Fori(0, 6) as i:
                uv(i, [AT["uv"] + 3 * (n + 2) for n in range(6)], lambda: transposes_u(i + 1))
            transposes_u(7)

            pe.wait_ge(tp_copied, 8)
            pe.wait_ge(t4_in, 16)
            for c in range(2):
                for f in range(6):
                    lat = f < 4
                    ts = range(4) if lat else range(4, 6)
                    n = 6 * c + f
                    if n < 2:
                        pe.wait_ge(pair_free[n % 2], uses(n % 2, AT["x0"]))
                    else:
                        pe.wait_ge(u_prod, n - 1)
                    for j in range(2):
                        tab = C4[:, j, :]
                        for t in ts:
                            o = (t * 512 + f * P) if lat else (2048 + (t - 4) * 256 + (f - 4) * P)
                            ins = mm(PS[:, 2 * (n % 2) + j, :], tab[:, o:o + P],
                                     UT[:, t, 4 * c:4 * c + 4, :].rearrange("p a b -> p (a b)"),
                                     start=t == ts[0], stop=t == ts[-1])
                    ins.then_inc(u_mm, 1)

            pe.wait_ge(u_prod, 12)
            for n in range(4):
                g = AT["x0"] + 3 * n
                two_blocks([g], 0, hn)
                ada([g + 1], 0)
                ada([g + 2], 0)
                pe.wait_ge(p_ready, 12)
                for b in range(2):
                    j = 2 * n + b
                    if j:
                        pe.wait_ge(g_ready, j)
                    for f in range(4):
                        for q in range(2):
                            mm(TP[:, 0:LAT], KS[:, q, f, j * P:j * P + P], C4[:, q, f * 512:f * 512 + 512],
                               start=f == 0 and q == 0, stop=f == 3 and q == 1)
                    for f in range(2):
                        for q in range(2):
                            o = 2048 + f * 256
                            ins = mm(TP[:, LAT:TOK], KS[:, q, 4 + f, j * P:j * P + P], C4[:, q, o:o + 256],
                                     start=f == 0 and q == 0, stop=f == 1 and q == 1)
                    ins.then_inc(inv_mm, 1)

            def z_turn(i):
                gs = [AT["z"] + 3 * n for n in range(4)]
                two_blocks(gs, i, hn)
                ada([g + 1 for g in gs], i)
                ada([g + 2 for g in gs], i)
            loops(pe, 4, z_turn)

            pe.wait_ge(g_ready, 8)

            def transposes_x(n):
                for b in range(2):
                    blk = 2 * n + b
                    pe.wait_ge(xs_ready, blk + 1)
                    if blk:
                        pe.wait_ge(xt_copied, blk)
                    for t in range(6):
                        ins = pe.transpose(TP[:, t * P:t * P + P], XBC[:, blk, t * P:t * P + P], C[:, IDENT, :])
                    ins.then_inc(xt_mm, 1)

            for n in range(6):
                two_blocks([AT["xbc"] + n], 0, hn)
                if n:
                    transposes_x(n - 1)
            pe.wait_ge(wdt_in, 16)
            for t in range(6):
                for k in range(KT):
                    ins = mm(PS[:, 6, 32 * t:32 * t + 32], HN[:, k, t * P:t * P + P], WD[:, k, :],
                             start=k == 0, stop=k == KT - 1)
            ins.then_inc(dt_mm, 1)
            pe.wait_ge(dt_a, 1)
            for d in range(2):
                mm(PS[:, 6, 192 * 0 + 96 * d:96 * d + 96].rearrange("p (t h) -> p t h", t=6),
                   C[:, KGTJ if d == 0 else KLTJ, :], DTA[:, :, 16 * d:16 * d + 16], start=True, stop=True)
            mm(PS[:, 6, 192:384], C[:, ONES, :], DTS[:, 192:384], start=True, stop=True).then_inc(dec_mm, 1)

            pe.wait_ge(xs_ready, 12)
            pe.wait_ge(dec_ready, 1)
            pe.wait_ge(mods_b, 1)
            pe.wait_ge(xt_copied, 10)
            for u in range(2):
                pe.wait_ge(pair_free[u], uses(u, AT["out0"]))

            def step(s, d, first):
                pe.wait_ge(s_bst, s + 1)
                if not (isinstance(s, int) and s == 0) and not first:
                    pe.wait_ge(s_cbm, s)
                for g in range(2):
                    ins = mm(PS[:, 5, g * P:g * P + P], BST[:, g, :], CT[g](s), start=True, stop=True)
                ins.then_inc(s_cb, 1)

                def segs(b):
                    pe.wait_ge(s_at, s * 4 + (b + 1))
                    if not (first and b < 2):
                        pe.wait_ge(s_exp, s * 4 + (b - 1))
                    r = b % 2
                    mm(PS[:, 2 * r, :], C[:, KGTJ if d == 0 else KLTJ, :], AT2[:, r, :], start=True, stop=True)
                    mm(PS[:, 2 * r + 1, :], C[:, ONES, :], AT2[:, r, :], start=True, stop=True).then_inc(s_seg, 1)

                def heads(b):
                    if b == 0:
                        pe.wait_ge(s_xdt, s + 1)
                        if not first:
                            pe.wait_ge(s_yadd, s)
                            if not (isinstance(s, int) and s == 1):
                                pe.wait_ge(s_stf, s * 2 - 2)
                    pe.wait_ge(s_mc, s * 4 + (b + 1))
                    r = b % 2
                    for h in range(4 * b, 4 * b + 4):
                        hh = h - 4 * b
                        acc = PSF[64 * (h % 2):64 * (h % 2) + 64, 3072 + P * (h // 2):3072 + P * (h // 2) + P]
                        mm(acc, XDT[:, 64 * h:64 * h + 64], LEB[:, r, hh * P:hh * P + P], start=True, stop=False)
                        ins = mm(acc, HST[:, d, 64 * h:64 * h + 64], LEB[:, r, 512 + hh * P:512 + hh * P + P],
                                 start=False, stop=True)
                    ins.then_inc(s_y, 1)

                segs(0)
                segs(1)
                heads(0)
                segs(2)
                heads(1)
                segs(3)
                heads(2)
                heads(3)
                pe.wait_ge(s_xde, s + 1)
                for g in range(2):
                    if not (first and g == 0):
                        pe.wait_ge(s_stf, s * 2 + g)
                    mm(PS[:, 4, :], BST[:, 2 + g, :], XDE[:, 512 * g:512 * g + 512], start=True, stop=True) \
                        .then_inc(s_st, 1)

            CT = [None, None]
            tile_of = {}

            def run_steps(n, tf, tb, s0):
                def turn(i):
                    for d in range(2):
                        s = i * 2 + (s0 + d)
                        t = tf(i) if d == 0 else tb(i)
                        for g in range(2):
                            CT[g] = (lambda g, t: lambda s: XBC[:, 10 + g, bass.ds(t * P, P)])(g, t)
                        step(s, d, s0 == 0 and d == 0 and peel[0])
                if s0 == 0:
                    peel[0] = True
                    turn(0)
                    peel[0] = False
                    turn(1)
                else:
                    loops(pe, n, turn)
            peel = [False]
            run_steps(2, lambda i: 4 + i, lambda i: 5 - i, 0)
            run_steps(4, lambda i: i * 1, lambda i: i * -1 + 3, 4)

            pe.wait_ge(yz_ready, 8)
            pe.wait_ge(s_exp, 48)
            norm_sums()

            def res_block(name, rhs, segs=SEGS, by_tile=None):
                def body(gs, i, r):
                    one_block(gs, i, rhs, segs, by_tile if len(gs) == 1 and isinstance(r, int) and r == 0 else None)
                job_turns(pe, name, 8, body, peel=2 if by_tile else 0)

            res_block("out0", lambda k: ((YGH[:, 1, k, :], YGL[1][:, k, :]) if k < KT else
                                         (YGH[:, 0, k - KT, :], YGL[0][:, k - KT, :])),
                      by_tile=lambda k: pe.wait_ge(mix_lo, k + 1))

            parts = lambda k: (HNH[:, k, :], HNL[:, k, :])

            def feed_forward(layer, n, segs):
                norm_sum(n, segs)
                for half in range(2):
                    name = f"{layer}{half}"

                    def up(gs, i, r):
                        ready = half == 0 and isinstance(r, int) and r == 0
                        two_blocks(gs, i, parts, segs,
                                   by_tile=(lambda k: pe.wait_ge(hn_ready, KT * n + k + 1)) if ready else None)
                    job_turns(pe, "up" + name, FH, up, peel=1)
                    pe.wait_ge(hid_ready, FH * (2 * layer + half + 1))
                    res_block("down" + name, lambda k: (HIDH[:, k, :], HIDL[:, k, :]), segs)

            feed_forward(0, 1, SEGS)

            norm_sum(2)
            LS = (SEGS[0],)

            def rotated(b, n):
                read([AT["qkv"] + n // 2], 0, b, pe)
                if n:
                    pe.wait_ge(q_done, n)
                mm(PS[:, 6, :], C[:, ROT, :], T[:, b, 0:LAT], start=True, stop=True).then_inc(q_rot, 1)

            for n in range(5):
                two_blocks([AT["qkv"] + n], 0, parts, LS if n < 4 else SEGS,
                           between=(lambda: (rotated(0, 2 * n - 2), rotated(1, 2 * n - 1))) if n else None,
                           by_tile=(lambda k: pe.wait_ge(hn_ready, 2 * KT + k + 1)) if n == 0 else None)
            g = AT["qkv"] + 5
            half_ready([g], 0, 1)
            for t in range(6):
                acc = PSF[:, 2048 + 256 * t:2048 + 256 * t + 256] if t < 4 else PS[:, 7, 256 * (t - 4):256 * (t - 3)]
                for k in range(KT):
                    wh, wl = (w[:, k // 4, 2 * (k % 4):2 * (k % 4) + 2, :].rearrange("p a b -> p (a b)")
                              for w in (WH, WL))
                    h, l = HNH[:, k, t * P:t * P + P], HNL[:, k, t * P:t * P + P]
                    mm(acc, h, wh, start=k == 0, stop=False)
                    prev = mm(acc, h, wl, start=False, stop=False)
                    ins = mm(acc, l, wh, start=False, stop=k == KT - 1)
            prev.then_inc(blocks_done, 1)
            ins.then_inc(blocks_done, 1)
            for b in range(2):
                rotated(b, 8 + b)

            pe.wait_ge(k_done, 2)
            pe.wait_ge(v_done, 2)
            for u in range(2):
                pe.wait_ge(pair_free[u], uses(u, AT["out1"]))

            def attend(i, first):
                pe.wait_ge(at_q, i + 1)

                def scores(n):
                    b, h = divmod(n, 4)
                    lo, hi = max(b - 1, 0) * P, min(b + 2, 4) * P
                    w = hi - lo
                    c0 = 512 - w
                    r = n % 2
                    if not (first and n < 2):
                        pe.wait_ge(at_exp, i * 16 + (n - 1))
                    S = PSF[:, 1024 * r:1024 * r + 768]
                    p0 = 64 * (h % 2)
                    q = QG[p0:p0 + 64, h // 2, b * P:b * P + P]
                    mm(S[:, c0:512], q, KG[p0:p0 + 64, lo:hi], start=True, stop=False)
                    if b > 0:
                        mm(S[:, c0:c0 + P], C[:, IDENT, :], C[:, MLEFT, :], start=False, stop=b == 3)
                    if b < 3:
                        mm(S[:, 384:512], C[:, IDENT, :], C[:, MRIGHT, :], start=False, stop=True)
                    mm(S[:, 512:768], q, KG[p0:p0 + 64, LAT:TOK], start=True, stop=True).then_inc(at_s, 1)

                def flip(n):
                    b = n // 4
                    w = (min(b + 2, 4) - max(b - 1, 0)) + 2
                    pe.wait_ge(at_exp, i * 16 + (n + 1))
                    if not (first and n == 0):
                        pe.wait_ge(at_ptc, i * 16 + n)
                    for t in range(w):
                        ins = pe.transpose(PSF[:, 2048 + t * P:2048 + t * P + P], PR[:, n % 2, t * P:t * P + P],
                                           C[:, IDENT, :])
                    ins.then_inc(at_pt, 1)

                def values(n):
                    b, h = divmod(n, 4)
                    lo, w = max(b - 1, 0), (min(b + 2, 4) - max(b - 1, 0)) + 2
                    pe.wait_ge(at_ptc, i * 16 + (n + 1))
                    if h == 0 and not (first and b == 0):
                        pe.wait_ge(at_o, i * 4 + b)
                    for t in range(w):
                        kt = lo + t if t < w - 2 else 4 + t - (w - 2)
                        ins = mm(PS[:, 6, 64 * h:64 * h + 64], PTS[:, n % 2, t * P:t * P + P],
                                 VG[:, kt, :],
                                 start=t == 0, stop=t == w - 1)
                    ins.then_inc(at_pv, 1)

                def out_t(b):
                    pe.wait_ge(at_o, i * 4 + (b + 1))
                    if not (first and b == 0):
                        pe.wait_ge(at_otlo, i * 4 + b)
                    for j in range(2):
                        ins = pe.transpose(PS[:, 7, j * P:j * P + P],
                                           OTOK[:, b, 2 * j:2 * j + 2, :].rearrange("p a b -> p (a b)"),
                                           C[:, IDENT, :])
                    ins.then_inc(at_ot, 1)

                for n in range(16 + 3):
                    if n < 16:
                        scores(n)
                    if 1 <= n <= 16:
                        flip(n - 1)
                    if 2 <= n <= 17:
                        values(n - 2)
                    if n >= 6 and (n - 6) % 4 == 0:
                        out_t((n - 6) // 4)

            attend(0, True)
            with pe.Fori(1, KV) as i:
                attend(i, False)

            pe.wait_ge(at_otlo, 16)
            for n in range(4):
                two_blocks([AT["out1"] + n], 0, lambda k: (OTH[:, k, :], OTL[:, k, :]), LS)
            feed_forward(1, 3, LS)
            norm_sum(4, LS)

        @block.scalar
        def _(act):
            ch = Count(act, a_ch)
            run = act.activation
            Id = ACT.Identity

            def apart():
                act.wait_ge(v_in, 16)

            act.dma_start(V[:, 0:VEC_W - 2], A["vec"]).then_inc(v_in, 16)
            act.dma_start(ZT[0:HY_EMB, :], A["zfeat"]).then_inc(small_in, 16)
            act.dma_start(W1S[0:HY_EMB, :], A["hy_w1"]).then_inc(small_in, 16)
            act.dma_start(WS[0:64, 0, :], A["hy_w2"]).then_inc(small_in, 16)
            act.dma_start(WS[0:64, 1, :], A["hy_w3"]).then_inc(small_in, 16)
            act.dma_start(FBV[0:64, 0:6], A["hy_fb"]).then_inc(small_in, 16)
            act.dma_start(W4[0:64, :], A["hy_w4"]).then_inc(small_in, 16)
            act.dma_start(C[:, :, :], A["const"].rearrange("p (a b) -> p a b", a=9)).then_inc(c_in, 16)
            act.dma_start(WIN[:, :, :], A["window"][:, 0, :, :]).then_inc(win_in, 16)
            act.dma_start(BB[:, :], A["hy_bias"][0:1, 0:512].broadcast_to([P, 512])).then_inc(bias_in, 16)
            act.dma_start(C3[:, :, :], A["tab3"].rearrange("p (a b) -> p a b", a=2)).then_inc(t3_in, 16)
            act.dma_start(X[:, :, :], A["xT"]).then_inc(x_in, 16)
            act.dma_start(WD[:, :, :], A["w_dt"]).then_inc(wdt_in, 16)

            act.wait_ge(v_in, 16)
            act.wait_ge(eps_ready, 1)
            run(CS[:, :, :], V[:, _cols["cc"]:_cols["cc"] + 16].rearrange("p (k c) -> p k c", c=2),
                ACT.Silu).then_inc(silu_c, 1)

            for layer in range(3):
                act.wait_ge(mlp_mm, layer + 1)
                act.wait_ge(fb_ready, 1)
                run(HF[0:64, layer, :], PSF[0:64, 0:TOK], Id, scale=FBV[0:64, layer:layer + 1],
                    bias=FBV[0:64, 6 + layer:7 + layer]).then_inc(mlp_arg, 1)
                act.wait_ge(mlp_red, layer + 1)
                run(HF[0:64, layer, :], HF[0:64, layer, :], ACT.Sin).then_inc(mlp_sin, 1)
            for c in range(2):
                for t in range(6):
                    n = 6 * c + t
                    act.wait_ge(kg_sd, n + 1)
                    if n:
                        act.wait_ge(ssq_added, n)
                    run(SQ2[:, :, :], SD[:, :, t, :], ACT.Square).then_inc(kg_sq, 1)
                act.wait_ge(kg_ssq, c + 1)
                if c:
                    act.wait_ge(kd_ev, 12)
                run(INV[:, :, :], PS[:, 4:6, :], ACT.Sqrt, scale=0.5, bias=vec("eps", 0)).then_inc(kg_root, 1)

            def root(n, segs=SEGS):
                lo, hi = segs[0][0], segs[-1][1]
                run(T[:, 2, lo:hi], NP[:, lo:hi], ACT.Sqrt, scale=1.0 / D, bias=vec("eps", 0)).then_inc(n_sqrt, 1)

            def high_parts(muls, segs=SEGS):
                lo, hi = segs[0][0], segs[-1][1]
                for k in range(KT):
                    act.wait_ge(n_mul, muls + k + 1)
                    run(HNH[:, k, lo:hi], HN[:, k, lo:hi], ACT.Copy).then_inc(hn_hi, 1)

            act.wait_ge(n_summed, 1)
            root(0)

            def conv_first(gs, i, b, wname, bname, blk, tbuf, wait=None):
                act.wait_ge(blocks_done, along([2 * g + 1 + b for g in gs], i))
                if wait:
                    wait()
                u = PLAN[gs[0]][b][0]
                apart()
                run(T[:, tbuf, :], pair(u), Id, scale=blk(wname), bias=blk(bname)).then_inc(cv_act, 1)

            act.wait_ge(kd_mm, 24)
            act.dma_start(C4[:, :, :], A["tab4"].rearrange("p (a b) -> p a b", a=2)).then_inc(t4_in, 16)

            def uv(gs, i, first):
                for b in range(2):
                    def free():
                        if not first:
                            act.wait_ge(u_ready, i)
                    conv_first(gs, i, b, "hcw", "hcb", lambda nm: dvec(nm, (24 if nm == "hcw" else 0) + 8 + 8 * b, nm_i), b,
                               free)
                    if b == 0 and not first:
                        copy_u(i - 1)

            def copy_u(i):
                act.wait_ge(tp_mm, i + 1)
                apart()
                dst = UT[:, :, bass.ds(i, 1) if not isinstance(i, int) else slice(i, i + 1), :]
                run(dst, TP.rearrange("p (t a c) -> p t a c", t=6, a=1), ACT.Copy).then_inc(tp_copied, 1)

            firstj = AT["uv"]
            nm_i = 0
            uv([firstj], 0, True)
            with act.Fori(1, 8) as i:
                nm_i = i
                gs = [firstj + 3 * n for n in range(8)]
                uv(gs, i, False)
            copy_u(7)

            for n in range(4):
                g = AT["x0"] + 3 * n
                for b in range(2):
                    j = 2 * n + b

                    def free():
                        if j >= 2:
                            act.wait_ge(g_ready, j - 1)
                        else:
                            act.wait_ge(p_ready, 12)
                    conv_first([g], 0, b, "hcw", "hcb", lambda nm: dvec(nm, (24 if nm == "hcw" else 0), j), b, free)

            act.wait_ge(inv_mm, 8)

            def z_turn(i):
                gs = [AT["z"] + 3 * n for n in range(4)]
                for b in range(2):
                    act.wait_ge(blocks_done, along([2 * g + 1 + b for g in gs], i))
                    apart()
                    blk = i * 2 + b
                    dst = Z[:, blk, :] if isinstance(blk, int) else \
                        Z[:, bass.ds(blk, 1), :].rearrange("p a b -> p (a b)")
                    run(dst, pair(b), ACT.Silu).then_inc(pair_free[b], 1)
            loops(act, 4, z_turn)

            def copy_x(blk):
                act.wait_ge(xt_mm, blk + 1)
                if blk < 8:
                    dst = XT_[:, :, blk, :]
                else:
                    dst = BT[:, :, blk - 8, :]
                run(dst, TP.rearrange("p (t c) -> p t c", t=6), ACT.Copy).then_inc(xt_copied, 1)

            for n in range(6):
                g = AT["xbc"] + n
                for b in range(2):
                    blk = 2 * n + b

                    def free():
                        if blk < 2:
                            act.wait_ge(g_ready, 8)
                    if blk >= 2:
                        act.wait_ge(xs_ready, blk - 1)
                    conv_first([g], 0, b, "scw", "scb", lambda nm: dvec(nm, (12 if nm == "scw" else 0), blk), b, free)
                for b in range(2):
                    blk = 2 * n + b
                    read([g], 0, b, act)
                    run(XBC[:, blk, :], T[:, b, :], ACT.Silu).then_inc(xs_ready, 1)
                if n:
                    copy_x(2 * n - 2)
                    copy_x(2 * n - 1)
            act.wait_ge(dta_raw, 1)
            run(SPU[:, 1, :], SPU[:, 0, :], ACT.Exp, scale=-1.0).then_inc(sp_exp, 1)
            run(vec("alog", 0, 32), vec("alog", 0, 32), ACT.Exp).then_inc(sp_exp, 1)
            act.wait_ge(dec_mm, 1)
            run(DEC, PS[:, 6, 0:384], ACT.Exp).then_inc(dec_ready, 1)
            for k in range(KT):
                act.wait_ge(xt_mm, 10)
                run(XBC[:, k, :], XBC[:, k, :], ACT.Copy, scale=vec("dskip", k)).then_inc(dx_ready, 1)

            def step(s, t, first):
                if not first:
                    act.wait_ge(s_st, s * 2)
                src = XBC[:, 8:10, bass.ds(t * P, P)]
                apart()
                run(BST[:, 0:2, :], src, ACT.Copy)
                bt = BT[:, bass.ds(t, 1), :, :].rearrange("p a b c -> p (a b) c") if not isinstance(t, int) \
                    else BT[:, t, :, :]
                run(BST[:, 2:4, :], bt, ACT.Copy).then_inc(s_bst, 1)
                for b in range(4):
                    act.wait_ge(s_seg, s * 4 + (b + 1))
                    if not (first and b < 2):
                        act.wait_ge(s_y, s * 4 + (b - 1))
                    r = b % 2
                    run(LEB[:, r, :], PSF[:, 1024 * r:1024 * r + 1024], ACT.Exp).then_inc(s_exp, 1)

            def both(i, s0, tf, tb):
                step(i * 2 + s0, tf(i), s0 == 0 and isinstance(i, int) and i == 0)
                step(i * 2 + (s0 + 1), tb(i), False)
            for i in range(2):
                both(i, 0, lambda i: 4 + i, lambda i: 5 - i)
            loops(act, 4, lambda i: both(i, 4, lambda i: i * 1, lambda i: i * -1 + 3))

            for k in range(KT):
                act.wait_ge(yz_ready, k + 1)
                if k >= 2:
                    act.wait_ge(sq_mm, k - 1)
                run(T[:, k % 2, :], XBC[:, k, :], ACT.Square).then_inc(sq_ready, 1)
                if k < 4:
                    run(YGH[:, 1, k, :], G[:, k, :], ACT.Copy).then_inc(mix_hi, 1)
            act.wait_ge(sq_mm, KT)
            root(1)
            for k in range(4, KT):
                run(YGH[:, 1, k, :], G[:, k, :], ACT.Copy).then_inc(mix_hi, 1)
            for k in range(KT):
                act.wait_ge(n_mul, k + 1)
                run(YGH[:, 0, k, :], XBC[:, k, :], ACT.Copy).then_inc(mix_hi, 1)

            def feed_forward(layer, n, segs):
                act.wait_ge(n_summed, n + 1)
                root(n + 1, segs)
                high_parts(KT * n, segs)
                lo, hi = segs[0][0], segs[-1][1]
                for half in range(2):
                    name = f"up{layer}{half}"
                    done = FH * (2 * layer + half)

                    def up(gs, i, r):
                        act.wait_ge(blocks_done, along([2 * g + 1 for g in gs], i))
                        act.wait_ge(pair_free[1], along([PLAN[g][1][1] for g in gs], i))
                        run(T[:, 0, lo:hi], pair(0)[:, lo:hi], ACT.Silu).then_inc(pair_free[0], 1)
                        read(gs, i, 1, act)
                        apart()
                        run(at_row(HIDH, r)[:, lo:hi], T[:, 1, lo:hi], ACT.Copy).then_inc(hid_hi, 1)
                    job_turns(act, name, FH, up, peel=1)

            feed_forward(0, 1, SEGS)

            act.wait_ge(n_summed, 3)
            root(3)
            high_parts(2 * KT)
            for n in range(5):
                g = AT["qkv"] + n
                w = LAT if n < 4 else TOK
                for b in range(2):
                    m = 2 * n + b
                    act.wait_ge(blocks_done, 2 * g + 1 + b)
                    if m >= 2:
                        act.wait_ge(q_done, m - 1)
                    run(T[:, b, 0:w], pair(b)[:, 0:w], ACT.Copy).then_inc(pair_free[b], 1)
            g = AT["qkv"] + 5
            act.wait_ge(blocks_done, 2 * g + 2)
            run(VT[:, 0:4, :], PSF[:, 2048:3072].rearrange("p (t c) -> p t c", t=4), ACT.Copy).then_inc(v_done, 1)
            act.wait_ge(blocks_done, 2 * g + 2)
            run(VT[:, 4:6, :], PS[:, 7, :].rearrange("p (t c) -> p t c", t=2), ACT.Copy).then_inc(v_done, 1)

            def attend(i, first):
                act.wait_ge(q_done, 10)
                if not first:
                    act.wait_ge(at_pv, i * 16)
                act.wait_ge(k_done, 2)
                act.wait_ge(v_done, 2)
                apart()
                at = i * 4 + _cols["sink"]
                run(AST[:, 200:204], V[:, bass.ds(at, 4)], ACT.Copy).then_inc(at_group, 1)
                run(KG, KD[:, bass.ds(i, 1), :].rearrange("p a b -> p (a b)"), ACT.Copy)
                run(VG[:, :, :], VT[:, :, bass.ds(i * 64, 64)], ACT.Copy)
                src = QT[:, bass.ds(i * 2, 2), :] if not isinstance(i, int) else QT[:, 2 * i:2 * i + 2, :]
                run(QG[:, :, :], src, ACT.Copy).then_inc(at_q, 1)
                act.wait_ge(at_group, i + 1)

                def probs(n):
                    b, h = divmod(n, 4)
                    w = (min(b + 2, 4) - max(b - 1, 0) + 2) * P
                    c0 = 768 - w
                    act.wait_ge(at_neg, i * 16 + (n + 1))
                    if not (first and n < 2):
                        act.wait_ge(at_pt, i * 16 + (n - 1))
                    r = n % 2
                    run(AST[:, 64 + n:65 + n], AST[:, 200 + h:201 + h], ACT.Exp, bias=AST[:, 32 + n:33 + n]) \
                        .then_inc(at_sinkexp, 1)
                    run(PR[:, r, 0:w], PSF[:, 1024 * r + c0:1024 * r + 768], ACT.Exp, scale=ATTN_SCALE,
                        bias=AST[:, 32 + n:33 + n], accum_out=AST[:, 96 + n:97 + n]).then_inc(at_exp, 1)

                def out_copy(b):
                    act.wait_ge(at_ot, i * 4 + (b + 1))
                    apart()
                    run(OTH[:, bass.ds(i * 2, 2), b * P:b * P + P],
                        PS[:, 7, 0:256].rearrange("p (a c) -> p a c", a=2), ACT.Copy).then_inc(at_othi, 1)

                for n in range(16 + 3):
                    if n < 16:
                        probs(n)
                    if n >= 7 and (n - 7) % 4 == 0:
                        out_copy((n - 7) // 4)
                out_copy(3)

            attend(0, True)
            with act.Fori(1, KV) as i:
                attend(i, False)

            feed_forward(1, 3, (SEGS[0],))
            act.wait_ge(n_summed, 5)
            root(5, (SEGS[0],))

        @block.vector
        def _(dve):
            ch = Count(dve, v_ch)
            TS, TT, STT = dve.tensor_scalar, dve.tensor_tensor, dve.scalar_tensor_tensor

            def halves(ap, n):
                return ap.rearrange("p (a c) -> p a c", a=n)

            dve.wait_ge(small_in, 16 * 6)
            TT(FBV[0:64, 6:9], FBV[0:64, 0:3], FBV[0:64, 3:6], ALU.mult).then_inc(fb_ready, 1)

            MAGIC = 1.5 * 2.0 ** 23
            TWO_PI_HI, TWO_PI_LO = 6.28125, 2 * float(np.pi) - 6.28125
            PI_IN = 3.1415925
            for layer in range(3):
                dve.wait_ge(mlp_arg, layer + 1)
                h, q = HF[0:64, layer, :], T[0:64, 0, :]
                ch.link(TS(q, h, 1.0 / (2 * float(np.pi)), MAGIC, ALU.mult, ALU.add))
                ch.link(TS(q, q, MAGIC, None, ALU.subtract))
                ch.link(STT(h, q, -TWO_PI_HI, h, ALU.mult, ALU.add))
                ch.link(STT(h, q, -TWO_PI_LO, h, ALU.mult, ALU.add))
                TS(h, h, PI_IN, -PI_IN, ALU.min, ALU.max).then_inc(mlp_red, 1)

            def mods(layer, lo, hi):
                ab = V[:, _cols["ada_b"] + 48 * layer + lo:_cols["ada_b"] + 48 * layer + hi]
                return TT(MOD[:, layer, lo:hi, :], MODP[:, layer, lo:hi, :],
                          ab.unsqueeze(2).broadcast_to([P, hi - lo, 2]), ALU.add)

            def gains(which, layer, m, name):
                g = vec(name, 8 * layer, 8).unsqueeze(2).broadcast_to([P, KT, 2])
                return STT(GA[:, which, :, :], MOD[:, layer, 8 * m:8 * m + 8, :], 1.0, g, ALU.add, ALU.mult)

            def add_squares(x, lo, hi, tmp=2):
                ch.link(TT(T[:, tmp, lo:hi], x[:, lo:hi], x[:, lo:hi], ALU.mult))
                return TT(T[:, 3, lo:hi], T[:, 3, lo:hi], T[:, tmp, lo:hi], ALU.add)

            hf, hb = Tt[:, 0:512], Tt[:, 512:1024]
            for c in range(2):
                for t in range(6):
                    n = 6 * c + t
                    if t == 0:
                        dve.wait_ge(win2_in if c else win_in, 16)
                        if c:
                            dve.wait_ge(kd_mm, 12)
                    dve.wait_ge(kg_mm, n + 1)
                    TT(hf, PS[:, 2 * (n % 2), :], WIN[:, t, :], ALU.mult)
                    ins = TT(hb, PS[:, 2 * (n % 2) + 1, :], WIN[:, t, :], ALU.mult)
                    ins.then_inc(kg_free, 1)
                    dve.wait_ge(kg_free, n + 1)
                    if t in (0, 4):
                        ch.link(dve.memset(hb[0:1, :], 0.0))
                    TT(SD[:, 0, t, :], hf, hb, ALU.add)
                    TT(SD[:, 1, t, :], hf, hb, ALU.subtract).then_inc(kg_sd, 1)
                    dve.wait_ge(kg_sd, n + 1)
                if c == 0:
                    dve.wait_ge(x_in, 16)
                    ch.link(dve.memset(T[:, 3, :], 0.0))
                    for k in range(KT):
                        ins = add_squares(X[:, k, :], 0, TOK, 0)
                        if k < KT - 1:
                            ch.link(ins)
                    ins.then_inc(sums_ready, 1)
                dve.wait_ge(kg_root, c + 1)
                dve.wait_ge(bias2_in if c else bias_in, 16)
                ch.link(dve.reciprocal(INV[:, :, :], INV[:, :, :]))
                for f in range(6):
                    inv = INV[:, f >= 4, :]
                    for j in range(2):
                        n = 12 * c + 2 * f + j
                        dst = KS[:, j, f, 512 * c:512 * c + 512]
                        dve.wait_ge(kd_mm, n + 1)
                        ins = TT(dst, PS[:, n % 4, :], inv, ALU.mult)
                        if j == 0:
                            ch.link(ins)
                            ins = TT(dst, dst, BB[:, :], ALU.add)
                        ins.then_inc(kd_ev, 1)

            def norm(n, which=None, layer=0, shift=0, segs=SEGS, last=False):
                lo, hi = segs[0][0], segs[-1][1]
                dve.wait_ge(n_sqrt, n + 1)
                ch.link(dve.reciprocal(T[:, 3, lo:hi], T[:, 2, lo:hi]))
                for k in range(KT):
                    ch.link(TT(HN[:, k, lo:hi], X[:, k, lo:hi], T[:, 3, lo:hi], ALU.mult))
                    if last:
                        TS(HN[:, k, lo:hi], HN[:, k, lo:hi], vec("fin", k), None, ALU.mult).then_inc(fin_ready, 1)
                        continue
                    for j, (a, b) in enumerate(segs):
                        ins = TS(HN[:, k, a:b], HN[:, k, a:b], GA[:, which, k, j:j + 1],
                                 MOD[:, layer, 8 * shift + k, j:j + 1], ALU.mult, ALU.add)
                    ins.then_inc(hn_ready if n == 0 else n_mul, 1)

            dve.wait_ge(v_in, 16)
            dve.wait_ge(blocks_done, 2 * AT["uv"])
            mods(0, 0, 16)
            ins = mods(1, 0, 16)
            ins.then_inc(mods_a, 1)
            dve.wait_ge(mods_a, 1)
            ch.link(gains(0, 0, 1, "n1"))
            norm(0, 0, 0, 0)

            def split_high(gs, i, b):
                s = gs[0] % SLOTS
                n = width(gs[0], b)
                dve.wait_ge(w_loaded[s][b], along([16 * (g // SLOTS + 1) for g in gs], i))
                dve.tensor_copy(WH[:, b, 0:n, :], W[:, s, HALF * b:HALF * b + n, :]).then_inc(w_hi, 1)

            def next_high(gs, i, b):
                if gs[-1] + 1 < len(JOBS):
                    dve.wait_ge(blocks_done, along([2 * g + 1 + b for g in gs], i))
                    split_high([g + 1 for g in gs], i, b)

            def conv(gs, i, b, wname, n, blk, count):
                dve.wait_ge(cv_act, count)
                p, t = pair(PLAN[gs[0]][b][0]), T[:, b, :]
                w0, w2 = blk(wname, 0), blk(wname, 2 * n)
                for w, shift in ((w0, -1), (w2, 1)):
                    for j, (lo, hi) in enumerate(SEGS):
                        a, e = (lo + 1, hi) if shift < 0 else (lo, hi - 1)
                        ins = STT(t[:, a:e], p[:, a + shift:e + shift], w, t[:, a:e], ALU.mult, ALU.add)
                    if shift < 0:
                        ch.link(ins)
                ins.then_inc(pair_free[PLAN[gs[0]][b][0]], 1)

            def uv(i):
                gs = [AT["uv"] + 3 * n for n in range(8)]
                for b in range(2):
                    conv(gs, i, b, "hcw", 24, lambda nm, o: dvec(nm, o + 8 + 8 * b, i), i * 2 + (b + 1))
            with dve.Fori(0, 8) as i:
                ch.enter(i, 2)
                uv(i)
                ch.leave(8)

            for c in range(2):
                for f in range(6):
                    n = 6 * c + f
                    kc, ks = (KS[:, j, f, 512 * c:512 * c + 512] for j in range(2))
                    dve.wait_ge(u_mm, n + 1)
                    if n:
                        dve.wait_ge(p_ready, n)
                    uc, us = PS[:, 2 * (n % 2), :], PS[:, 2 * (n % 2) + 1, :]
                    for m, (x, y) in enumerate(((uc, kc), (us, ks), (uc, ks), (us, kc))):
                        ins = TT(Tt[:, 512 * m:512 * m + 512], x, y, ALU.mult)
                    ins.then_inc(u_prod, 1)

            for n in range(4):
                g = AT["x0"] + 3 * n
                for b in range(2):
                    conv([g], 0, b, "hcw", 24, lambda nm, o: dvec(nm, o, 2 * n + b), 16 + 2 * n + b + 1)
                read([g], 0, 1, dve)
                for b in range(2):
                    j = 2 * n + b
                    dve.wait_ge(inv_mm, j + 1)
                    STT(G[:, j, 0:LAT], TP[:, 0:LAT], 1.0 / LAT, T[:, b, 0:LAT], ALU.mult, ALU.mult)
                    STT(G[:, j, LAT:TOK], TP[:, LAT:TOK], 1.0 / CTX, T[:, b, LAT:TOK], ALU.mult, ALU.mult) \
                        .then_inc(g_ready, 1)

            dve.wait_ge(blocks_done, 2 * AT["xbc"])
            mods(0, 16, 48)
            mods(1, 16, 48).then_inc(mods_b, 1)
            dve.wait_ge(mods_b, 1)
            gains(1, 0, 4, "n2").then_inc(pair_free[2], 1)
            gains(2, 1, 1, "n1")
            gains(3, 1, 4, "n2").then_inc(gains_ready, 1)

            for n in range(6):
                for b in range(2):
                    conv([AT["xbc"] + n], 0, b, "scw", 12, lambda nm, o: dvec(nm, o, 2 * n + b), 24 + 2 * n + b + 1)

            dve.wait_ge(dt_mm, 1)
            raw, e, q = SPT, SPU[:, 1, :], SPU[:, 0, :]
            ch.link(TT(raw.rearrange("p (t h) -> p t h", t=6), PS[:, 6, 0:192].rearrange("p (t h) -> p t h", t=6),
                       vec("dtb", 0, 32).unsqueeze(1).broadcast_to([P, 6, 32]), ALU.add))
            STT(q, raw, -1.0, raw, ALU.mult, ALU.max).then_inc(dta_raw, 1)
            dve.wait_ge(sp_exp, 2)
            s2, r = DTS[:, 0:192], DTS[:, 192:384]
            ch.link(TS(r, e, 2.0, None, ALU.add))
            ch.link(dve.reciprocal(r, r))
            ch.link(TT(e, e, r, ALU.mult))
            ch.link(TT(s2, e, e, ALU.mult))
            ch.link(TS(q, s2, 1.0 / 17, None, ALU.mult))
            for m in range(7, 0, -1):
                ch.link(STT(q, q, 1.0 / (2 * m + 1), s2, ALU.add, ALU.mult))
            ch.link(STT(q, q, 1.0, e, ALU.add, ALU.mult))
            ch.link(TS(raw, raw, 0.0, None, ALU.max))
            ch.link(STT(DTS[:, 0:192], q, 2.0, raw, ALU.mult, ALU.add))
            STT(DTA[:, :, :], DTP[:, :, :], -1.0, vec("alog", 0, 32).unsqueeze(1).broadcast_to([P, 6, 32]),
                ALU.mult, ALU.mult).then_inc(dt_a, 1)

            dve.wait_ge(st_zero, 1)
            dve.wait_ge(dec_ready, 1)
            dve.wait_ge(xt_copied, 10)
            dve.wait_ge(dx_ready, KT)

            def at(ap3, t):
                return ap3[:, bass.ds(t, 1), :].rearrange("p a b -> p (a b)")

            DECF = DEC[:, 0:96].rearrange("p (t h) -> p t h", t=6)
            DECB = DEC[:, 96:192].rearrange("p (t h) -> p t h", t=6)
            TOT = DEC[:, 192:384].rearrange("p (t h) -> p t h", t=6)
            XTF = region(6144, 6, D)

            def step(s, d, t, first):
                if not first:
                    dve.wait_ge(s_y, s * 4)
                    dve.wait_ge(s_xde, s)
                TT(XDT.rearrange("p (h c) -> p h c", h=HEADS), at(XTF, t).rearrange("p (h c) -> p h c", h=HEADS),
                   at(DTP, t)[:, 16 * d:16 * d + 16].unsqueeze(2).broadcast_to([P, HEADS, HD]), ALU.mult) \
                    .then_inc(s_xdt, 1)
                dve.wait_ge(s_cb, s + 1)
                mask = C[:, LE if d == 0 else GE, :].unsqueeze(1)
                TT(CBM[:, 0, :, :], PS[:, 5, 0:256].rearrange("p (g c) -> p g c", g=2),
                   mask.broadcast_to([P, 2, P]), ALU.mult).then_inc(s_cbm, 1)
                dve.wait_ge(s_cbm, s + 1)
                for b in range(4):
                    g, r = b // 2, b % 2
                    dve.wait_ge(s_exp, s * 4 + (b + 1))
                    l3 = LEB[:, r, 0:512].rearrange("p (h c) -> p h c", h=4)
                    e3 = LEB[:, r, 512:1024].rearrange("p (h c) -> p h c", h=4)
                    TT(l3, l3, CBM[:, 0, g, :].unsqueeze(1).broadcast_to([P, 4, P]), ALU.mult)
                    ct = XBC[:, 10 + g, bass.ds(t * P, P)].unsqueeze(1)
                    TT(e3, e3, ct.broadcast_to([P, 4, P]), ALU.mult).then_inc(s_mc, 1)
                dve.wait_ge(s_y, s * 4 + 4)
                xs = XBC[:, 0:KT, bass.ds(t * P, P)]
                TT(xs, xs, PSF[:, 3072:4096].rearrange("p (k c) -> p k c", k=KT), ALU.add).then_inc(s_yadd, 1)
                h3 = HST[:, d, :].rearrange("p (h c) -> p h c", h=HEADS)
                ch.link(TT(h3, h3, at(TOT, t)[:, 16 * d:16 * d + 16].unsqueeze(2).broadcast_to([P, HEADS, HD]),
                           ALU.mult))
                for g in range(2):
                    dve.wait_ge(s_st, s * 2 + (g + 1))
                    hg = HST[:, d, 512 * g:512 * g + 512]
                    TT(hg, hg, PS[:, 4, :], ALU.add).then_inc(s_stf, 1)

            def both(i, s0, tf, tb):
                first = s0 == 0 and isinstance(i, int) and i == 0
                step(i * 2 + s0, 0, tf(i), first)
                step(i * 2 + (s0 + 1), 1, tb(i), False)
            for i in range(2):
                both(i, 0, lambda i: 4 + i, lambda i: 5 - i)
            with dve.Fori(0, 4) as i:
                ch.enter(i, 2)
                both(i, 4, lambda i: i * 1, lambda i: i * -1 + 3)
                ch.leave(4)
            dve.wait_ge(s_yadd, 12)

            dve.wait_ge(s_bst, 12)
            for b in range(2):
                split_high([G0], 0, b)
            for k in range(KT):
                TT(XBC[:, k, :], XBC[:, k, :], Z[:, k, :], ALU.mult).then_inc(yz_ready, 1)
            dve.wait_ge(n_sqrt, 2)
            ch.link(dve.reciprocal(T[:, 3, :], T[:, 2, :]))
            for k in range(KT):
                STT(XBC[:, k, :], XBC[:, k, :], vec("sng", k), T[:, 3, :], ALU.mult, ALU.mult).then_inc(n_mul, 1)

            def column(layer, m, k, j):
                c = k * 1 + 8 * m if not isinstance(k, int) else k + 8 * m
                return MOD[:, layer, bass.ds(c, 1), j:j + 1].rearrange("p a b -> p (a b)")

            def res(name, layer, m, segs, squares=True):
                two = name == "out1"
                lo, hi = segs[0][0], segs[-1][1]
                if squares:
                    ch.link(dve.memset(T[:, 3, lo:hi], 0.0))

                def body(gs, i, r):
                    if not two:
                        next_high(gs, i, 0)
                    for b in range(2 if two else 1):
                        if two or b == 0:
                            next_high(gs, i, b if two else 1)
                        k = r if not two else 2 * r + b
                        if two:
                            dve.wait_ge(blocks_done, along([2 * g + 1 + b for g in gs], i))
                        u = PLAN[gs[0]][b][0]
                        x = at_row(X, k)
                        if gs[-1] + 1 == len(JOBS):
                            dve.wait_ge(blocks_done, 2 * len(JOBS))
                        for j, (a, e) in enumerate(segs):
                            ins = STT(x[:, a:e], pair(u)[:, a:e], column(layer, m, k, j), x[:, a:e],
                                      ALU.mult, ALU.add)
                        ins.then_inc(pair_free[u], 1)
                        if squares:
                            read(gs, i, b, dve)
                            ch.link(add_squares(x, lo, hi))
                if two:
                    for r in range(4):
                        body([AT[name] + r], 0, r)
                else:
                    peel = 2 if name == "out0" else 0
                    job_turns(dve, name, 8, body, ch, 2 * SLOTS if squares else 0, peel)
                if squares:
                    TS(T[:, 3, lo:hi], T[:, 3, lo:hi], 1.0, None, ALU.mult).then_inc(sums_ready, 1)

            def feed_forward(layer, n, segs):
                norm(n + 1, 2 * layer + 1, layer, 3, segs)
                lo, hi = segs[0][0], segs[-1][1]
                for half in range(2):
                    name = f"{layer}{half}"
                    done = FH * (2 * layer + half)

                    def up(gs, i, r):
                        next_high(gs, i, 0)
                        next_high(gs, i, 1)
                        read(gs, i, 0, dve)
                        TT(T[:, 1, lo:hi], T[:, 0, lo:hi], pair(1)[:, lo:hi], ALU.mult).then_inc(pair_free[1], 1)
                        dve.wait_ge(hid_hi, r + (done + 1))
                        TT(at_row(HIDL, r)[:, lo:hi], T[:, 1, lo:hi], at_row(HIDH, r)[:, lo:hi].bitcast(f32),
                           ALU.subtract).then_inc(hid_ready, 1)
                        dve.wait_ge(hid_ready, r + (done + 1))
                    job_turns(dve, "up" + name, FH, up, peel=1)
                    res("down" + name, layer, 5, segs, squares=half == 1)

            dve.wait_ge(n_mul, KT)
            res("out0", 0, 2, SEGS)
            feed_forward(0, 1, SEGS)
            norm(3, 2, 1, 0)

            dve.wait_ge(rope_in, 16)
            for m in range(10):
                b = m % 2
                if b == 0:
                    for h in range(2):
                        next_high([AT["qkv"] + m // 2], 0, h)
                    if m == 8:
                        for h in range(2):
                            next_high([AT["qkv"] + 5], 0, h)
                dve.wait_ge(q_rot, m + 1)
                TT(T[:, 2, 0:LAT], PS[:, 6, :], RC[:, 1, :], ALU.mult)
                ch.link(TT(T[:, 3, 0:LAT], T[:, b, 0:LAT], RC[:, 0, :], ALU.mult))
                dst = QT[:, m, :] if m < 8 else T[:, b, 0:LAT]
                TT(dst, T[:, 3, 0:LAT], T[:, 2, 0:LAT], ALU.add).then_inc(q_done, 1)
                dve.wait_ge(q_done, m + 1)
                if m >= 8:
                    for g in range(2):
                        for half in range(2):
                            ins = dve.tensor_copy(KD[64 * half:64 * half + 64, 2 * b + g, :],
                                                  T[64 * g:64 * g + 64, b, :])
                    ins.then_inc(k_done, 1)

            def attend(i, first):
                def row_max(n):
                    b, h = divmod(n, 4)
                    w = (min(b + 2, 4) - max(b - 1, 0) + 2) * P
                    r = n % 2
                    dve.wait_ge(at_s, i * 16 + (n + 1))
                    ch.link(dve.tensor_reduce(AST[:, n:n + 1], PSF[:, 1024 * r + 768 - w:1024 * r + 768], AX.X, ALU.max))
                    at = i * 4 + (_cols["sink"] + h)
                    sink = V[:, bass.ds(at, 1)]
                    ch.link(TS(AST[:, 16 + n:17 + n], AST[:, n:n + 1], ATTN_SCALE, sink, ALU.mult, ALU.max))
                    TS(AST[:, 32 + n:33 + n], AST[:, 16 + n:17 + n], -1.0, None, ALU.mult).then_inc(at_neg, 1)

                def keys(n):
                    b = n // 4
                    w = (min(b + 2, 4) - max(b - 1, 0) + 2) * P
                    dve.wait_ge(at_pt, i * 16 + (n + 1))
                    if not (first and n < 2):
                        dve.wait_ge(at_pv, i * 16 + (n - 1))
                    dve.tensor_copy(PTS[:, n % 2, 0:w], PSF[:, 2048:2048 + w]).then_inc(at_ptc, 1)

                def out_low(b):
                    dve.wait_ge(at_othi, i * 4 + (b + 1))
                    rows = slice(b * P, b * P + P)
                    TT(OTL[:, bass.ds(i * 2, 2), rows], PS[:, 7, 0:256].rearrange("p (a c) -> p a c", a=2),
                       OTH[:, bass.ds(i * 2, 2), rows].bitcast(f32), ALU.subtract).then_inc(at_otlo, 1)

                def outputs(b):
                    dve.wait_ge(at_pv, i * 16 + (4 * b + 4))
                    c = 4 * b
                    ch.link(TT(AST[:, 112 + c:116 + c], AST[:, 64 + c:68 + c], AST[:, 96 + c:100 + c], ALU.add))
                    ch.link(dve.reciprocal(AST[:, 128 + c:132 + c], AST[:, 112 + c:116 + c]))
                    if not first:
                        dve.wait_ge(at_ot, i * 4 + (b - 3))
                    TT(OTOK[:, b, :, :], PS[:, 6, 0:256].rearrange("p (h c) -> p h c", h=4),
                       AST[:, 128 + c:132 + c].unsqueeze(2).broadcast_to([P, 4, HD]), ALU.mult).then_inc(at_o, 1)

                for n in range(16 + 3):
                    if n < 16:
                        row_max(n)
                    if 1 <= n <= 16:
                        keys(n - 1)
                    if n >= 8 and n % 4 == 0:
                        out_low(n // 4 - 2)
                    if n >= 5 and (n - 5) % 4 == 0:
                        outputs((n - 5) // 4)
                out_low(3)

            attend(0, True)
            with dve.Fori(1, KV) as i:
                ch.enter(i, 2 * 16 + 2 * 4)
                ch.n -= ch.per
                ch.base = ch.n
                attend(i, False)
                ch.leave(KV)

            res("out1", 1, 2, (SEGS[0],))
            feed_forward(1, 3, (SEGS[0],))
            norm(5, segs=(SEGS[0],), last=True)

        @block.gpsimd
        def _(pool):
            TT = pool.tensor_tensor
            pool.memset(vec("eps", 0), EPS).then_inc(eps_ready, 1)
            def add_ssq(c):
                for t in range(6):
                    n = 6 * c + t
                    pool.wait_ge(kg_sq, n + 1)
                    acc = SSA[:, t >= 4, :]
                    if t in (0, 4):
                        if c and t == 0:
                            pool.wait_ge(kg_ssq, 1)
                        TT(acc, SQ2[:, 0, :], SQ2[:, 1, :], ALU.add).then_inc(ssq_added, 1)
                        continue
                    pool.wait_ge(ssq_added, n)
                    TT(acc, acc, SQ2[:, 0, :], ALU.add).then_inc(g_ch, 1)
                    pool.wait_ge(g_ch, n - (c * 2 + (1 if t < 4 else 2)) + 1 - 0)
                    TT(acc, acc, SQ2[:, 1, :], ALU.add).then_inc(ssq_added, 1)
            add_ssq(0)
            pool.wait_ge(kg_free, 6)
            pool.dma_start(WIN[:, :, :], A["window"][:, 1, :, :]).then_inc(win2_in, 16)
            pool.wait_ge(kd_ev, 12)
            pool.dma_start(BB[:, :], A["hy_bias"][0:1, 512:1024].broadcast_to([P, 512])).then_inc(bias2_in, 16)
            add_ssq(1)

            def product(i, first):
                read([AT["uv"] + 3 * n for n in range(8)], i, 0, pool)
                read([AT["uv"] + 3 * n for n in range(8)], i, 1, pool)
                if not first:
                    pool.wait_ge(tp_mm, i)
                TT(T[:, 2, :], T[:, 0, :], T[:, 1, :], ALU.mult).then_inc(u_ready, 1)
            product(0, True)
            with pool.Fori(1, 8) as i:
                product(i, False)

            for c in range(2):
                for f in range(6):
                    n = 6 * c + f
                    kc, ks = (KS[:, j, f, 512 * c:512 * c + 512] for j in range(2))
                    pool.wait_ge(u_prod, n + 1)
                    TT(kc, Tt[:, 0:512], Tt[:, 512:1024], ALU.subtract)
                    TT(ks, Tt[:, 1024:1536], Tt[:, 1536:2048], ALU.add).then_inc(p_ready, 1)

            pool.wait_ge(xs_ready, XBC_BLKS)
            pool.memset(HST[:, :, :], 0.0).then_inc(st_zero, 1)
            pool.wait_ge(dec_ready, 1)

            def step(s, d, t, first):
                tri = C[:, LE if d == 0 else GE, :].unsqueeze(1).broadcast_to([P, 4, P])

                def ramp(b):
                    if not (first and b < 2):
                        pool.wait_ge(s_seg, s * 4 + (b - 1))
                    a = DTA[:, bass.ds(t, 1), 16 * d + 4 * b:16 * d + 4 * b + 4].rearrange("p a b -> p (a b)")
                    TT(AT2[:, b % 2, :].rearrange("p (h c) -> p h c", h=4), tri,
                       a.unsqueeze(2).broadcast_to([P, 4, P]), ALU.mult).then_inc(s_at, 1)
                ramp(0)
                ramp(1)
                pool.wait_ge(s_xdt, s + 1)
                if not first:
                    pool.wait_ge(s_st, s * 2)
                dec = DEC[:, 96 * d:96 * d + 96].rearrange("p (t h) -> p t h", t=6)
                TT(XDE.rearrange("p (h c) -> p h c", h=HEADS), XDT.rearrange("p (h c) -> p h c", h=HEADS),
                   dec[:, bass.ds(t, 1), :].rearrange("p a b -> p (a b)").unsqueeze(2)
                   .broadcast_to([P, HEADS, HD]), ALU.mult).then_inc(s_xde, 1)
                ramp(2)
                ramp(3)

            def both(i, s0, tf, tb):
                step(i * 2 + s0, 0, tf(i), s0 == 0 and isinstance(i, int) and i == 0)
                step(i * 2 + (s0 + 1), 1, tb(i), False)
            for i in range(2):
                both(i, 0, lambda i: 4 + i, lambda i: 5 - i)
            loops(pool, 4, lambda i: both(i, 4, lambda i: i * 1, lambda i: i * -1 + 3))

            def low(gs, i):
                s = gs[0] % SLOTS
                for b in range(2):
                    n = width(gs[0], b)
                    pool.wait_ge(w_hi, along([2 * (g - G0) + b + 1 for g in gs], i))
                    TT(WL[:, b, 0:n, :], W[:, s, HALF * b:HALF * b + n, :], WH[:, b, 0:n, :].bitcast(f32),
                       ALU.subtract).then_inc(w_lo, 1)

            def next_low(name, count, peel=0):
                job_turns(pool, name, count, lambda gs, i, r: low([g + 1 for g in gs], i), peel=peel)

            low([G0], 0)
            for n in range(2 * KT):
                j, k = (1, n) if n < KT else (0, n - KT)
                src = (G if j else XBC)[:, k, :]
                pool.wait_ge(mix_hi, n + 1)
                TT(YGL[j][:, k, :], src, YGH[:, j, k, :].bitcast(f32), ALU.subtract).then_inc(mix_lo, 1)
            next_low("out0", 8, 2)

            def low_parts(n, segs=SEGS):
                lo, hi = segs[0][0], segs[-1][1]
                for k in range(KT):
                    pool.wait_ge(hn_hi, KT * (n - 1) + k + 1)
                    TT(HNL[:, k, lo:hi], HN[:, k, lo:hi], HNH[:, k, lo:hi].bitcast(f32), ALU.subtract) \
                        .then_inc(hn_ready, 1)

            def feed_forward(layer, n, segs):
                low_parts(n, segs)
                for half in range(2):
                    next_low(f"up{layer}{half}", FH, 1)
                    if layer == 1 and half == 1:
                        for r in range(7):
                            low([AT["down11"] + r + 1], 0)
                    else:
                        next_low(f"down{layer}{half}", 8)
            feed_forward(0, 1, SEGS)
            low_parts(2)
            pool.wait_ge(blocks_done, 2 * AT["qkv"])
            pool.dma_start(RC[:, :, :], A["rope"].rearrange("p (a b) -> p a b", a=2)).then_inc(rope_in, 16)
            for r in range(6):
                low([AT["qkv"] + r + 1], 0)
            for r in range(4):
                low([AT["out1"] + r + 1], 0)
            feed_forward(1, 3, (SEGS[0],))


def _constants():
    k = np.arange(P)
    K, J = k[:, None], k[None, :]
    c = np.zeros((P, 9, P), np.float32)
    c[:, IDENT] = K == J
    c[:, ONES] = 1
    c[:, KGTJ] = K > J
    c[:, KLTJ] = K < J
    c[:, LE] = K <= J
    c[:, GE] = K >= J
    for m in range(P):
        c[m + 16 if m % 32 < 16 else m - 16, ROT, m] = -1 if m % 32 < 16 else 1
    c[:, MLEFT] = np.where(J >= K, 0, NEG)
    c[:, MRIGHT] = np.where(J <= K, 0, NEG)

    def table(shift):
        parts = []
        for fn in (np.cos, np.sin):
            cols = []
            for L in (LAT, CTX):
                t, f = np.arange(L)[:, None] + shift, np.arange(L)[None, :] + 0.5
                m = fn(np.pi * t * f / L)
                cols.append(m.reshape(L // P, P, L).transpose(1, 0, 2).reshape(P, -1))
            parts.append(np.concatenate(cols, 1))
        return np.concatenate(parts, 1).astype(np.float32)

    f4 = np.float32
    feats, wins = [], []
    for L in (LAT, CTX):
        t = np.arange(L, dtype=f4)
        unit = t / f4(L - 1)
        ang = f4(2.0 * np.pi) * t / f4(L)
        f = np.linspace(1e-4, HY_BANDS - 1, HY_BANDS, dtype=f4)
        feats.append(np.concatenate([unit[:, None], np.cos(ang[:, None] * f), -np.sin(ang[:, None] * f)], 1).T)
        deltas = np.linspace(np.log(1e-2) / 1.5, np.log(1e-2) / 0.3, D, dtype=f4)
        w = np.exp(-unit[:, None] * np.abs(deltas)[None, :])
        wins.append(w.reshape(L // P, P, 2, 512).transpose(1, 2, 0, 3))
    rows = LAT // GRID_W
    row = np.repeat(np.arange(rows), GRID_W).astype(f4)
    col = np.tile(np.arange(GRID_W), rows).astype(f4)
    inv = f4(ROPE_BASE) ** (-np.arange(16, dtype=f4) / f4(16))
    ang = np.zeros((P, LAT), f4)
    for m in range(P):
        ang[m] = (row if m % 64 < 32 else col) * inv[m % 16]
    rope = np.concatenate([np.cos(ang), np.sin(ang)], 1)
    return {"const": c.reshape(P, 9 * P), "tab3": table(0.0), "tab4": table(0.5),
            "zfeat": np.concatenate(feats, 1).astype(f4), "window": np.concatenate(wins, 2).astype(f4),
            "rope": rope.astype(f4)}


def _layout(a):
    def tiles(w, cols):
        return w[:, cols:cols + P].reshape(-1, P, P).transpose(1, 0, 2)

    hy, z0, x0 = a["hy_in_w"][0], 0, D
    h0 = D + XBC_BLKS * P + 2 * HEADS
    wall = np.zeros((len(JOBS), P, JT, P), np.float32)
    for g, (kind, layer, n) in enumerate(JOBS):
        if kind == "ada":
            two = [(a["ada_w"][layer], (2 * n + b) * P) for b in range(2)]
        elif kind == "uv":
            two = [(hy, h0 + (8 + 8 * b + n) * P) for b in range(2)]
        elif kind == "x0":
            two = [(hy, h0 + (2 * n + b) * P) for b in range(2)]
        elif kind == "z":
            two = [(hy, (2 * n + b) * P) for b in range(2)]
        elif kind == "xbc":
            two = [(hy, D + (2 * n + b) * P) for b in range(2)]
        elif kind == "out0":
            wall[g] = np.roll(tiles(a["hy_out_w"][0], n * P), KT, 1)
            continue
        elif kind == "up":
            two = [(a["ffn_w_in"][layer], b * FFN + n * P) for b in range(2)]
        elif kind == "down":
            half, blk = n
            t = tiles(a["ffn_w_out"][layer][half * FH * P:(half + 1) * FH * P], blk * P)
            wall[g, :, 0:DOWN[0]] = t[:, 0:DOWN[0]]
            wall[g, :, HALF:HALF + DOWN[1]] = t[:, DOWN[0]:]
            continue
        elif kind in ("q", "k"):
            two = [(a["attn_qkv_w"][0], (8 if kind == "k" else 0) * P + (2 * n + b) * P) for b in range(2)]
        elif kind == "v":
            w = a["attn_qkv_w"][0][:, D + 256:D + 512].reshape(KT, P, 2, P)
            wall[g] = w.transpose(1, 0, 2, 3).reshape(P, JT, P)
            continue
        elif kind == "out1":
            two = [(a["attn_out_w"][0], (2 * n + b) * P) for b in range(2)]
        for b, (w, c) in enumerate(two):
            wall[g, :, KT * b:KT * b + KT] = tiles(w, c)

    def feat(v):
        return v.reshape(-1, P).T

    vec = np.zeros((P, VEC_W - 2), np.float32)

    def put(name, v):
        vec[:, _cols[name]:_cols[name] + v.shape[1]] = v

    put("ada_b", feat(a["ada_b"].reshape(-1)))
    put("n1", feat(a["norm1_g"].reshape(-1)))
    put("n2", feat(a["norm2_g"].reshape(-1)))
    put("fin", feat(a["final_g"]))
    put("sng", feat(a["ssd_norm_g"][0]))
    put("scw", feat(a["ssd_conv_w"][0].reshape(-1)))
    put("scb", feat(a["ssd_conv_b"][0]))
    put("hcw", feat(a["hy_conv_w"][0].reshape(-1)))
    put("hcb", feat(a["hy_conv_b"][0]))
    put("dskip", feat(np.repeat(a["ssd_d"][0], HD)))
    put("cc", np.stack([feat(a["c"][0]), feat(a["c_ctx"])], 2).reshape(P, 16))
    put("sink", np.repeat(a["attn_sinks"][0:1], P, 0))
    put("dtb", np.repeat(a["ssd_dt_bias"].reshape(1, 32), P, 0))
    put("alog", np.repeat(a["ssd_a_log"].reshape(1, 32), P, 0))
    xt = np.concatenate([a["x"][0].T, a["ctx"][0].T], 1)
    wdt = hy[:, D + XBC_BLKS * P:h0]
    return {
        "wall": wall.reshape(len(JOBS), P, JT * P), "vec": vec,
        "xT": xt.reshape(KT, P, TOK).transpose(1, 0, 2), "w_dt": wdt.reshape(KT, P, 32).transpose(1, 0, 2),
        "hy_w1": a["hy_w1"][0], "hy_w2": a["hy_w2"][0], "hy_w3": a["hy_w3"][0], "hy_w4": a["hy_w4"][0],
        "hy_fb": np.concatenate([a["hy_freq"][0].T, np.stack([a["hy_b1"][0], a["hy_b2"][0], a["hy_b3"][0]], 1)], 1),
        "hy_bias": a["hy_bias"],
    }


def kernel(**inputs):
    import concourse.bacc as bacc
    from concourse.bass_utils import run_bass_kernel_spmd as run

    arrays = {k: np.ascontiguousarray(v) for k, v in
              {**_layout({k: np.asarray(v) for k, v in inputs.items()}), **_constants()}.items()}
    nc = bacc.Bacc("TRN2", target_bir_lowering=False, num_devices=1)
    args = {k: nc.dram_tensor(f"in_{k}", v.shape, mybir.dt.from_np(v.dtype), kind="ExternalInput").ap()
            for k, v in arrays.items()}
    out = nc.dram_tensor("out_T", (P, KT, LAT), mybir.dt.float32, kind="ExternalOutput").ap()
    build_kernel(nc, args, out)
    r = run(nc, [{f"in_{k}": v for k, v in arrays.items()}], core_ids=[0])
    y = r.results[0]["out_T"]
    return np.ascontiguousarray(y.transpose(1, 0, 2).reshape(D, LAT).T).reshape(1, LAT, D)
```

```python
import concourse.bass as bass
import numpy as np
from concourse import mybir
from contextlib import ExitStack

D = 1024
LAT, CTX = 512, 256
TOK = LAT + CTX
P = 128
KT = D // P
HEADS, HD, GROUPS, STATE = 16, 64, 2, 128
XBC_BLKS = (D + 2 * GROUPS * STATE) // P
HY_FFN, HY_BANDS = 64, 16
HY_EMB = 1 + 2 * HY_BANDS
FFN = 2816
FB = FFN // P
FH = FB // 2
KV, QH = 4, 16
EPS = 1e-6
GRID_W = 64
ROPE_BASE = 10000.0
ATTN_SCALE = 64 ** -0.5
NEG = -1.0e30
STEPS = 2 * TOK // P
SLOTS = 3
JT = 16
HALF = JT // 2
DOWN = (6, 5)
SEGS = ((0, LAT), (LAT, TOK))

_cols = {}
_at = 0
for _n, _w in (("ada_b", 2 * 48), ("n1", 16), ("n2", 16), ("fin", 8), ("sng", 8), ("scw", 3 * 12), ("scb", 12),
               ("hcw", 3 * 24), ("hcb", 24), ("dskip", 8), ("cc", 16), ("sink", 16), ("dtb", 32), ("alog", 32),
               ("eps", 2)):
    _cols[_n] = _at
    _at += _w
VEC_W = _at
IDENT, ONES, KGTJ, KLTJ, LE, GE, ROT, MLEFT, MRIGHT = range(9)


def weight_jobs():
    jobs, at = [], {}

    def stage(name, items):
        at[name] = len(jobs)
        jobs.extend(items)

    ada0 = [("ada", 0, n) for n in range(24)]
    ada1 = [("ada", 1, n) for n in range(24)]
    stage("ada_a", ada0[:8] + ada1[:8])
    stage("uv", [j for n in range(8) for j in (("uv", 0, n), ada0[8 + 2 * n], ada0[9 + 2 * n])])
    stage("x0", [j for n in range(4) for j in (("x0", 0, n), ada1[8 + 2 * n], ada1[9 + 2 * n])])
    stage("z", [j for n in range(4) for j in (("z", 0, n), ada1[16 + 2 * n], ada1[17 + 2 * n])])
    stage("xbc", [("xbc", 0, n) for n in range(6)])
    stage("out0", [("out0", 0, n) for n in range(8)])
    for layer in range(2):
        if layer:
            stage("qkv", [("q", 0, n) for n in range(4)] + [("k", 0, 0), ("v", 0, 0)])
            stage("out1", [("out1", 0, n) for n in range(4)])
        for half in range(2):
            stage(f"up{layer}{half}", [("up", layer, half * FH + n) for n in range(FH)])
            stage(f"down{layer}{half}", [("down", layer, (half, n)) for n in range(8)])
    return jobs, at


JOBS, AT = weight_jobs()


def job_blocks(kind):
    return {"ada": 0, "out0": 1, "down": 1, "v": 0}.get(kind, 2)


def plan():
    used, turn, out, last = [0, 0, 1], 0, [], None
    for kind, layer, _ in JOBS:
        n = job_blocks(kind)
        if n == 1 and kind != last:
            turn = 0
        pairs = []
        for u in range(n):
            pair = u if n == 2 else turn
            pairs.append((pair, used[pair]))
            used[pair] += 1
        if n == 1:
            turn = (turn + 1) % 3
        last = kind
        out.append(pairs)
    return out


PLAN = plan()
PAIR = {g: n for n, g in enumerate([g for g, job in enumerate(JOBS) if job[0] == "ada"][::2])}
G0 = AT["out0"]
SPLIT = [g for g, job in enumerate(JOBS) if job[0] != "ada"]
NTH = {g: n for n, g in enumerate(SPLIT)}


def width(g, b):
    return DOWN[b] if JOBS[g][0] == "down" else HALF


def uses(u, g):
    return sum(p == u for blocks in PLAN[:g] for p, _ in blocks) + (u == 2)


def along(values, i):
    if isinstance(i, int):
        return values[i]
    step = values[1] - values[0]
    assert all(b - a == step for a, b in zip(values, values[1:])), values
    return i * step + values[0]


class Count:

    def __init__(self, eng, sem):
        self.eng, self.sem, self.n, self.i, self.per = eng, sem, 0, None, 0

    def now(self):
        return self.n if self.i is None else self.i * self.per + self.n

    def inc(self, ins):
        ins.then_inc(self.sem, 1)
        self.n += 1
        return self.now()

    def link(self, ins):
        self.eng.wait_ge(self.sem, self.inc(ins))

    def enter(self, i, per):
        self.i, self.per, self.base = i, per, self.n
        if not isinstance(i, int):
            self.first = True

    def leave(self, times):
        assert self.n - self.base == self.per, (self.n - self.base, self.per)
        self.n = self.base + self.per * times
        self.i = None


def build_kernel(nc, A, out):
    f32 = mybir.dt.float32
    f32r = mybir.dt.float32r
    ALU = mybir.AluOpType
    ACT = mybir.ActivationFunctionType
    AX = mybir.AxisListType
    ctx = ExitStack()
    with ctx:
        def sb(name, shape):
            return ctx.enter_context(nc.sbuf_tensor(name, shape, f32))

        def sem(name):
            return ctx.enter_context(nc.semaphore(name))

        x_at = -(-nc.sbuf_base // 32) * 32
        Xt = sb("residual", [P, KT * TOK])
        X = Xt[:, :].rearrange("p (k t) -> p k t", k=KT)
        hn_at = -(-nc.sbuf_base // 32) * 32
        HNt = sb("normed", [P, KT * TOK])
        w_at = -(-nc.sbuf_base // 32) * 32
        W = sb("weights", [P, SLOTS, JT, P])
        C = sb("consts", [P, 9, P])
        V = sb("vectors", [P, VEC_W])
        MOD = sb("mods", [P, 2, 48, 2])
        ROOTS = sb("filter_roots", [P, 32])
        MARK = sb("mark", [P, 2])
        GA = sb("gains", [P, 4, KT, 2])
        CS = sb("silu_c", [P, KT, 2])
        Tt = sb("temps", [P, 4 * TOK])
        r_at = -(-nc.sbuf_base // 32) * 32
        R = sb("phase", [P, 29184])

        wd_at = -(-nc.sbuf_base // 32) * 32
        WD = sb("w_dt", [P, KT, 32])
        spu_at = -(-nc.sbuf_base // 32) * 32
        SPU = sb("softplus_tmp", [P, 2, 192])

        def part(name, base, at, *dims):
            return nc.alloc_sbuf_tensor_at(name, [P, *dims], f32r, offset=base + 4 * at)

        WH = part("weights_hi", r_at, 26112, 2, HALF, P)
        WL = part("weights_lo", w_at, 0, SLOTS, JT, P)
        WDH, WDL = part("w_dt_hi", spu_at, 0, KT, 32), part("w_dt_lo", wd_at, 0, KT, 32)
        HNH0 = part("normed_first_hi", x_at, 0, KT, TOK)
        YGH = part("mixed_hi", r_at, 0, 2, KT, TOK)
        YGL = [part("ssd_lo", r_at, 18432, KT, TOK), part("hyena_lo", r_at, 12288, KT, TOK)]
        HNH = part("normed_hi", r_at, 16896, KT, TOK)
        HNL = part("normed_lo", hn_at, 0, KT, TOK)
        HIDH = part("hidden_hi", r_at, 0, FH, TOK)
        HIDL = part("hidden_lo", r_at, FH * TOK, FH, TOK)
        spare1 = ((G0 + 1) % SLOTS) * JT * P
        AT2H = part("ramps_hi", hn_at, 0, 2, 512)
        AT2L = part("ramps_lo", w_at, spare1, 2, 512)
        SUMS = part("sums_of_rows", w_at, spare1 + 1024, 3, P)
        DTAH = part("dt_a_hi", w_at, spare1 + 1408, 6, 32)
        DTAL = part("dt_a_lo", w_at, spare1 + 1600, 6, 32)
        OTH = part("attended_hi", hn_at, 0, KT, LAT)
        OTL = part("attended_lo", r_at, 16896, KT, LAT)
        HN = HNt[:, :].rearrange("p (k t) -> p k t", k=KT)
        T = Tt[:, :].rearrange("p (k t) -> p k t", k=4)

        def region(at, *dims):
            n = 1
            for d in dims:
                n *= d
            names = "abcd"[:len(dims)]
            ap = R[:, at:at + n]
            if len(dims) == 1:
                return ap
            return ap.rearrange(f"p ({' '.join(names)}) -> p {' '.join(names)}",
                                **{names[i]: dims[i] for i in range(1, len(dims))})

        def inside(base, at, *dims):
            n = 1
            for d in dims:
                n *= d
            names = "abcd"[:len(dims)]
            ap = base[:, at:at + n]
            if len(dims) == 1:
                return ap
            return ap.rearrange(f"p ({' '.join(names)}) -> p {' '.join(names)}",
                                **{names[i]: dims[i] for i in range(1, len(dims))})

        KS = region(0, 2, 6, D)
        UT = region(12288, 6, KT, P)
        G = region(12288, KT, TOK)
        C4 = region(18432, 2, 2560)
        C3 = region(12288, 2, 2560)
        SD = region(17408, 2, 6, 512)
        W4 = region(23552, 2 * D)
        HF = inside(Xt, 0, 3, TOK)
        WIN = inside(HNt, 0, 6, 512)
        INV = inside(HNt, 3072, 2, 512)
        BB = inside(HNt, 4096, 512)
        SQ2 = inside(HNt, 4608, 2, 512)
        SSA = Tt[:, 1024:2048].rearrange("p (a c) -> p a c", a=2)
        KR = [ROOTS[:, 0:16], ROOTS[:, 16:32]]
        W1S = inside(Xt, 2304, 64)
        WS = inside(Xt, 2368, 2, 64)
        FBV = inside(Xt, 2496, 9)
        ZT = inside(Xt, 2560, TOK)
        Z = region(0, KT, TOK)
        XBC = region(18432, XBC_BLKS, TOK)
        XT_ = region(6144, 6, KT, P)
        BT = region(27648, 6, 2, P)
        QT = region(0, KT, LAT)
        KD = region(4096, KV, TOK)
        VT = region(7168, 6, 256)
        RC = region(8704, 2, LAT)
        QG = region(9728, 2, LAT)
        PR = region(10752, 2, 640)
        PTS = region(12032, 2, 640)
        OTOK = region(13312, 4, 4, HD)
        AST = region(14336, 256)
        KG = region(14592, TOK)
        VG = region(15360, 6, HD)
        LEB = inside(HNt, 1024, 2, 1024)
        spare = W[:, (G0 + 2) % SLOTS, :, :].rearrange("p a b -> p (a b)")
        XDT = [inside(HNt, 3072, 1024), spare[:, 0:1024]]
        XDE = inside(HNt, 4096, 1024)
        BST = [inside(HNt, 5120, 4, P), spare[:, 1024:1536].rearrange("p (a b) -> p a b", a=4)]
        CBM = inside(HNt, 5632, 2, 2, P)
        HST = inside(Tt, 0, 2, 1024)
        DTS = inside(Tt, 2048, 1024)
        DTP = DTS[:, 0:192].rearrange("p (t h) -> p t h", t=6)
        DTA = DTS[:, 192:384].rearrange("p (t h) -> p t h", t=6)
        DEC = DTS[:, 384:768]
        SPT = DTS[:, 768:960]

        ROWS = [inside(HNt, 5632, 512), region(23552, 512)]

        PS = ctx.enter_context(nc.psum_tensor("psum", [P, 8, 512], f32))
        PSF = PS[:, :, :].rearrange("p b c -> p (b c)")

        def pair(u):
            return PSF[:, 1024 * u:1024 * u + TOK]

        TP = PSF[:, 2048:2048 + TOK]
        NP = PSF[:, 3072:3072 + TOK]
        NS = PS[:, 7, 256:268]
        RS = [T[:, 2, 0:12], T[:, 2, 16:28]]
        MODP = PS[:, 7, 0:192].rearrange("p (l b c) -> p l b c", l=2, b=48)

        def vec(name, n, w=1):
            return V[:, _cols[name] + n:_cols[name] + n + w]

        def dvec(name, base, i, step=1):
            at = i * step + (_cols[name] + base)
            return V[:, bass.ds(at, 1)] if not isinstance(at, int) else V[:, at:at + 1]

        w_loaded = [[sem(f"w_loaded{s}{b}") for b in range(2)] for s in range(SLOTS)]
        w_hi, w_lo = sem("weights_hi_ready"), sem("weights_lo_ready")
        blocks_done = sem("blocks_done")
        pair_free = [sem(f"pair_free{u}") for u in range(3)]
        a_ch, v_ch, g_ch = sem("act_order"), sem("dve_order"), sem("pool_order")
        x_in, c_in, v_in, small_in, t3_in, t4_in, win_in, rope_in = (
            sem(n) for n in ("x_in", "c_in", "v_in", "small_in", "t3_in", "t4_in", "win_in", "rope_in"))
        silu_c, mods_a, mods_b = sem("silu_c_ready"), sem("mods_a_ready"), sem("mods_b_ready")
        gains_ready = sem("gains_ready")
        names = """filter_bias filter_mm filter_arg filter_reduced filter_sin
            kg_mm kg_free kg_sd kg_sq kg_ssq kg_root kd_mm kd_ev bias_in
            sq_ready sq_mm norm_sqrt norm_mul hn_ready conv_first
            u_ready tp_mm tp_copied u_mm u_prod p_ready inv_mm g_ready
            x_stored xt_mm xt_copied dt_mm dt_abs dt_exp dt_ready dec_mm dec_ready dx_ready states_zero
            step_at step_seg step_exp step_mc step_y step_cb step_cbm step_xdt step_xde step_st step_added
            step_state step_b yz_ready
            q_rot q_done k_done v_done
            at_q at_s at_neg at_sink at_exp at_pt at_ptc at_pv at_o at_ot
            fin_ready out_done eps_ready win2_in bias2_in at_group
            n_rec n_spread kg_rec kg_spread inv_ready sq_order dta_split wdt_in wdt_hi wdt_lo row_copied flipped sums_ready norm_summed hn_hi hid_hi hid_ready ssq_added mixed_hi mixed_lo at_othi at_otlo"""
        (fb_ready, mlp_mm, mlp_arg, mlp_red, mlp_sin,
         kg_mm, kg_free, kg_sd, kg_sq, kg_ssq, kg_root, kd_mm, kd_ev, bias_in,
         sq_ready, sq_mm, n_sqrt, n_mul, hn_ready, cv_act,
         u_ready, tp_mm, tp_copied, u_mm, u_prod, p_ready, inv_mm, g_ready,
         xs_ready, xt_mm, xt_copied, dt_mm, dta_raw, sp_exp, dt_a, dec_mm, dec_ready, dx_ready, st_zero,
         s_at, s_seg, s_exp, s_mc, s_y, s_cb, s_cbm, s_xdt, s_xde, s_st, s_yadd,
         s_stf, s_bst, yz_ready,
         q_rot, q_done, k_done, v_done,
         at_q, at_s, at_neg, at_sinkexp, at_exp, at_pt, at_ptc, at_pv, at_o, at_ot,
         fin_ready, out_done, eps_ready, win2_in, bias2_in, at_group,
         n_rec, n_spread, kg_rec, kg_spread, inv_ready, sq_order, dta_split, wdt_in, wdt_hi, wdt_lo, row_copied, flipped, sums_ready, n_summed, hn_hi, hid_hi, hid_ready, ssq_added, mix_hi, mix_lo, at_othi, at_otlo) = (sem(n) for n in names.split())

        def at_row(ap, k):
            return ap[:, bass.ds(k, 1), :].rearrange("p a b -> p (a b)")

        def read(gs, i, b, eng):
            eng.wait_ge(pair_free[PLAN[gs[0]][b][0]], along([PLAN[g][b][1] + 1 for g in gs], i))

        def loops(eng, n, body, chain=None, per=0):
            if n == 0:
                return
            if n == 1:
                body(0)
                return
            if chain is None:
                with eng.Fori(0, n) as i:
                    body(i)
                return
            with eng.Fori(0, n) as i:
                chain.enter(i, per)
                body(i)
                chain.leave(n)

        def job_turns(eng, name, count, body, chain=None, per=0, peel=0):
            first = AT[name]
            for r in range(peel):
                body([first + r], 0, r)
            full = (count - peel) // SLOTS

            def turn(i):
                for r in range(SLOTS):
                    body([first + peel + n * SLOTS + r for n in range(full)], i, i * SLOTS + (peel + r))
            loops(eng, full, turn, chain, per)
            for r in range(peel + full * SLOTS, count):
                body([first + r], 0, r)

        def chunk_turns(eng, body, chain=None, per=0):
            body(0, (None, 4, 5, 5), False)
            body(2, (5, 5, 4, 0), False)
            loops(eng, 3, lambda i: body(i * 2 + 4, (i * -1 + 4, i * 1, i * -1 + 3, i + 1), False), chain, per)
            body(10, (1, 3, 0, None), True)

        block = ctx.enter_context(nc.Block())

        @block.sync
        def _(sp):
            def load(gs, i, old):
                s = gs[0] % SLOTS
                for b in range(2):
                    if old == "steps":
                        sp.wait_ge(s_y, 4 * STEPS)
                    if old in ("product", "steps"):
                        sp.wait_ge(blocks_done, along([2 * (g - SLOTS) + 1 + b for g in gs], i))
                    n = width(gs[0], b)
                    sp.dma_start(W[:, s, HALF * b:HALF * b + n, :],
                                 A["wall"][along(gs, i), :, HALF * b * P:(HALF * b + n) * P].rearrange(
                                     "p (t n) -> p t n", n=P)).then_inc(w_loaded[s][b], 16)

            def run(first, end, old):
                full = (end - first) // SLOTS

                def turn(i):
                    for r in range(SLOTS):
                        load([first + n * SLOTS + r for n in range(full)], i, old)
                loops(sp, full, turn)
                for g in range(first + full * SLOTS, end):
                    load([g], 0, old)

            cuts = {0, SLOTS, G0 + 1, G0 + SLOTS, len(JOBS)}
            for g in range(1, len(JOBS)):
                if (JOBS[g][0] == "down") != (JOBS[g - 1][0] == "down"):
                    cuts.add(g)
            cuts = sorted(cuts)
            for lo, hi in zip(cuts, cuts[1:]):
                run(lo, hi, "" if lo < SLOTS else "steps" if lo == G0 + 1 else "product")
            for half in range(2):
                ks = slice(half * KT // 2, (half + 1) * KT // 2)
                sp.wait_ge(fin_ready, (half + 1) * KT // 2)
                sp.dma_start(out[:, ks, :], HN[:, ks, 0:LAT]).then_inc(out_done, 16)
            sp.wait_ge(out_done, 32)

        @block.tensor
        def _(pe):
            mm = pe.matmul

            def half_ready(gs, i, b):
                if JOBS[gs[0]][0] == "ada":
                    pe.wait_ge(w_loaded[gs[0] % SLOTS][b], along([16 * (g // SLOTS + 1) for g in gs], i))
                else:
                    pe.wait_ge(w_lo, along([2 * NTH[g] + b + 1 for g in gs], i))

            def pair_ready(gs, i, b):
                u = PLAN[gs[0]][b][0]
                if PLAN[gs[0]][b][1] or len(gs) > 1:
                    pe.wait_ge(pair_free[u], along([PLAN[g][b][1] for g in gs], i))
                return u

            def tiles(gs, acc, b, n, rhs, segs, first, last, by_tile=None):
                s = gs[0] % SLOTS
                for k in range(n):
                    if by_tile:
                        by_tile[0](k)
                    st, en = first and k == 0, last and k == n - 1
                    high, low = rhs(k)
                    for lo, hi in segs:
                        mm(acc[:, lo:hi], WH[:, b, k, :], high[:, lo:hi], start=st, stop=False)
                        mm(acc[:, lo:hi], WL[:, s, HALF * b + k, :], high[:, lo:hi], start=False, stop=False)
                    if by_tile:
                        by_tile[1](k)
                    for lo, hi in segs:
                        ins = mm(acc[:, lo:hi], WH[:, b, k, :], low[:, lo:hi], start=False, stop=en)
                ins.then_inc(blocks_done, 1)

            def two_blocks(gs, i, rhs, segs=SEGS, between=None, by_tile=None):
                for b in range(2):
                    half_ready(gs, i, b)
                    u = pair_ready(gs, i, b)
                    tiles(gs, pair(u), b, KT, rhs, segs, True, True, by_tile if b == 0 else None)
                    if b == 0 and between:
                        between()

            def one_block(gs, i, rhs, segs=SEGS, by_tile=None):
                u = pair_ready(gs, i, 0)
                n0 = width(gs[0], 0)
                for b in range(2):
                    half_ready(gs, i, b)
                    tiles(gs, pair(u), b, width(gs[0], b), lambda k: rhs(n0 * b + k), segs, b == 0, b == 1,
                          by_tile and [lambda k, wait=wait: wait(n0 * b + k) for wait in by_tile])

            def ada(gs, i):
                for part in range(2):
                    jobs = [g + part for g in gs]
                    s = jobs[0] % SLOTS
                    for b in range(2):
                        half_ready(jobs, i, b)
                        if part == b == 0 and not (len(gs) == 1 and PAIR[gs[0]] == 0):
                            pe.wait_ge(row_copied, along([PAIR[g] for g in gs], i))
                        for k in range(2):
                            ins = mm(PS[0:2, 6, :], CS[:, 4 * part + 2 * b + k, :],
                                     W[:, s, 8 * b + 4 * k:8 * b + 4 * k + 4, :].rearrange("p a c -> p (a c)"),
                                     start=part == b == k == 0, stop=part == b == k == 1)
                        ins.then_inc(blocks_done, 1)

            def flips(gs, i):
                if PAIR[gs[0]] == 0:
                    pe.wait_ge(c_in, 16)
                pe.wait_ge(row_copied, along([PAIR[g] + 1 for g in gs], i))
                row = ROWS[PAIR[gs[-1]] >= 8]
                for q in range(4):
                    col = along([4 * JOBS[g][2] + 2 * q + 96 * JOBS[g][1] for g in gs], i)
                    dst = PS[:, 7, bass.ds(col, 2)] if not isinstance(col, int) else PS[:, 7, col:col + 2]
                    ins = mm(dst, row[0:2, q * P:q * P + P], C[0:2, IDENT, 0:2], start=True, stop=True)
                ins.then_inc(flipped, 1)

            def waits(high, high_base, low, low_base):
                return [lambda k: pe.wait_ge(high, high_base + k + 1), lambda k: pe.wait_ge(low, low_base + k + 1)]

            hn = lambda k: (HNH0[:, k, :], HNL[:, k, :])

            def norm_sums(segs=SEGS):
                for k in range(KT):
                    pe.wait_ge(sq_ready, k + 1)
                    for a, b in segs:
                        ins = mm(NP[:, a:b], C[:, ONES, :], T[:, k % 2, a:b], start=k == 0, stop=k == KT - 1)
                    ins.then_inc(sq_mm, 1)

            def norm_sum(n, segs=SEGS):
                tiles = segs[-1][1] // P
                pe.wait_ge(sums_ready, n + 1)
                for t in range(tiles):
                    ins = mm(NS[:, 2 * t:2 * t + 2], T[:, 3, t * P:t * P + P], C[:, ONES, 0:2],
                             start=True, stop=True)
                ins.then_inc(n_summed, 1)
                pe.wait_ge(n_rec, n + 1)
                for t in range(tiles):
                    ins = mm(NP[:, t * P:t * P + P], RS[1][:, 2 * t:2 * t + 1].broadcast_to([P, P]),
                             C[:, IDENT, :], start=True, stop=True)
                ins.then_inc(n_spread, 1)

            pe.wait_ge(silu_c, 1)
            early = list(range(AT["ada_a"], AT["uv"], 2))
            rows = []

            def fill():
                if rows:
                    flips([rows.pop()], 0)
                if early:
                    rows.append(early.pop(0))
                    ada([rows[0]], 0)

            fill()
            pe.wait_ge(small_in, 16 * 6)
            for layer in range(3):
                if layer:
                    pe.wait_ge(mlp_sin, layer)
                for a, b in SEGS:
                    if layer == 0:
                        ins = mm(PSF[0:64, a:b], W1S[0:HY_EMB, :], ZT[0:HY_EMB, a:b], start=True, stop=True)
                    else:
                        ins = mm(PSF[0:64, a:b], WS[0:64, layer - 1, :], HF[0:64, layer - 1, a:b],
                                 start=True, stop=True)
                ins.then_inc(mlp_mm, 1)
                fill()
            pe.wait_ge(mlp_sin, 3)
            pe.wait_ge(t3_in, 16)
            for c in range(2):
                for t in range(6):
                    n = 6 * c + t
                    if n >= 2:
                        pe.wait_ge(kg_free, n - 1)
                    if c and t < 2:
                        pe.wait_ge(kd_ev, 12 * c)
                    for j in range(2):
                        ins = mm(PS[:, 2 * (n % 2) + j, :], HF[0:64, 2, t * P:t * P + P],
                                 W4[0:64, D * j + 512 * c:D * j + 512 * c + 512], start=True, stop=True)
                    ins.then_inc(kg_mm, 1)
                    if t % 2:
                        fill()
                def filter_roots():
                    pe.wait_ge(ssq_added, 6 * (c + 1))
                    if c:
                        pe.wait_ge(inv_ready, 1)
                    for q in range(8):
                        ins = mm(PS[:, 4, 2 * q:2 * q + 2], SSA[:, q // 4, P * (q % 4):P * (q % 4) + P],
                                 C[:, ONES, 0:2], start=True, stop=True)
                    ins.then_inc(kg_ssq, 1)
                    pe.wait_ge(kg_rec, c + 1)
                    for q in range(8):
                        ins = mm(PSF[:, 2048 + P * q:2048 + P * q + P],
                                 KR[1][:, 2 * q:2 * q + 1].broadcast_to([P, P]), C[:, IDENT, :], start=True, stop=True)
                    ins.then_inc(kg_spread, 1)

                for f in range(6):
                    lat = f < 4
                    ts = range(4) if lat else range(4, 6)
                    L = LAT if lat else CTX
                    if f == 2:
                        filter_roots()
                    for j in range(2):
                        n = 12 * c + 2 * f + j
                        pe.wait_ge(kg_free, 6 * (c + 1))
                        if n >= 4:
                            pe.wait_ge(kd_ev, n - 3)
                        tab = C3[:, j, :]
                        for t in ts:
                            o = (t * 512 + f * P) if lat else (2048 + (t - 4) * 256 + (f - 4) * P)
                            ins = mm(PS[:, n % 4, :], tab[:, o:o + P], SD[:, j, t, :],
                                     start=t == ts[0], stop=t == ts[-1])
                        ins.then_inc(kd_mm, 1)
                        if j and f % 2:
                            fill()

            while early or rows:
                fill()
            pe.wait_ge(mods_a, 1)
            norm_sum(0)
            pe.wait_ge(kd_ev, 24)
            def transposes_u(i, first=False):
                pe.wait_ge(u_ready, i + 1)
                if not first:
                    pe.wait_ge(tp_copied, i)
                for t in range(6):
                    ins = pe.transpose(TP[:, t * P:t * P + P], T[:, 2, t * P:t * P + P], C[:, IDENT, :])
                ins.then_inc(tp_mm, 1)

            def uv(i, gs, between=None, by_tile=None):
                def work():
                    between()
                    flips([g - 2 for g in gs], i)
                two_blocks(gs, i, hn, between=between and work, by_tile=by_tile)
                ada([g + 1 for g in gs], i)

            uv(0, [AT["uv"]], by_tile=waits(hn_hi, 0, hn_ready, 0))
            uv(0, [AT["uv"] + 3], lambda: transposes_u(0, True))
            with pe.Fori(0, 6) as i:
                uv(i, [AT["uv"] + 3 * (n + 2) for n in range(6)], lambda: transposes_u(i + 1))
            transposes_u(7)

            pe.wait_ge(tp_copied, 8)
            pe.wait_ge(t4_in, 16)
            for c in range(2):
                for f in range(6):
                    lat = f < 4
                    ts = range(4) if lat else range(4, 6)
                    n = 6 * c + f
                    if n < 2:
                        pe.wait_ge(pair_free[n % 2], uses(n % 2, AT["x0"]))
                    else:
                        pe.wait_ge(u_prod, n - 1)
                    for j in range(2):
                        tab = C4[:, j, :]
                        for t in ts:
                            o = (t * 512 + f * P) if lat else (2048 + (t - 4) * 256 + (f - 4) * P)
                            ins = mm(PS[:, 2 * (n % 2) + j, :], tab[:, o:o + P],
                                     UT[:, t, 4 * c:4 * c + 4, :].rearrange("p a b -> p (a b)"),
                                     start=t == ts[0], stop=t == ts[-1])
                    ins.then_inc(u_mm, 1)

            pe.wait_ge(u_prod, 12)
            for n in range(4):
                g = AT["x0"] + 3 * n
                two_blocks([g], 0, hn, between=lambda: flips([g - 2], 0))
                ada([g + 1], 0)
                pe.wait_ge(p_ready, 12)
                for b in range(2):
                    j = 2 * n + b
                    if j:
                        pe.wait_ge(g_ready, j)
                    for f in range(4):
                        for q in range(2):
                            mm(TP[:, 0:LAT], KS[:, q, f, j * P:j * P + P], C4[:, q, f * 512:f * 512 + 512],
                               start=f == 0 and q == 0, stop=f == 3 and q == 1)
                    for f in range(2):
                        for q in range(2):
                            o = 2048 + f * 256
                            ins = mm(TP[:, LAT:TOK], KS[:, q, 4 + f, j * P:j * P + P], C4[:, q, o:o + 256],
                                     start=f == 0 and q == 0, stop=f == 1 and q == 1)
                    ins.then_inc(inv_mm, 1)

            def z_turn(i):
                gs = [AT["z"] + 3 * n for n in range(4)]
                two_blocks(gs, i, hn, between=lambda: flips([g - 2 for g in gs], i))
                ada([g + 1 for g in gs], i)
            loops(pe, 4, z_turn)

            pe.wait_ge(g_ready, 8)
            pe.wait_ge(wdt_lo, 1)
            for t in range(6):
                acc = PS[:, 4, 32 * t:32 * t + 32]
                for k in range(KT):
                    h, l = HNH0[:, k, t * P:t * P + P], HNL[:, k, t * P:t * P + P]
                    mm(acc, h, WDH[:, k, :], start=k == 0, stop=False)
                    mm(acc, h, WDL[:, k, :], start=False, stop=False)
                    ins = mm(acc, l, WDH[:, k, :], start=False, stop=k == KT - 1)
            ins.then_inc(dt_mm, 1)


            def transposes_x(blk):
                if blk == 0:
                    pe.wait_ge(dta_raw, 1)
                else:
                    pe.wait_ge(xt_copied, blk)
                pe.wait_ge(xs_ready, blk + 1)
                for t in range(6):
                    ins = pe.transpose(TP[:, t * P:t * P + P], XBC[:, blk, t * P:t * P + P], C[:, IDENT, :])
                ins.then_inc(xt_mm, 1)

            for n in range(6):
                two_blocks([AT["xbc"] + n], 0, hn, between=(lambda: flips([AT["xbc"] - 2], 0)) if n == 0 else
                           None if n == 5 else (lambda: transposes_x(2 * n - 2)))
                if n == 5:
                    transposes_x(8)
                if n:
                    transposes_x(2 * n - 1)
                if n == 2:
                    pe.wait_ge(dt_a, 1)
                    for d in range(2):
                        mm(PS[:, 6, 192 * 0 + 96 * d:96 * d + 96].rearrange("p (t h) -> p t h", t=6),
                           C[:, KGTJ if d == 0 else KLTJ, :], DTA[:, :, 16 * d:16 * d + 16], start=True, stop=True)
                    mm(PS[:, 6, 192:384], C[:, ONES, :], DTS[:, 192:384], start=True, stop=True).then_inc(dec_mm, 1)
            pe.wait_ge(xs_ready, 12)
            pe.wait_ge(dec_ready, 1)
            pe.wait_ge(mods_b, 1)
            pe.wait_ge(xt_copied, 10)
            for u in range(2):
                pe.wait_ge(pair_free[u], uses(u, AT["out0"]))

            def at_least(sem_, value):
                if not (isinstance(value, int) and value <= 0):
                    pe.wait_ge(sem_, value)

            def products_cb(s, d, t):
                pe.wait_ge(s_bst, s + 1)
                at_least(s_cbm, s)
                for g in range(2):
                    ins = mm(PS[:, 5, g * P:g * P + P], BST[d][:, g, :], XBC[:, 10 + g, bass.ds(t * P, P)],
                             start=True, stop=True)
                ins.then_inc(s_cb, 1)

            def segs(s, d, b):
                pe.wait_ge(s_at, s * 4 + (b + 1))
                at_least(s_exp, s * 4 + (b - 1))
                r = b % 2
                mm(PS[:, 2 * r, :], SUMS[:, 1 + d, :], AT2H[:, r, :], start=True, stop=False)
                mm(PS[:, 2 * r, :], SUMS[:, 1 + d, :], AT2L[:, r, :], start=False, stop=True)
                mm(PS[:, 2 * r + 1, :], SUMS[:, 0, :], AT2H[:, r, :], start=True, stop=False)
                mm(PS[:, 2 * r + 1, :], SUMS[:, 0, :], AT2L[:, r, :], start=False, stop=True).then_inc(s_seg, 1)

            def heads(s, d, b):
                if b == 0:
                    pe.wait_ge(s_xdt, s + 1)
                    at_least(s_stf, s * 2 - 2)
                if b in (0, 2):
                    at_least(s_yadd, s * 2 - 1 if b == 0 else s * 2)
                pe.wait_ge(s_mc, s * 4 + (b + 1))
                r = b % 2
                for h in range(4 * b, 4 * b + 4):
                    hh = h - 4 * b
                    acc = PSF[64 * (h % 2):64 * (h % 2) + 64, 3072 + P * (h // 2):3072 + P * (h // 2) + P]
                    mm(acc, XDT[d][:, 64 * h:64 * h + 64], LEB[:, r, hh * P:hh * P + P], start=True, stop=False)
                    ins = mm(acc, HST[:, d, 64 * h:64 * h + 64], LEB[:, r, 512 + hh * P:512 + hh * P + P],
                             start=False, stop=True)
                ins.then_inc(s_y, 1)

            def states(s, d, g):
                if g == 0:
                    pe.wait_ge(s_xde, s + 1)
                at_least(s_stf, s * 2 + g)
                mm(PS[:, 4, :], BST[d][:, 2 + g, :], XDE[:, 512 * g:512 * g + 512], start=True, stop=True) \
                    .then_inc(s_st, 1)

            def turn(s0, chunks, last):
                for d in range(2):
                    s = s0 + d
                    more = not (last and d == 1)
                    before = (not (isinstance(s, int) and s == 0)) and not (last and d == 1)
                    heads(s, d, 0)
                    segs(s, d, 2)
                    heads(s, d, 1)
                    if before:
                        states(s - 1, 1 - d, 1)
                    segs(s, d, 3)
                    if more:
                        products_cb(s + 1, 1 - d, chunks[d + 2])
                    heads(s, d, 2)
                    if more:
                        segs(s + 1, 1 - d, 0)
                    heads(s, d, 3)
                    if more:
                        segs(s + 1, 1 - d, 1)
                    if not last:
                        states(s, d, 0)

            products_cb(0, 0, 4)
            segs(0, 0, 0)
            segs(0, 0, 1)
            chunk_turns(pe, turn)

            mixed = lambda k: ((YGH[:, 1, k, :], YGL[1][:, k, :]) if k < KT else
                               (YGH[:, 0, k - KT, :], YGL[0][:, k - KT, :]))
            mixed_waits = waits(mix_hi, 0, mix_lo, 0)
            half_ready([G0], 0, 0)
            first = pair(pair_ready([G0], 0, 0))
            tiles([G0], first, 0, KT, mixed, SEGS, True, False, mixed_waits)
            norm_sums()
            half_ready([G0], 0, 1)
            tiles([G0], first, 1, KT, lambda k: mixed(KT + k), SEGS, False, True,
                  [lambda k, wait=wait: wait(KT + k) for wait in mixed_waits])

            def res_block(name, rhs, segs=SEGS, by_tile=None, skip=0):
                def body(gs, i, r):
                    if isinstance(r, int) and r < skip:
                        return
                    one_block(gs, i, rhs, segs, by_tile if len(gs) == 1 and isinstance(r, int) and r == 0 else None)
                job_turns(pe, name, 8, body, peel=2 if by_tile else 0)

            res_block("out0", mixed, by_tile=mixed_waits, skip=1)

            parts = lambda k: (HNH[:, k, :], HNL[:, k, :])

            def feed_forward(layer, n, segs):
                norm_sum(n, segs)
                for half in range(2):
                    name = f"{layer}{half}"

                    def up(gs, i, r):
                        ready = half == 0 and isinstance(r, int) and r == 0
                        two_blocks(gs, i, parts, segs,
                                   by_tile=waits(hn_hi, KT * n, hn_ready, KT * n) if ready else None)
                    job_turns(pe, "up" + name, FH, up, peel=1)
                    done = FH * (2 * layer + half)
                    res_block("down" + name, lambda k: (HIDH[:, k, :], HIDL[:, k, :]), segs,
                              by_tile=waits(hid_hi, done, hid_ready, done))

            feed_forward(0, 1, SEGS)

            norm_sum(2)
            LS = (SEGS[0],)

            def rotated(b, n):
                read([AT["qkv"] + n // 2], 0, b, pe)
                if n:
                    pe.wait_ge(q_done, n)
                mm(PS[:, 6, :], C[:, ROT, :], T[:, b, 0:LAT], start=True, stop=True).then_inc(q_rot, 1)

            for n in range(5):
                two_blocks([AT["qkv"] + n], 0, parts, LS if n < 4 else SEGS,
                           between=(lambda: (rotated(0, 2 * n - 2), rotated(1, 2 * n - 1))) if n else None,
                           by_tile=waits(hn_hi, 2 * KT, hn_ready, 2 * KT) if n == 0 else None)
            g = AT["qkv"] + 5
            half_ready([g], 0, 1)
            for t in range(6):
                acc = PSF[:, 2048 + 256 * t:2048 + 256 * t + 256] if t < 4 else PS[:, 7, 256 * (t - 4):256 * (t - 3)]
                for k in range(KT):
                    wh = WH[:, k // 4, 2 * (k % 4):2 * (k % 4) + 2, :].rearrange("p a b -> p (a b)")
                    wl = WL[:, g % SLOTS, 2 * k:2 * k + 2, :].rearrange("p a b -> p (a b)")
                    h, l = HNH[:, k, t * P:t * P + P], HNL[:, k, t * P:t * P + P]
                    mm(acc, h, wh, start=k == 0, stop=False)
                    prev = mm(acc, h, wl, start=False, stop=False)
                    ins = mm(acc, l, wh, start=False, stop=k == KT - 1)
            prev.then_inc(blocks_done, 1)
            ins.then_inc(blocks_done, 1)
            for b in range(2):
                rotated(b, 8 + b)

            pe.wait_ge(k_done, 2)
            pe.wait_ge(v_done, 2)
            for u in range(2):
                pe.wait_ge(pair_free[u], uses(u, AT["out1"]))

            def attend(i, first):
                pe.wait_ge(at_q, i + 1)

                def scores(n):
                    b, h = divmod(n, 4)
                    lo, hi = max(b - 1, 0) * P, min(b + 2, 4) * P
                    w = hi - lo
                    c0 = 512 - w
                    r = n % 2
                    if not (first and n < 2):
                        pe.wait_ge(at_exp, i * 16 + (n - 1))
                    S = PSF[:, 1024 * r:1024 * r + 768]
                    p0 = 64 * (h % 2)
                    q = QG[p0:p0 + 64, h // 2, b * P:b * P + P]
                    mm(S[:, c0:512], q, KG[p0:p0 + 64, lo:hi], start=True, stop=False)
                    if b > 0:
                        mm(S[:, c0:c0 + P], C[:, IDENT, :], C[:, MLEFT, :], start=False, stop=b == 3)
                    if b < 3:
                        mm(S[:, 384:512], C[:, IDENT, :], C[:, MRIGHT, :], start=False, stop=True)
                    mm(S[:, 512:768], q, KG[p0:p0 + 64, LAT:TOK], start=True, stop=True).then_inc(at_s, 1)

                def flip(n):
                    b = n // 4
                    w = (min(b + 2, 4) - max(b - 1, 0)) + 2
                    pe.wait_ge(at_exp, i * 16 + (n + 1))
                    if not (first and n == 0):
                        pe.wait_ge(at_ptc, i * 16 + n)
                    for t in range(w):
                        ins = pe.transpose(PSF[:, 2048 + t * P:2048 + t * P + P], PR[:, n % 2, t * P:t * P + P],
                                           C[:, IDENT, :])
                    ins.then_inc(at_pt, 1)

                def values(n):
                    b, h = divmod(n, 4)
                    lo, w = max(b - 1, 0), (min(b + 2, 4) - max(b - 1, 0)) + 2
                    pe.wait_ge(at_ptc, i * 16 + (n + 1))
                    if h == 0 and not (first and b == 0):
                        pe.wait_ge(at_o, i * 4 + b)
                    for t in range(w):
                        kt = lo + t if t < w - 2 else 4 + t - (w - 2)
                        ins = mm(PS[:, 6, 64 * h:64 * h + 64], PTS[:, n % 2, t * P:t * P + P],
                                 VG[:, kt, :],
                                 start=t == 0, stop=t == w - 1)
                    ins.then_inc(at_pv, 1)

                def out_t(b):
                    pe.wait_ge(at_o, i * 4 + (b + 1))
                    if not (first and b == 0):
                        pe.wait_ge(at_otlo, i * 4 + b)
                    for j in range(2):
                        ins = pe.transpose(PS[:, 7, j * P:j * P + P],
                                           OTOK[:, b, 2 * j:2 * j + 2, :].rearrange("p a b -> p (a b)"),
                                           C[:, IDENT, :])
                    ins.then_inc(at_ot, 1)

                for n in range(16 + 3):
                    if n < 16:
                        scores(n)
                    if 1 <= n <= 16:
                        flip(n - 1)
                    if 2 <= n <= 17:
                        values(n - 2)
                    if n >= 6 and (n - 6) % 4 == 0:
                        out_t((n - 6) // 4)

            attend(0, True)
            with pe.Fori(1, KV) as i:
                attend(i, False)

            pe.wait_ge(at_otlo, 16)
            for n in range(4):
                two_blocks([AT["out1"] + n], 0, lambda k: (OTH[:, k, :], OTL[:, k, :]), LS)
            feed_forward(1, 3, LS)
            norm_sum(4, LS)

        @block.scalar
        def _(act):
            ch = Count(act, a_ch)
            run = act.activation
            Id = ACT.Identity

            def apart():
                act.wait_ge(v_in, 16)

            act.dma_start(V[:, 0:VEC_W - 2], A["vec"]).then_inc(v_in, 16)
            act.dma_start(ZT[0:HY_EMB, :], A["zfeat"]).then_inc(small_in, 16)
            act.dma_start(W1S[0:HY_EMB, :], A["hy_w1"]).then_inc(small_in, 16)
            act.dma_start(WS[0:64, 0, :], A["hy_w2"]).then_inc(small_in, 16)
            act.dma_start(WS[0:64, 1, :], A["hy_w3"]).then_inc(small_in, 16)
            act.dma_start(FBV[0:64, 0:6], A["hy_fb"]).then_inc(small_in, 16)
            act.dma_start(W4[0:64, :], A["hy_w4"]).then_inc(small_in, 16)
            act.dma_start(C[:, :, :], A["const"].rearrange("p (a b) -> p a b", a=9)).then_inc(c_in, 16)
            act.dma_start(WIN[:, :, :], A["window"][:, 0, :, :]).then_inc(win_in, 16)
            act.dma_start(BB[:, :], A["hy_bias"][0:1, 0:512].broadcast_to([P, 512])).then_inc(bias_in, 16)
            act.dma_start(C3[:, :, :], A["tab3"].rearrange("p (a b) -> p a b", a=2)).then_inc(t3_in, 16)
            act.dma_start(WD[:, :, :], A["w_dt"]).then_inc(wdt_in, 16)

            act.wait_ge(v_in, 16)
            act.wait_ge(eps_ready, 1)
            run(CS[:, :, :], V[:, _cols["cc"]:_cols["cc"] + 16].rearrange("p (k c) -> p k c", c=2),
                ACT.Silu).then_inc(silu_c, 1)

            def copy_row(gs, i):
                act.wait_ge(blocks_done, along([2 * g + 4 for g in gs], i))
                first = len(gs) == 1 and PAIR[gs[0]] == 0
                if not first:
                    act.wait_ge(flipped, along([PAIR[g] for g in gs], i))
                run(ROWS[PAIR[gs[-1]] >= 8][0:2, :], PS[0:2, 6, :], ACT.Copy).then_inc(row_copied, 1)

            copy_row([AT["ada_a"]], 0)
            for layer in range(3):
                act.wait_ge(mlp_mm, layer + 1)
                act.wait_ge(fb_ready, 1)
                run(HF[0:64, layer, :], PSF[0:64, 0:TOK], Id, scale=FBV[0:64, layer:layer + 1],
                    bias=FBV[0:64, 6 + layer:7 + layer]).then_inc(mlp_arg, 1)
                act.wait_ge(mlp_red, layer + 1)
                run(HF[0:64, layer, :], HF[0:64, layer, :], ACT.Sin).then_inc(mlp_sin, 1)
                copy_row([AT["ada_a"] + 2 * (layer + 1)], 0)
            early = 4
            for c in range(2):
                for t in range(6):
                    n = 6 * c + t
                    act.wait_ge(kg_sd, n + 1)
                    if n:
                        act.wait_ge(ssq_added, n)
                    run(SQ2[:, :, :], SD[:, :, t, :], ACT.Square).then_inc(kg_sq, 1)
                    if t % 2 and early < 8:
                        copy_row([AT["ada_a"] + 2 * early], 0)
                        early += 1
                if c:
                    act.wait_ge(kg_mm, 12)
                    act.dma_start(X[:, :, :], A["xT"]).then_inc(x_in, 16)
                act.wait_ge(kg_ssq, c + 1)
                run(KR[0], PS[:, 4, 0:16], ACT.Sqrt, scale=0.5, bias=vec("eps", 0)).then_inc(kg_root, 1)
                act.wait_ge(kg_spread, c + 1)
                if c:
                    act.wait_ge(kd_ev, 12)
                run(INV[:, :, :], PS[:, 4:6, :], ACT.Copy).then_inc(inv_ready, 1)
                while early < 8:
                    copy_row([AT["ada_a"] + 2 * early], 0)
                    early += 1

            def sqrt_table():
                run(MARK[:, 1:2], vec("eps", 0), ACT.Sqrt)

            def root(segs=SEGS):
                n = 2 * segs[-1][1] // P
                run(RS[0][:, 0:n], NS[:, 0:n], ACT.Sqrt, scale=1.0 / D, bias=vec("eps", 0)).then_inc(n_sqrt, 1)

            def high_parts(muls, segs=SEGS, high=HNH):
                lo, hi = segs[0][0], segs[-1][1]
                for k in range(KT):
                    act.wait_ge(n_mul, muls + k + 1)
                    run(high[:, k, lo:hi], HN[:, k, lo:hi], ACT.Copy).then_inc(hn_hi, 1)

            act.wait_ge(n_summed, 1)
            root()
            high_parts(0, high=HNH0)

            def conv_first(gs, i, b, wname, bname, blk, tbuf, wait=None):
                act.wait_ge(blocks_done, along([2 * g + 1 + b for g in gs], i))
                if wait:
                    wait()
                u = PLAN[gs[0]][b][0]
                apart()
                run(T[:, tbuf, :], pair(u), Id, scale=blk(wname), bias=blk(bname)).then_inc(cv_act, 1)

            act.wait_ge(kd_mm, 24)
            act.dma_start(C4[:, :, :], A["tab4"].rearrange("p (a b) -> p a b", a=2)).then_inc(t4_in, 16)

            def uv(gs, i, first):
                if not first:
                    copy_row([g - 2 for g in gs], i)
                for b in range(2):
                    def free():
                        if not first:
                            act.wait_ge(u_ready, i)
                    conv_first(gs, i, b, "hcw", "hcb", lambda nm: dvec(nm, (24 if nm == "hcw" else 0) + 8 + 8 * b, nm_i), b,
                               free)
                    if b == 0 and not first:
                        copy_u(i - 1)

            def copy_u(i):
                act.wait_ge(tp_mm, i + 1)
                apart()
                dst = UT[:, :, bass.ds(i, 1) if not isinstance(i, int) else slice(i, i + 1), :]
                run(dst, TP.rearrange("p (t a c) -> p t a c", t=6, a=1), ACT.Copy).then_inc(tp_copied, 1)

            firstj = AT["uv"]
            nm_i = 0
            uv([firstj], 0, True)
            with act.Fori(1, 8) as i:
                nm_i = i
                gs = [firstj + 3 * n for n in range(8)]
                uv(gs, i, False)
            copy_u(7)

            for n in range(4):
                g = AT["x0"] + 3 * n
                copy_row([g - 2], 0)
                for b in range(2):
                    j = 2 * n + b

                    def free():
                        if j >= 2:
                            act.wait_ge(g_ready, j - 1)
                        else:
                            act.wait_ge(p_ready, 12)
                    conv_first([g], 0, b, "hcw", "hcb", lambda nm: dvec(nm, (24 if nm == "hcw" else 0), j), b, free)

            act.wait_ge(inv_mm, 8)

            def z_turn(i):
                gs = [AT["z"] + 3 * n for n in range(4)]
                copy_row([g - 2 for g in gs], i)
                for b in range(2):
                    act.wait_ge(blocks_done, along([2 * g + 1 + b for g in gs], i))
                    apart()
                    blk = i * 2 + b
                    dst = Z[:, blk, :] if isinstance(blk, int) else \
                        Z[:, bass.ds(blk, 1), :].rearrange("p a b -> p (a b)")
                    run(dst, pair(b), ACT.Silu).then_inc(pair_free[b], 1)
            loops(act, 4, z_turn)

            def copy_x(blk):
                act.wait_ge(xt_mm, blk + 1)
                if blk < 8:
                    dst = XT_[:, :, blk, :]
                else:
                    dst = BT[:, :, blk - 8, :]
                run(dst, TP.rearrange("p (t c) -> p t c", t=6), ACT.Copy).then_inc(xt_copied, 1)

            def x_by_token(k):
                copy_x(k)
                if k < KT:
                    run(XBC[:, k, :], XBC[:, k, :], ACT.Copy, scale=vec("dskip", k)).then_inc(dx_ready, 1)

            copy_row([AT["xbc"] - 2], 0)
            act.wait_ge(dta_raw, 1)
            run(SPU[:, 1, :], SPU[:, 0, :], ACT.Exp, scale=-1.0).then_inc(sp_exp, 1)
            run(vec("alog", 0, 32), vec("alog", 0, 32), ACT.Exp).then_inc(sp_exp, 1)
            for n in range(6):
                g = AT["xbc"] + n
                for b in range(2):
                    blk = 2 * n + b

                    def free():
                        if blk < 2:
                            act.wait_ge(g_ready, 8)
                    if blk >= 2:
                        act.wait_ge(xs_ready, blk - 1)
                    conv_first([g], 0, b, "scw", "scb", lambda nm: dvec(nm, (12 if nm == "scw" else 0), blk), b, free)
                    if b == 0 and 0 < n < 5:
                        x_by_token(2 * n - 2)
                for b in range(2):
                    blk = 2 * n + b
                    read([g], 0, b, act)
                    run(XBC[:, blk, :], T[:, b, :], ACT.Silu).then_inc(xs_ready, 1)
                if n:
                    if n == 5:
                        x_by_token(8)
                    x_by_token(2 * n - 1)
                if n == 3:
                    act.wait_ge(dec_mm, 1)
                    run(DEC, PS[:, 6, 0:384], ACT.Exp).then_inc(dec_ready, 1)
            act.wait_ge(blocks_done, 2 * G0)
            act.dma_start(X[:, :, :], A["xT"]).then_inc(x_in, 16)
            def place_b(s, d, t):
                if not (isinstance(s, int) and s < 2):
                    act.wait_ge(s_st, s * 2 - 2)
                    apart()
                run(BST[d][:, 0:2, :], XBC[:, 8:10, bass.ds(t * P, P)], ACT.Copy)
                run(BST[d][:, 2:4, :], BT[:, bass.ds(t, 1), :, :].rearrange("p a b c -> p (a b) c"),
                    ACT.Copy).then_inc(s_bst, 1)

            def turn(s0, chunks, last):
                for d in range(2):
                    s = s0 + d
                    for b in range(4):
                        if b == 3 and not (last and d == 1):
                            place_b(s + 1, 1 - d, chunks[d + 2])
                        act.wait_ge(s_seg, s * 4 + (b + 1))
                        if not (isinstance(s, int) and s == 0 and b < 2):
                            act.wait_ge(s_y, s * 4 + (b - 1))
                        r = b % 2
                        run(LEB[:, r, :], PSF[:, 1024 * r:1024 * r + 1024], ACT.Exp).then_inc(s_exp, 1)

            act.wait_ge(xt_copied, 10)
            act.wait_ge(xs_ready, XBC_BLKS)
            place_b(0, 0, 4)
            chunk_turns(act, turn)

            act.wait_ge(s_xdt, STEPS)
            for k in range(KT):
                run(YGH[:, 1, k, :], G[:, k, :], ACT.Copy).then_inc(mix_hi, 1)
            for k in range(KT):
                act.wait_ge(yz_ready, k + 1)
                if k >= 2:
                    act.wait_ge(sq_mm, k - 1)
                run(T[:, k % 2, :], XBC[:, k, :], ACT.Square).then_inc(sq_ready, 1)
            act.wait_ge(sq_mm, KT)
            run(T[:, 2, :], NP, ACT.Sqrt, scale=1.0 / D, bias=vec("eps", 0)).then_inc(n_sqrt, 1)
            for k in range(KT):
                act.wait_ge(n_mul, KT + k + 1)
                run(YGH[:, 0, k, :], XBC[:, k, :], ACT.Copy).then_inc(mix_hi, 1)

            def feed_forward(layer, n, segs):
                sqrt_table()
                act.wait_ge(n_summed, n + 1)
                root(segs)
                high_parts(KT * (n + 1), segs)
                lo, hi = segs[0][0], segs[-1][1]
                for half in range(2):
                    name = f"up{layer}{half}"
                    done = FH * (2 * layer + half)

                    def up(gs, i, r):
                        act.wait_ge(blocks_done, along([2 * g + 1 for g in gs], i))
                        act.wait_ge(pair_free[1], along([PLAN[g][1][1] for g in gs], i))
                        run(T[:, 0, lo:hi], pair(0)[:, lo:hi], ACT.Silu).then_inc(pair_free[0], 1)
                        read(gs, i, 1, act)
                        apart()
                        run(at_row(HIDH, r)[:, lo:hi], T[:, 1, lo:hi], ACT.Copy).then_inc(hid_hi, 1)
                    job_turns(act, name, FH, up, peel=1)

            feed_forward(0, 1, SEGS)

            sqrt_table()
            act.wait_ge(n_summed, 3)
            root()
            high_parts(3 * KT)
            for n in range(5):
                g = AT["qkv"] + n
                w = LAT if n < 4 else TOK
                for b in range(2):
                    m = 2 * n + b
                    act.wait_ge(blocks_done, 2 * g + 1 + b)
                    if m >= 2:
                        act.wait_ge(q_done, m - 1)
                    run(T[:, b, 0:w], pair(b)[:, 0:w], ACT.Copy).then_inc(pair_free[b], 1)
            g = AT["qkv"] + 5
            act.wait_ge(blocks_done, 2 * g + 2)
            run(VT[:, 0:4, :], PSF[:, 2048:3072].rearrange("p (t c) -> p t c", t=4), ACT.Copy).then_inc(v_done, 1)
            act.wait_ge(blocks_done, 2 * g + 2)
            run(VT[:, 4:6, :], PS[:, 7, :].rearrange("p (t c) -> p t c", t=2), ACT.Copy).then_inc(v_done, 1)

            def attend(i, first):
                act.wait_ge(q_done, 10)
                if not first:
                    act.wait_ge(at_pv, i * 16)
                act.wait_ge(k_done, 2)
                act.wait_ge(v_done, 2)
                apart()
                at = i * 4 + _cols["sink"]
                run(AST[:, 200:204], V[:, bass.ds(at, 4)], ACT.Copy).then_inc(at_group, 1)
                run(KG, KD[:, bass.ds(i, 1), :].rearrange("p a b -> p (a b)"), ACT.Copy)
                run(VG[:, :, :], VT[:, :, bass.ds(i * 64, 64)], ACT.Copy)
                src = QT[:, bass.ds(i * 2, 2), :] if not isinstance(i, int) else QT[:, 2 * i:2 * i + 2, :]
                run(QG[:, :, :], src, ACT.Copy).then_inc(at_q, 1)
                act.wait_ge(at_group, i + 1)

                def probs(n):
                    b, h = divmod(n, 4)
                    w = (min(b + 2, 4) - max(b - 1, 0) + 2) * P
                    c0 = 768 - w
                    act.wait_ge(at_neg, i * 16 + (n + 1))
                    if not (first and n < 2):
                        act.wait_ge(at_pt, i * 16 + (n - 1))
                    r = n % 2
                    run(AST[:, 64 + n:65 + n], AST[:, 200 + h:201 + h], ACT.Exp, bias=AST[:, 32 + n:33 + n]) \
                        .then_inc(at_sinkexp, 1)
                    run(PR[:, r, 0:w], PSF[:, 1024 * r + c0:1024 * r + 768], ACT.Exp, scale=ATTN_SCALE,
                        bias=AST[:, 32 + n:33 + n], accum_out=AST[:, 96 + n:97 + n]).then_inc(at_exp, 1)

                def out_copy(b):
                    act.wait_ge(at_ot, i * 4 + (b + 1))
                    apart()
                    run(OTH[:, bass.ds(i * 2, 2), b * P:b * P + P],
                        PS[:, 7, 0:256].rearrange("p (a c) -> p a c", a=2), ACT.Copy).then_inc(at_othi, 1)

                for n in range(16 + 3):
                    if n < 16:
                        probs(n)
                    if n >= 7 and (n - 7) % 4 == 0:
                        out_copy((n - 7) // 4)
                out_copy(3)

            attend(0, True)
            with act.Fori(1, KV) as i:
                attend(i, False)

            feed_forward(1, 3, (SEGS[0],))
            sqrt_table()
            act.wait_ge(n_summed, 5)
            root((SEGS[0],))

        @block.vector
        def _(dve):
            ch = Count(dve, v_ch)
            TS, TT, STT = dve.tensor_scalar, dve.tensor_tensor, dve.scalar_tensor_tensor

            def halves(ap, n):
                return ap.rearrange("p (a c) -> p a c", a=n)

            dve.wait_ge(small_in, 16 * 6)
            TT(FBV[0:64, 6:9], FBV[0:64, 0:3], FBV[0:64, 3:6], ALU.mult).then_inc(fb_ready, 1)

            MAGIC = 1.5 * 2.0 ** 23
            TWO_PI_HI, TWO_PI_LO = 6.28125, 2 * float(np.pi) - 6.28125
            PI_IN = 3.1415925
            for layer in range(3):
                dve.wait_ge(mlp_arg, layer + 1)
                h, q = HF[0:64, layer, :], T[0:64, 0, :]
                ch.link(TS(q, h, 1.0 / (2 * float(np.pi)), MAGIC, ALU.mult, ALU.add))
                ch.link(TS(q, q, MAGIC, None, ALU.subtract))
                ch.link(STT(h, q, -TWO_PI_HI, h, ALU.mult, ALU.add))
                ch.link(STT(h, q, -TWO_PI_LO, h, ALU.mult, ALU.add))
                TS(h, h, PI_IN, -PI_IN, ALU.min, ALU.max).then_inc(mlp_red, 1)

            def mods(layer, lo, hi):
                ab = V[:, _cols["ada_b"] + 48 * layer + lo:_cols["ada_b"] + 48 * layer + hi]
                return TT(MOD[:, layer, lo:hi, :], MODP[:, layer, lo:hi, :],
                          ab.unsqueeze(2).broadcast_to([P, hi - lo, 2]), ALU.add)

            def gains(which, layer, m, name):
                g = vec(name, 8 * layer, 8).unsqueeze(2).broadcast_to([P, KT, 2])
                return STT(GA[:, which, :, :], MOD[:, layer, 8 * m:8 * m + 8, :], 1.0, g, ALU.add, ALU.mult)

            def add_squares(x, lo, hi):
                ch.link(TT(T[:, 2, lo:hi], x[:, lo:hi], x[:, lo:hi], ALU.mult))
                return TT(T[:, 3, lo:hi], T[:, 3, lo:hi], T[:, 2, lo:hi], ALU.add)

            hf, hb = Tt[:, 0:512], Tt[:, 512:1024]
            for c in range(2):
                for t in range(6):
                    n = 6 * c + t
                    if t == 0:
                        dve.wait_ge(win2_in if c else win_in, 16)
                        if c:
                            dve.wait_ge(kd_mm, 12)
                    dve.wait_ge(kg_mm, n + 1)
                    TT(hf, PS[:, 2 * (n % 2), :], WIN[:, t, :], ALU.mult)
                    ins = TT(hb, PS[:, 2 * (n % 2) + 1, :], WIN[:, t, :], ALU.mult)
                    ins.then_inc(kg_free, 1)
                    dve.wait_ge(kg_free, n + 1)
                    if t in (0, 4):
                        ch.link(dve.memset(hb[0:1, :], 0.0))
                    TT(SD[:, 0, t, :], hf, hb, ALU.add)
                    TT(SD[:, 1, t, :], hf, hb, ALU.subtract).then_inc(kg_sd, 1)
                    dve.wait_ge(kg_sd, n + 1)
                dve.wait_ge(kg_root, c + 1)
                dve.wait_ge(bias2_in if c else bias_in, 16)
                dve.reciprocal(KR[1], KR[0]).then_inc(kg_rec, 1)
                dve.wait_ge(inv_ready, c + 1)
                for f in range(6):
                    inv = INV[:, f >= 4, :]
                    for j in range(2):
                        n = 12 * c + 2 * f + j
                        dst = KS[:, j, f, 512 * c:512 * c + 512]
                        dve.wait_ge(kd_mm, n + 1)
                        ins = TT(dst, PS[:, n % 4, :], inv, ALU.mult)
                        if j == 0:
                            ch.link(ins)
                            ins = TT(dst, dst, BB[:, :], ALU.add)
                        ins.then_inc(kd_ev, 1)

            def norm(n, which=None, layer=0, shift=0, segs=SEGS, last=False):
                lo, hi = segs[0][0], segs[-1][1]
                dve.wait_ge(n_sqrt, n + 1)
                c = 2 * hi // P
                dve.reciprocal(RS[1][:, 0:c], RS[0][:, 0:c]).then_inc(n_rec, 1)
                dve.wait_ge(n_spread, n + 1 if n == 0 else n)
                for k in range(KT):
                    if last:
                        STT(HN[:, k, lo:hi], X[:, k, lo:hi], vec("fin", k), NP[:, lo:hi], ALU.mult, ALU.mult) \
                            .then_inc(fin_ready, 1)
                        continue
                    ch.link(TT(HN[:, k, lo:hi], X[:, k, lo:hi], NP[:, lo:hi], ALU.mult))
                    for j, (a, b) in enumerate(segs):
                        ins = TS(HN[:, k, a:b], HN[:, k, a:b], GA[:, which, k, j:j + 1],
                                 MOD[:, layer, 8 * shift + k, j:j + 1], ALU.mult, ALU.add)
                    ins.then_inc(n_mul, 1)

            def split_high(gs, i, b):
                s = gs[0] % SLOTS
                n = width(gs[0], b)
                dve.wait_ge(w_loaded[s][b], along([16 * (g // SLOTS + 1) for g in gs], i))
                dve.tensor_copy(WH[:, b, 0:n, :], W[:, s, HALF * b:HALF * b + n, :]).then_inc(w_hi, 1)

            def next_high(gs, i, b):
                if gs[-1] + 1 < len(JOBS):
                    dve.wait_ge(blocks_done, along([2 * g + 1 + b for g in gs], i))
                    split_high([SPLIT[NTH[g] + 1] for g in gs], i, b)

            dve.wait_ge(wdt_in, 16)
            dve.tensor_copy(WDH[:, :, :], WD[:, :, :]).then_inc(wdt_hi, 1)
            for b in range(2):
                split_high([AT["uv"]], 0, b)
            dve.wait_ge(v_in, 16)
            dve.wait_ge(flipped, 8)
            mods(0, 0, 16)
            ins = mods(1, 0, 16)
            ins.then_inc(mods_a, 1)
            dve.wait_ge(mods_a, 1)
            ch.link(gains(0, 0, 1, "n1"))
            norm(0, 0, 0, 0)

            def conv(gs, i, b, wname, n, blk, count):
                dve.wait_ge(cv_act, count)
                p, t = pair(PLAN[gs[0]][b][0]), T[:, b, :]
                w0, w2 = blk(wname, 0), blk(wname, 2 * n)
                for w, shift in ((w0, -1), (w2, 1)):
                    for j, (lo, hi) in enumerate(SEGS):
                        a, e = (lo + 1, hi) if shift < 0 else (lo, hi - 1)
                        ins = STT(t[:, a:e], p[:, a + shift:e + shift], w, t[:, a:e], ALU.mult, ALU.add)
                    if shift < 0:
                        ch.link(ins)
                ins.then_inc(pair_free[PLAN[gs[0]][b][0]], 1)

            def uv(i):
                gs = [AT["uv"] + 3 * n for n in range(8)]
                for b in range(2):
                    conv(gs, i, b, "hcw", 24, lambda nm, o: dvec(nm, o + 8 + 8 * b, i), i * 2 + (b + 1))
                    next_high(gs, i, b)
            with dve.Fori(0, 8) as i:
                ch.enter(i, 2)
                uv(i)
                ch.leave(8)

            for c in range(2):
                for f in range(6):
                    n = 6 * c + f
                    kc, ks = (KS[:, j, f, 512 * c:512 * c + 512] for j in range(2))
                    dve.wait_ge(u_mm, n + 1)
                    if n:
                        dve.wait_ge(p_ready, n)
                    uc, us = PS[:, 2 * (n % 2), :], PS[:, 2 * (n % 2) + 1, :]
                    for m, (x, y) in enumerate(((uc, kc), (us, ks), (uc, ks), (us, kc))):
                        ins = TT(Tt[:, 512 * m:512 * m + 512], x, y, ALU.mult)
                    ins.then_inc(u_prod, 1)

            for n in range(4):
                g = AT["x0"] + 3 * n
                for b in range(2):
                    conv([g], 0, b, "hcw", 24, lambda nm, o: dvec(nm, o, 2 * n + b), 16 + 2 * n + b + 1)
                    next_high([g], 0, b)
                read([g], 0, 1, dve)
                for b in range(2):
                    j = 2 * n + b
                    dve.wait_ge(inv_mm, j + 1)
                    STT(G[:, j, 0:LAT], TP[:, 0:LAT], 1.0 / LAT, T[:, b, 0:LAT], ALU.mult, ALU.mult)
                    STT(G[:, j, LAT:TOK], TP[:, LAT:TOK], 1.0 / CTX, T[:, b, LAT:TOK], ALU.mult, ALU.mult) \
                        .then_inc(g_ready, 1)

            def z_turn(i):
                for b in range(2):
                    next_high([AT["z"] + 3 * n for n in range(4)], i, b)
            loops(dve, 4, z_turn)

            dve.wait_ge(dt_mm, 1)
            raw, e, q = SPT, SPU[:, 1, :], SPU[:, 0, :]
            ch.link(TT(raw.rearrange("p (t h) -> p t h", t=6), PS[:, 4, 0:192].rearrange("p (t h) -> p t h", t=6),
                       vec("dtb", 0, 32).unsqueeze(1).broadcast_to([P, 6, 32]), ALU.add))
            STT(q, raw, -1.0, raw, ALU.mult, ALU.max).then_inc(dta_raw, 1)
            dve.wait_ge(sp_exp, 2)
            s2, r = DTS[:, 0:192], DTS[:, 192:384]
            ch.link(TS(r, e, 2.0, None, ALU.add))
            ch.link(dve.reciprocal(r, r))
            ch.link(TT(e, e, r, ALU.mult))
            ch.link(TT(s2, e, e, ALU.mult))
            ch.link(TS(q, s2, 1.0 / 17, None, ALU.mult))
            for m in range(7, 0, -1):
                ch.link(STT(q, q, 1.0 / (2 * m + 1), s2, ALU.add, ALU.mult))
            ch.link(STT(q, q, 1.0, e, ALU.add, ALU.mult))
            ch.link(TS(raw, raw, 0.0, None, ALU.max))
            ch.link(STT(DTS[:, 0:192], q, 2.0, raw, ALU.mult, ALU.add))
            STT(DTA[:, :, :], DTP[:, :, :], -1.0, vec("alog", 0, 32).unsqueeze(1).broadcast_to([P, 6, 32]),
                ALU.mult, ALU.mult).then_inc(dt_a, 1)

            dve.wait_ge(flipped, 24)
            mods(0, 16, 48)
            mods(1, 16, 48).then_inc(mods_b, 1)
            dve.wait_ge(mods_b, 1)
            gains(1, 0, 4, "n2").then_inc(pair_free[2], 1)
            gains(2, 1, 1, "n1")
            gains(3, 1, 4, "n2").then_inc(gains_ready, 1)

            for n in range(6):
                for b in range(2):
                    if n < 5:
                        next_high([AT["xbc"] + n], 0, b)
                    conv([AT["xbc"] + n], 0, b, "scw", 12, lambda nm, o: dvec(nm, o, 2 * n + b), 24 + 2 * n + b + 1)

            dve.wait_ge(blocks_done, 2 * G0)
            dve.tensor_copy(SUMS[:, :, :], C[:, ONES:KLTJ + 1, :])
            ch.link(dve.tensor_copy(DTAH[:, :, :], DTA[:, :, :]))
            TT(DTAL[:, :, :], DTA[:, :, :], DTAH[:, :, :].bitcast(f32), ALU.subtract).then_inc(dta_split, 1)
            dve.wait_ge(st_zero, 1)
            dve.wait_ge(dec_ready, 1)
            dve.wait_ge(xt_copied, 10)
            dve.wait_ge(dx_ready, KT)

            def at(ap3, t):
                return ap3[:, bass.ds(t, 1), :].rearrange("p a b -> p (a b)")

            DECF = DEC[:, 0:96].rearrange("p (t h) -> p t h", t=6)
            DECB = DEC[:, 96:192].rearrange("p (t h) -> p t h", t=6)
            TOT = DEC[:, 192:384].rearrange("p (t h) -> p t h", t=6)
            XTF = region(6144, 6, D)

            def scale_x(s, d, t):
                if not (isinstance(s, int) and s < 2):
                    dve.wait_ge(s_y, s * 4 - 4)
                    dve.wait_ge(s_xde, s - 1)
                TT(XDT[d].rearrange("p (h c) -> p h c", h=HEADS), at(XTF, t).rearrange("p (h c) -> p h c", h=HEADS),
                   at(DTP, t)[:, 16 * d:16 * d + 16].unsqueeze(2).broadcast_to([P, HEADS, HD]), ALU.mult) \
                    .then_inc(s_xdt, 1)

            def mask_cb(s, d):
                dve.wait_ge(s_cb, s + 1)
                if not (isinstance(s, int) and s < 2):
                    dve.wait_ge(s_mc, s * 4 - 4)
                TT(CBM[:, d, :, :], PS[:, 5, 0:256].rearrange("p (g c) -> p g c", g=2),
                   C[:, LE if d == 0 else GE, :].unsqueeze(1).broadcast_to([P, 2, P]), ALU.mult).then_inc(s_cbm, 1)

            def weigh(s, d, t, b):
                g, r = b // 2, b % 2
                if b == 0:
                    dve.wait_ge(s_cbm, s + 1)
                dve.wait_ge(s_exp, s * 4 + (b + 1))
                l3 = LEB[:, r, 0:512].rearrange("p (h c) -> p h c", h=4)
                e3 = LEB[:, r, 512:1024].rearrange("p (h c) -> p h c", h=4)
                TT(l3, l3, CBM[:, d, g, :].unsqueeze(1).broadcast_to([P, 4, P]), ALU.mult)
                ct = XBC[:, 10 + g, bass.ds(t * P, P)].unsqueeze(1)
                TT(e3, e3, ct.broadcast_to([P, 4, P]), ALU.mult).then_inc(s_mc, 1)

            def add_y(s, t, half):
                dve.wait_ge(s_y, s * 4 + (2 * half + 2))
                xs = XBC[:, 4 * half:4 * half + 4, bass.ds(t * P, P)]
                TT(xs, xs, PS[:, 6 + half, :].rearrange("p (k c) -> p k c", k=4), ALU.add).then_inc(s_yadd, 1)

            def decay_state(s, d, t):
                h3 = HST[:, d, :].rearrange("p (h c) -> p h c", h=HEADS)
                ch.link(TT(h3, h3, at(TOT, t)[:, 16 * d:16 * d + 16].unsqueeze(2).broadcast_to([P, HEADS, HD]),
                           ALU.mult))

            def add_state(s, d, g):
                dve.wait_ge(s_st, s * 2 + (g + 1))
                hg = HST[:, d, 512 * g:512 * g + 512]
                TT(hg, hg, PS[:, 4, :], ALU.add).then_inc(s_stf, 1)

            def turn(s0, chunks, last):
                for d in range(2):
                    s, told, t = s0 + d, chunks[d], chunks[d + 1]
                    before = not (isinstance(s, int) and s == 0)
                    weigh(s, d, t, 0)
                    if before:
                        add_y(s - 1, told, 1)
                        if not (last and d == 1):
                            decay_state(s - 1, 1 - d, told)
                            add_state(s - 1, 1 - d, 0)
                    weigh(s, d, t, 1)
                    if not (last and d == 1):
                        scale_x(s + 1, 1 - d, chunks[d + 2])
                    weigh(s, d, t, 2)
                    if before and not (last and d == 1):
                        add_state(s - 1, 1 - d, 1)
                    if before:
                        dve.wait_ge(s_yadd, s * 2)
                    add_y(s, t, 0)
                    if not (last and d == 1):
                        mask_cb(s + 1, 1 - d)
                    weigh(s, d, t, 3)

            scale_x(0, 0, 4)
            mask_cb(0, 0)
            chunk_turns(dve, turn, ch, 2)
            add_y(STEPS - 1, 0, 1)
            dve.wait_ge(s_yadd, 2 * STEPS)
            dve.wait_ge(s_bst, STEPS)
            for b in range(2):
                split_high([G0], 0, b)
            for k in range(KT):
                TT(XBC[:, k, :], XBC[:, k, :], Z[:, k, :], ALU.mult).then_inc(yz_ready, 1)
            dve.wait_ge(n_sqrt, 2)
            ch.link(dve.reciprocal(T[:, 3, :], T[:, 2, :]))
            for k in range(KT):
                STT(XBC[:, k, :], XBC[:, k, :], vec("sng", k), T[:, 3, :], ALU.mult, ALU.mult).then_inc(n_mul, 1)

            def column(layer, m, k, j):
                c = k * 1 + 8 * m if not isinstance(k, int) else k + 8 * m
                return MOD[:, layer, bass.ds(c, 1), j:j + 1].rearrange("p a b -> p (a b)")

            def res(name, layer, m, segs, squares=True):
                two = name == "out1"
                lo, hi = segs[0][0], segs[-1][1]
                if squares:
                    ch.link(dve.memset(T[:, 3, lo:hi], 0.0))

                def body(gs, i, r):
                    if not two:
                        next_high(gs, i, 0)
                    for b in range(2 if two else 1):
                        if two or b == 0:
                            next_high(gs, i, b if two else 1)
                        k = r if not two else 2 * r + b
                        if two:
                            dve.wait_ge(blocks_done, along([2 * g + 1 + b for g in gs], i))
                        u = PLAN[gs[0]][b][0]
                        x = at_row(X, k)
                        if gs[-1] + 1 == len(JOBS):
                            dve.wait_ge(blocks_done, 2 * len(JOBS))
                        for j, (a, e) in enumerate(segs):
                            ins = STT(x[:, a:e], pair(u)[:, a:e], column(layer, m, k, j), x[:, a:e],
                                      ALU.mult, ALU.add)
                        ins.then_inc(pair_free[u], 1)
                        if squares:
                            read(gs, i, b, dve)
                            ch.link(add_squares(x, lo, hi))
                if two:
                    for r in range(4):
                        body([AT[name] + r], 0, r)
                else:
                    peel = 2 if name == "out0" else 0
                    job_turns(dve, name, 8, body, ch, 2 * SLOTS if squares else 0, peel)
                if squares:
                    dve.memset(MARK[:, 0:1], 0.0).then_inc(sums_ready, 1)

            def feed_forward(layer, n, segs):
                norm(n + 1, 2 * layer + 1, layer, 3, segs)
                lo, hi = segs[0][0], segs[-1][1]
                for half in range(2):
                    name = f"{layer}{half}"
                    done = FH * (2 * layer + half)

                    def up(gs, i, r):
                        next_high(gs, i, 0)
                        next_high(gs, i, 1)
                        read(gs, i, 0, dve)
                        TT(T[:, 1, lo:hi], T[:, 0, lo:hi], pair(1)[:, lo:hi], ALU.mult).then_inc(pair_free[1], 1)
                        dve.wait_ge(hid_hi, r + (done + 1))
                        TT(at_row(HIDL, r)[:, lo:hi], T[:, 1, lo:hi], at_row(HIDH, r)[:, lo:hi].bitcast(f32),
                           ALU.subtract).then_inc(hid_ready, 1)
                        dve.wait_ge(hid_ready, r + (done + 1))
                    job_turns(dve, "up" + name, FH, up, peel=1)
                    res("down" + name, layer, 5, segs, squares=half == 1)

            dve.wait_ge(n_mul, 2 * KT)
            dve.wait_ge(x_in, 32)
            res("out0", 0, 2, SEGS)
            feed_forward(0, 1, SEGS)
            norm(3, 2, 1, 0)

            dve.wait_ge(rope_in, 16)
            for m in range(10):
                b = m % 2
                if b == 0:
                    for h in range(2):
                        next_high([AT["qkv"] + m // 2], 0, h)
                    if m == 8:
                        for h in range(2):
                            next_high([AT["qkv"] + 5], 0, h)
                dve.wait_ge(q_rot, m + 1)
                TT(T[:, 2, 0:LAT], PS[:, 6, :], RC[:, 1, :], ALU.mult)
                ch.link(TT(T[:, 3, 0:LAT], T[:, b, 0:LAT], RC[:, 0, :], ALU.mult))
                dst = QT[:, m, :] if m < 8 else T[:, b, 0:LAT]
                TT(dst, T[:, 3, 0:LAT], T[:, 2, 0:LAT], ALU.add).then_inc(q_done, 1)
                dve.wait_ge(q_done, m + 1)
                if m >= 8:
                    for g in range(2):
                        for half in range(2):
                            ins = dve.tensor_copy(KD[64 * half:64 * half + 64, 2 * b + g, :],
                                                  T[64 * g:64 * g + 64, b, :])
                    ins.then_inc(k_done, 1)

            def attend(i, first):
                def row_max(n):
                    b, h = divmod(n, 4)
                    w = (min(b + 2, 4) - max(b - 1, 0) + 2) * P
                    r = n % 2
                    dve.wait_ge(at_s, i * 16 + (n + 1))
                    ch.link(dve.tensor_reduce(AST[:, n:n + 1], PSF[:, 1024 * r + 768 - w:1024 * r + 768], AX.X, ALU.max))
                    at = i * 4 + (_cols["sink"] + h)
                    sink = V[:, bass.ds(at, 1)]
                    ch.link(TS(AST[:, 16 + n:17 + n], AST[:, n:n + 1], ATTN_SCALE, sink, ALU.mult, ALU.max))
                    TS(AST[:, 32 + n:33 + n], AST[:, 16 + n:17 + n], -1.0, None, ALU.mult).then_inc(at_neg, 1)

                def keys(n):
                    b = n // 4
                    w = (min(b + 2, 4) - max(b - 1, 0) + 2) * P
                    dve.wait_ge(at_pt, i * 16 + (n + 1))
                    if not (first and n < 2):
                        dve.wait_ge(at_pv, i * 16 + (n - 1))
                    dve.tensor_copy(PTS[:, n % 2, 0:w], PSF[:, 2048:2048 + w]).then_inc(at_ptc, 1)

                def out_low(b):
                    dve.wait_ge(at_othi, i * 4 + (b + 1))
                    rows = slice(b * P, b * P + P)
                    TT(OTL[:, bass.ds(i * 2, 2), rows], PS[:, 7, 0:256].rearrange("p (a c) -> p a c", a=2),
                       OTH[:, bass.ds(i * 2, 2), rows].bitcast(f32), ALU.subtract).then_inc(at_otlo, 1)

                def outputs(b):
                    dve.wait_ge(at_pv, i * 16 + (4 * b + 4))
                    c = 4 * b
                    ch.link(TT(AST[:, 112 + c:116 + c], AST[:, 64 + c:68 + c], AST[:, 96 + c:100 + c], ALU.add))
                    ch.link(dve.reciprocal(AST[:, 128 + c:132 + c], AST[:, 112 + c:116 + c]))
                    if not first:
                        dve.wait_ge(at_ot, i * 4 + (b - 3))
                    TT(OTOK[:, b, :, :], PS[:, 6, 0:256].rearrange("p (h c) -> p h c", h=4),
                       AST[:, 128 + c:132 + c].unsqueeze(2).broadcast_to([P, 4, HD]), ALU.mult).then_inc(at_o, 1)

                for n in range(16 + 3):
                    if n < 16:
                        row_max(n)
                    if 1 <= n <= 16:
                        keys(n - 1)
                    if n >= 8 and n % 4 == 0:
                        out_low(n // 4 - 2)
                    if n >= 5 and (n - 5) % 4 == 0:
                        outputs((n - 5) // 4)
                out_low(3)

            attend(0, True)
            with dve.Fori(1, KV) as i:
                ch.enter(i, 2 * 16 + 2 * 4)
                ch.n -= ch.per
                ch.base = ch.n
                attend(i, False)
                ch.leave(KV)

            res("out1", 1, 2, (SEGS[0],))
            feed_forward(1, 3, (SEGS[0],))
            norm(5, segs=(SEGS[0],), last=True)

        @block.gpsimd
        def _(pool):
            TT = pool.tensor_tensor
            pool.memset(vec("eps", 0), EPS).then_inc(eps_ready, 1)
            def add_ssq(c):
                for t in range(6):
                    n = 6 * c + t
                    pool.wait_ge(kg_sq, n + 1)
                    acc = SSA[:, t >= 4, :]
                    if t in (0, 4):
                        if c and t == 0:
                            pool.wait_ge(kg_ssq, 1)
                        TT(acc, SQ2[:, 0, :], SQ2[:, 1, :], ALU.add).then_inc(ssq_added, 1)
                        continue
                    pool.wait_ge(ssq_added, n)
                    TT(acc, acc, SQ2[:, 0, :], ALU.add).then_inc(g_ch, 1)
                    pool.wait_ge(g_ch, 4 * c + {1: 1, 2: 2, 3: 3, 5: 4}[t])
                    TT(acc, acc, SQ2[:, 1, :], ALU.add).then_inc(ssq_added, 1)
            add_ssq(0)
            pool.wait_ge(kg_free, 6)
            pool.dma_start(WIN[:, :, :], A["window"][:, 1, :, :]).then_inc(win2_in, 16)
            pool.wait_ge(kd_ev, 12)
            pool.dma_start(BB[:, :], A["hy_bias"][0:1, 512:1024].broadcast_to([P, 512])).then_inc(bias2_in, 16)
            add_ssq(1)
            pool.wait_ge(x_in, 16)
            pool.wait_ge(kg_sd, 12)
            for k in range(KT):
                dst = T[:, 0 if k else 3, :]
                TT(dst, X[:, k, :], X[:, k, :], ALU.mult).then_inc(sq_order, 1)
                pool.wait_ge(sq_order, max(2 * k, 1))
                if k:
                    TT(T[:, 3, :], T[:, 3, :], T[:, 0, :], ALU.add).then_inc(sq_order, 1)
                    pool.wait_ge(sq_order, 2 * k + 1)
            pool.memset(vec("eps", 1), EPS).then_inc(sums_ready, 1)

            def low(gs, i, halves=(0, 1)):
                s = gs[0] % SLOTS
                for b in halves:
                    at = slice(HALF * b, HALF * b + width(gs[0], b))
                    pool.wait_ge(w_hi, along([2 * NTH[g] + b + 1 for g in gs], i))
                    TT(WL[:, s, at, :], W[:, s, at, :], WH[:, b, 0:width(gs[0], b), :].bitcast(f32),
                       ALU.subtract).then_inc(w_lo, 1)

            def following(gs):
                return [SPLIT[NTH[g] + 1] for g in gs]

            def next_low(name, count, peel=0):
                job_turns(pool, name, count, lambda gs, i, r: low(following(gs), i), peel=peel)

            def low_parts(n, segs=SEGS, high=HNH):
                lo, hi = segs[0][0], segs[-1][1]
                for k in range(KT):
                    pool.wait_ge(hn_hi, KT * n + k + 1)
                    TT(HNL[:, k, lo:hi], HN[:, k, lo:hi], high[:, k, lo:hi].bitcast(f32), ALU.subtract) \
                        .then_inc(hn_ready, 1)

            pool.wait_ge(wdt_hi, 1)
            TT(WDL[:, :, :], WD[:, :, :], WDH[:, :, :].bitcast(f32), ALU.subtract).then_inc(wdt_lo, 1)
            low([AT["uv"]], 0)
            low_parts(0, high=HNH0)

            def product(i, first):
                low([AT["uv"] + 3 * (n + 1) for n in ([0] if first else range(8))], i, (0,))
                read([AT["uv"] + 3 * n for n in range(8)], i, 0, pool)
                read([AT["uv"] + 3 * n for n in range(8)], i, 1, pool)
                if not first:
                    pool.wait_ge(tp_mm, i)
                TT(T[:, 2, :], T[:, 0, :], T[:, 1, :], ALU.mult).then_inc(u_ready, 1)
                low([AT["uv"] + 3 * (n + 1) for n in ([0] if first else range(8))], i, (1,))
            product(0, True)
            with pool.Fori(1, 8) as i:
                product(i, False)

            for c in range(2):
                for f in range(6):
                    n = 6 * c + f
                    kc, ks = (KS[:, j, f, 512 * c:512 * c + 512] for j in range(2))
                    pool.wait_ge(u_prod, n + 1)
                    TT(kc, Tt[:, 0:512], Tt[:, 512:1024], ALU.subtract)
                    TT(ks, Tt[:, 1024:1536], Tt[:, 1536:2048], ALU.add).then_inc(p_ready, 1)

            for n in range(4):
                low(following([AT["x0"] + 3 * n]), 0)
            loops(pool, 4, lambda i: low(following([AT["z"] + 3 * n for n in range(4)]), i))
            for n in range(5):
                low([AT["xbc"] + n + 1], 0)

            pool.wait_ge(xs_ready, XBC_BLKS)
            pool.memset(HST[:, :, :], 0.0).then_inc(st_zero, 1)
            pool.wait_ge(dec_ready, 1)

            def ramp(s, d, t, b):
                if not (isinstance(s, int) and s == 0 and b < 2):
                    pool.wait_ge(s_seg, s * 4 + (b - 1))
                tri = C[:, LE if d == 0 else GE, :].unsqueeze(1).broadcast_to([P, 4, P])
                for ramps, part_ in ((AT2H, DTAH), (AT2L, DTAL)):
                    a = part_[:, bass.ds(t, 1), 16 * d + 4 * b:16 * d + 4 * b + 4].rearrange("p a b -> p (a b)")
                    ins = TT(ramps[:, b % 2, :].rearrange("p (h c) -> p h c", h=4), tri,
                             a.bitcast(f32).unsqueeze(2).broadcast_to([P, 4, P]), ALU.mult)
                ins.then_inc(s_at, 1)

            def to_end(s, d, t):
                pool.wait_ge(s_xdt, s + 1)
                if not (isinstance(s, int) and s == 0):
                    pool.wait_ge(s_st, s * 2)
                dec = DEC[:, 96 * d:96 * d + 96].rearrange("p (t h) -> p t h", t=6)
                TT(XDE.rearrange("p (h c) -> p h c", h=HEADS), XDT[d].rearrange("p (h c) -> p h c", h=HEADS),
                   dec[:, bass.ds(t, 1), :].rearrange("p a b -> p (a b)").unsqueeze(2)
                   .broadcast_to([P, HEADS, HD]), ALU.mult).then_inc(s_xde, 1)

            def turn(s0, chunks, last):
                for d in range(2):
                    s = s0 + d
                    ramp(s, d, chunks[d + 1], 2)
                    ramp(s, d, chunks[d + 1], 3)
                    if not (last and d == 1):
                        ramp(s + 1, 1 - d, chunks[d + 2], 0)
                    if not last:
                        to_end(s, d, chunks[d + 1])
                    if not (last and d == 1):
                        ramp(s + 1, 1 - d, chunks[d + 2], 1)

            pool.wait_ge(dta_split, 1)
            ramp(0, 0, 4, 0)
            ramp(0, 0, 4, 1)
            chunk_turns(pool, turn)

            low([G0], 0)
            for n in range(2 * KT):
                j, k = (1, n) if n < KT else (0, n - KT)
                src = (G if j else XBC)[:, k, :]
                pool.wait_ge(mix_hi, n + 1)
                TT(YGL[j][:, k, :], src, YGH[:, j, k, :].bitcast(f32), ALU.subtract).then_inc(mix_lo, 1)
            next_low("out0", 8, 2)

            def feed_forward(layer, n, segs):
                low_parts(n, segs)
                for half in range(2):
                    next_low(f"up{layer}{half}", FH, 1)
                    if layer == 1 and half == 1:
                        for r in range(7):
                            low([AT["down11"] + r + 1], 0)
                    else:
                        next_low(f"down{layer}{half}", 8)
            feed_forward(0, 1, SEGS)
            low_parts(2)
            pool.wait_ge(blocks_done, 2 * AT["qkv"])
            pool.dma_start(RC[:, :, :], A["rope"].rearrange("p (a b) -> p a b", a=2)).then_inc(rope_in, 16)
            for r in range(6):
                low([AT["qkv"] + r + 1], 0)
            for r in range(4):
                low([AT["out1"] + r + 1], 0)
            feed_forward(1, 3, (SEGS[0],))


def _constants():
    k = np.arange(P)
    K, J = k[:, None], k[None, :]
    c = np.zeros((P, 9, P), np.float32)
    c[:, IDENT] = K == J
    c[:, ONES] = 1
    c[:, KGTJ] = K > J
    c[:, KLTJ] = K < J
    c[:, LE] = K <= J
    c[:, GE] = K >= J
    for m in range(P):
        c[m + 16 if m % 32 < 16 else m - 16, ROT, m] = -1 if m % 32 < 16 else 1
    c[:, MLEFT] = np.where(J >= K, 0, NEG)
    c[:, MRIGHT] = np.where(J <= K, 0, NEG)

    def table(shift):
        parts = []
        for fn in (np.cos, np.sin):
            cols = []
            for L in (LAT, CTX):
                t, f = np.arange(L)[:, None] + shift, np.arange(L)[None, :] + 0.5
                m = fn(np.pi * t * f / L)
                cols.append(m.reshape(L // P, P, L).transpose(1, 0, 2).reshape(P, -1))
            parts.append(np.concatenate(cols, 1))
        return np.concatenate(parts, 1).astype(np.float32)

    f4 = np.float32
    feats, wins = [], []
    for L in (LAT, CTX):
        t = np.arange(L, dtype=f4)
        unit = t / f4(L - 1)
        ang = f4(2.0 * np.pi) * t / f4(L)
        f = np.linspace(1e-4, HY_BANDS - 1, HY_BANDS, dtype=f4)
        feats.append(np.concatenate([unit[:, None], np.cos(ang[:, None] * f), -np.sin(ang[:, None] * f)], 1).T)
        deltas = np.linspace(np.log(1e-2) / 1.5, np.log(1e-2) / 0.3, D, dtype=f4)
        w = np.exp(-unit[:, None] * np.abs(deltas)[None, :])
        wins.append(w.reshape(L // P, P, 2, 512).transpose(1, 2, 0, 3))
    rows = LAT // GRID_W
    row = np.repeat(np.arange(rows), GRID_W).astype(f4)
    col = np.tile(np.arange(GRID_W), rows).astype(f4)
    inv = f4(ROPE_BASE) ** (-np.arange(16, dtype=f4) / f4(16))
    ang = np.zeros((P, LAT), f4)
    for m in range(P):
        ang[m] = (row if m % 64 < 32 else col) * inv[m % 16]
    rope = np.concatenate([np.cos(ang), np.sin(ang)], 1)
    return {"const": c.reshape(P, 9 * P), "tab3": table(0.0), "tab4": table(0.5),
            "zfeat": np.concatenate(feats, 1).astype(f4), "window": np.concatenate(wins, 2).astype(f4),
            "rope": rope.astype(f4)}


def _layout(a):
    def tiles(w, cols):
        return w[:, cols:cols + P].reshape(-1, P, P).transpose(1, 0, 2)

    hy, z0, x0 = a["hy_in_w"][0], 0, D
    h0 = D + XBC_BLKS * P + 2 * HEADS
    wall = np.zeros((len(JOBS), P, JT, P), np.float32)
    for g, (kind, layer, n) in enumerate(JOBS):
        if kind == "ada":
            w = a["ada_w"][layer][(n % 2) * 4 * P:(n % 2 + 1) * 4 * P, (n // 2) * 4 * P:(n // 2 + 1) * 4 * P]
            wall[g] = w.reshape(4, P, 4, P).transpose(1, 0, 2, 3).reshape(P, JT, P)
            continue
        elif kind == "uv":
            two = [(hy, h0 + (8 + 8 * b + n) * P) for b in range(2)]
        elif kind == "x0":
            two = [(hy, h0 + (2 * n + b) * P) for b in range(2)]
        elif kind == "z":
            two = [(hy, (2 * n + b) * P) for b in range(2)]
        elif kind == "xbc":
            two = [(hy, D + (2 * n + b) * P) for b in range(2)]
        elif kind == "out0":
            wall[g] = np.roll(tiles(a["hy_out_w"][0], n * P), KT, 1)
            continue
        elif kind == "up":
            two = [(a["ffn_w_in"][layer], b * FFN + n * P) for b in range(2)]
        elif kind == "down":
            half, blk = n
            t = tiles(a["ffn_w_out"][layer][half * FH * P:(half + 1) * FH * P], blk * P)
            wall[g, :, 0:DOWN[0]] = t[:, 0:DOWN[0]]
            wall[g, :, HALF:HALF + DOWN[1]] = t[:, DOWN[0]:]
            continue
        elif kind in ("q", "k"):
            two = [(a["attn_qkv_w"][0], (8 if kind == "k" else 0) * P + (2 * n + b) * P) for b in range(2)]
        elif kind == "v":
            w = a["attn_qkv_w"][0][:, D + 256:D + 512].reshape(KT, P, 2, P)
            wall[g] = w.transpose(1, 0, 2, 3).reshape(P, JT, P)
            continue
        elif kind == "out1":
            two = [(a["attn_out_w"][0], (2 * n + b) * P) for b in range(2)]
        for b, (w, c) in enumerate(two):
            wall[g, :, KT * b:KT * b + KT] = tiles(w, c)

    def feat(v):
        return v.reshape(-1, P).T

    vec = np.zeros((P, VEC_W - 2), np.float32)

    def put(name, v):
        vec[:, _cols[name]:_cols[name] + v.shape[1]] = v

    put("ada_b", feat(a["ada_b"].reshape(-1)))
    put("n1", feat(a["norm1_g"].reshape(-1)))
    put("n2", feat(a["norm2_g"].reshape(-1)))
    put("fin", feat(a["final_g"]))
    put("sng", feat(a["ssd_norm_g"][0]))
    put("scw", feat(a["ssd_conv_w"][0].reshape(-1)))
    put("scb", feat(a["ssd_conv_b"][0]))
    put("hcw", feat(a["hy_conv_w"][0].reshape(-1)))
    put("hcb", feat(a["hy_conv_b"][0]))
    put("dskip", feat(np.repeat(a["ssd_d"][0], HD)))
    put("cc", np.stack([feat(a["c"][0]), feat(a["c_ctx"])], 2).reshape(P, 16))
    put("sink", np.repeat(a["attn_sinks"][0:1], P, 0))
    put("dtb", np.repeat(a["ssd_dt_bias"].reshape(1, 32), P, 0))
    put("alog", np.repeat(a["ssd_a_log"].reshape(1, 32), P, 0))
    xt = np.concatenate([a["x"][0].T, a["ctx"][0].T], 1)
    wdt = hy[:, D + XBC_BLKS * P:h0]
    return {
        "wall": wall.reshape(len(JOBS), P, JT * P), "vec": vec,
        "xT": xt.reshape(KT, P, TOK).transpose(1, 0, 2), "w_dt": wdt.reshape(KT, P, 32).transpose(1, 0, 2),
        "hy_w1": a["hy_w1"][0], "hy_w2": a["hy_w2"][0], "hy_w3": a["hy_w3"][0], "hy_w4": a["hy_w4"][0],
        "hy_fb": np.concatenate([a["hy_freq"][0].T, np.stack([a["hy_b1"][0], a["hy_b2"][0], a["hy_b3"][0]], 1)], 1),
        "hy_bias": a["hy_bias"],
    }


def kernel(**inputs):
    import concourse.bacc as bacc
    from concourse.bass_utils import run_bass_kernel_spmd as run

    arrays = {k: np.ascontiguousarray(v) for k, v in
              {**_layout({k: np.asarray(v) for k, v in inputs.items()}), **_constants()}.items()}
    nc = bacc.Bacc("TRN2", target_bir_lowering=False, num_devices=1)
    args = {k: nc.dram_tensor(f"in_{k}", v.shape, mybir.dt.from_np(v.dtype), kind="ExternalInput").ap()
            for k, v in arrays.items()}
    out = nc.dram_tensor("out_T", (P, KT, LAT), mybir.dt.float32, kind="ExternalOutput").ap()
    build_kernel(nc, args, out)
    r = run(nc, [{f"in_{k}": v for k, v in arrays.items()}], core_ids=[0])
    y = r.results[0]["out_T"]
    return np.ascontiguousarray(y.transpose(1, 0, 2).reshape(D, LAT).T).reshape(1, LAT, D)
```
